# Optimizing a Trainium2 kernel written in Bass

```python
import math
import jax
import jax.numpy as jnp
from jax import lax
import numpy as np
import jax, jax.numpy as jnp

D_MODEL = 1024
BATCH = 1
SEQ = 256
DEPTH = 2

N_HEADS = 8
N_KV_HEADS = 2
HEAD_DIM = 64
Q_PER_KV = N_HEADS // N_KV_HEADS
ATTN_WIDTH = N_HEADS * HEAD_DIM
KV_WIDTH = N_KV_HEADS * HEAD_DIM
N_BRANCH = 3
CMP_LEN = 32
CMP_STRIDE = 16
CMP_HIDDEN = 128
SEL_LEN = 64
SEL_TOPK = 16
N_LOCAL_SEL = 2
WINDOW = 512
Q_BLOCK = 64
CONV_WIDTH = D_MODEL // 2
CONV_KERNEL = 31
MIX_WIDTH = ATTN_WIDTH + CONV_WIDTH
IN_WIDTH = ATTN_WIDTH + 6 * KV_WIDTH + N_HEADS * N_BRANCH + 2 * CONV_WIDTH
ROPE_THETA = 500000.0
ROPE_DIM = HEAD_DIM // 4
D_FF = 7 * D_MODEL // 2
N_EXPERTS = 8
TOP_K = 2
MOE_BLOCK = 128
EPS = 1e-6


def rms_norm(x, g):
    xf = x.astype(jnp.float32)
    y = xf * lax.rsqrt(jnp.mean(xf * xf, axis=-1, keepdims=True) + EPS)
    return (y * g.astype(jnp.float32)).astype(x.dtype)

def layer_norm(x, g, b):
    xf = x.astype(jnp.float32)
    xc = xf - jnp.mean(xf, axis=-1, keepdims=True)
    y = xc * lax.rsqrt(jnp.mean(xc * xc, axis=-1, keepdims=True) + EPS)
    return (y * g.astype(jnp.float32) + b.astype(jnp.float32)).astype(x.dtype)

def masked_softmax(s, mask):
    s = jnp.where(mask, s.astype(jnp.float32), -jnp.inf)
    m = jnp.max(s, axis=-1, keepdims=True)
    m = jnp.where(jnp.isfinite(m), m, 0.0)
    p = jnp.exp(s - m)
    return p / jnp.maximum(jnp.sum(p, axis=-1, keepdims=True), jnp.finfo(jnp.float32).tiny)

def rope_partial(x, pos):
    half = ROPE_DIM // 2
    inv_freq = ROPE_THETA ** (-2.0 * jnp.arange(half, dtype=jnp.float32) / ROPE_DIM)
    ang = pos.astype(jnp.float32)[..., None, None] * inv_freq
    cos, sin = jnp.cos(ang), jnp.sin(ang)
    xr = x[..., :ROPE_DIM].astype(jnp.float32)
    x1, x2 = xr[..., :half], xr[..., half:]
    rot = jnp.concatenate([x1 * cos - x2 * sin, x2 * cos + x1 * sin], axis=-1).astype(x.dtype)
    return jnp.concatenate([rot, x[..., ROPE_DIM:]], axis=-1)

def swiglu(x, wg, wu, wd):
    return (jax.nn.silu(x @ wg) * (x @ wu)) @ wd

def in_proj_split_points():
    sizes = [ATTN_WIDTH] + [KV_WIDTH] * 6 + [N_HEADS * N_BRANCH, 2 * CONV_WIDTH]
    return [int(v) for v in np.cumsum(sizes)[:-1]]

def n_cmp_blocks(s):
    return (s - CMP_LEN) // CMP_STRIDE + 1

def cmp_block_ends(s):
    return np.arange(n_cmp_blocks(s)) * CMP_STRIDE + CMP_LEN - 1

def selection_map(s):
    c0 = np.arange(n_cmp_blocks(s)) * CMP_STRIDE
    s0 = np.arange(s // SEL_LEN) * SEL_LEN
    ov = np.minimum(c0[:, None] + CMP_LEN, s0[None, :] + SEL_LEN) - np.maximum(c0[:, None], s0[None, :])
    return jnp.asarray(np.clip(ov, 0, None) / CMP_LEN, dtype=jnp.float32)

def compress_blocks(kv, pos_emb, w1, w2):
    b, s = kv.shape[0], kv.shape[1]
    n_cmp = n_cmp_blocks(s)
    idx = np.arange(n_cmp)[:, None] * CMP_STRIDE + np.arange(CMP_LEN)[None, :]
    blocks = kv[:, idx] + pos_emb[None, None, :, None, :]
    blocks = blocks.transpose(0, 1, 3, 2, 4).reshape(b, n_cmp, N_KV_HEADS, CMP_LEN * HEAD_DIM)
    hid = jax.nn.gelu(jnp.einsum('bnkf,fh->bnkh', blocks, w1))
    return jnp.einsum('bnkh,hd->bnkd', hid, w2)

def nsa_attention(q, k_cmp, v_cmp, k_slc, v_slc, k_win, v_win, gates):
    b, s = q.shape[0], q.shape[1]
    n_sel = s // SEL_LEN
    top_n = min(SEL_TOPK, n_sel)
    scale = HEAD_DIM ** -0.5
    q = q.reshape(b, s, N_KV_HEADS, Q_PER_KV, HEAD_DIM)
    gates = gates.reshape(b, s, N_KV_HEADS, Q_PER_KV, N_BRANCH)
    cmp_end = jnp.asarray(cmp_block_ends(s))
    sel_map = selection_map(s)
    k_blk = k_slc.reshape(b, n_sel, SEL_LEN, N_KV_HEADS, HEAD_DIM).transpose(0, 3, 1, 2, 4)
    v_blk = v_slc.reshape(b, n_sel, SEL_LEN, N_KV_HEADS, HEAD_DIM).transpose(0, 3, 1, 2, 4)
    pad = ((0, 0), (WINDOW, 0), (0, 0), (0, 0))
    k_wpad = jnp.pad(k_win, pad)
    v_wpad = jnp.pad(v_win, pad)
    b_ix = jnp.arange(b)[:, None, None, None]
    h_ix = jnp.arange(N_KV_HEADS)[None, None, :, None]
    blk_ids = jnp.arange(n_sel)

    def query_block(c):
        t0 = c * Q_BLOCK
        t = t0 + jnp.arange(Q_BLOCK)
        qc = lax.dynamic_slice_in_dim(q, t0, Q_BLOCK, axis=1)
        gc = lax.dynamic_slice_in_dim(gates, t0, Q_BLOCK, axis=1)
        s_c = jnp.einsum('bqkgd,bnkd->bqkgn', qc, k_cmp) * scale
        mask_c = (cmp_end[None, :] <= t[:, None])[None, :, None, None, :]
        p_c = masked_softmax(s_c, mask_c)
        o_c = jnp.einsum('bqkgn,bnkd->bqkgd', p_c.astype(v_cmp.dtype), v_cmp)
        imp = jnp.einsum('bqkgn,nj->bqkj', p_c, sel_map)
        cur = (t // SEL_LEN)[:, None]
        causal_blk = blk_ids[None, :] <= cur
        forced = (blk_ids[None, :] == 0) | (causal_blk & (blk_ids[None, :] > cur - N_LOCAL_SEL))
        score = jnp.where(forced[None, :, None, :], jnp.inf,
                          jnp.where(causal_blk[None, :, None, :], imp, -jnp.inf))
        _, sel_idx = lax.top_k(score, top_n)
        k_sel = k_blk[b_ix, h_ix, sel_idx].reshape(b, Q_BLOCK, N_KV_HEADS, top_n * SEL_LEN, HEAD_DIM)
        v_sel = v_blk[b_ix, h_ix, sel_idx].reshape(b, Q_BLOCK, N_KV_HEADS, top_n * SEL_LEN, HEAD_DIM)
        tok = (sel_idx[..., None] * SEL_LEN + jnp.arange(SEL_LEN)).reshape(
            b, Q_BLOCK, N_KV_HEADS, 1, top_n * SEL_LEN)
        mask_s = tok <= t[None, :, None, None, None]
        s_s = jnp.einsum('bqkgd,bqkmd->bqkgm', qc, k_sel) * scale
        p_s = masked_softmax(s_s, mask_s)
        o_s = jnp.einsum('bqkgm,bqkmd->bqkgd', p_s.astype(v_sel.dtype), v_sel)
        k_w = lax.dynamic_slice_in_dim(k_wpad, t0, WINDOW + Q_BLOCK, axis=1)
        v_w = lax.dynamic_slice_in_dim(v_wpad, t0, WINDOW + Q_BLOCK, axis=1)
        src = t0 - WINDOW + jnp.arange(WINDOW + Q_BLOCK)
        mask_w = ((src[None, :] >= 0) & (src[None, :] <= t[:, None])
                  & (src[None, :] > t[:, None] - WINDOW))[None, :, None, None, :]
        s_w = jnp.einsum('bqkgd,bwkd->bqkgw', qc, k_w) * scale
        p_w = masked_softmax(s_w, mask_w)
        o_w = jnp.einsum('bqkgw,bwkd->bqkgd', p_w.astype(v_w.dtype), v_w)
        return gc[..., 0:1] * o_c + gc[..., 1:2] * o_s + gc[..., 2:3] * o_w

    out = lax.map(query_block, jnp.arange(s // Q_BLOCK))
    return out.transpose(1, 0, 2, 3, 4, 5).reshape(b, s, ATTN_WIDTH)

def conformer_conv(u, conv_w, conv_b, ln_g, ln_b):
    a, g = jnp.split(u, 2, axis=-1)
    h = a * jax.nn.sigmoid(g)
    h = jnp.pad(h, ((0, 0), (CONV_KERNEL - 1, 0), (0, 0)))
    y = lax.conv_general_dilated(h, conv_w[:, None, :], window_strides=(1,), padding='VALID',
                                 dimension_numbers=('NWC', 'WIO', 'NWC'),
                                 feature_group_count=CONV_WIDTH)
    y = y + conv_b
    return jax.nn.silu(layer_norm(y, ln_g, ln_b))

def moe_swiglu(h, router, wg, wu, wd):
    b, s, d = h.shape
    n_tok = b * s
    xt = h.reshape(n_tok, d)
    logits = (xt @ router).astype(jnp.float32)
    top_logit, top_e = lax.top_k(logits, TOP_K)
    gate = jax.nn.softmax(top_logit, axis=-1)
    n_asg = n_tok * TOP_K
    e_flat = top_e.reshape(n_asg)
    tok_flat = jnp.broadcast_to(jnp.arange(n_tok)[:, None], (n_tok, TOP_K)).reshape(n_asg)
    g_flat = gate.reshape(n_asg)
    order = jnp.argsort(e_flat)
    e_s, tok_s, g_s = e_flat[order], tok_flat[order], g_flat[order]
    counts = jnp.bincount(e_flat, length=N_EXPERTS)
    padded = (counts + MOE_BLOCK - 1) // MOE_BLOCK * MOE_BLOCK
    start = jnp.cumsum(counts) - counts
    pend = jnp.cumsum(padded)
    pstart = pend - padded
    dest = pstart[e_s] + jnp.arange(n_asg) - start[e_s]
    n_blocks = -(-n_asg // MOE_BLOCK) + N_EXPERTS
    n_slots = n_blocks * MOE_BLOCK
    slot_tok = jnp.full((n_slots,), n_tok, jnp.int32).at[dest].set(tok_s.astype(jnp.int32))
    slot_gate = jnp.zeros((n_slots,), jnp.float32).at[dest].set(g_s)
    blk_e = jnp.clip(jnp.searchsorted(pend, jnp.arange(n_blocks) * MOE_BLOCK, side='right'),
                     0, N_EXPERTS - 1)
    x_pad = jnp.concatenate([xt, jnp.zeros((1, d), xt.dtype)], axis=0)
    xs = x_pad[slot_tok].reshape(n_blocks, MOE_BLOCK, d)

    def expert_block(args):
        xb, e = args
        return swiglu(xb, wg[e], wu[e], wd[e])

    ys = lax.map(expert_block, (xs, blk_e)).reshape(n_slots, d)
    ys = ys * slot_gate[:, None].astype(ys.dtype)
    out = jax.ops.segment_sum(ys, slot_tok, num_segments=n_tok + 1)[:n_tok]
    return out.reshape(b, s, d)

def first_inputs(seed: int = 0) -> dict:
    key = jax.random.key(seed)
    keys = list(jax.random.split(key, 32))

    def nrm(i, shape, scale):
        return scale * jax.random.normal(keys[i], shape, jnp.float32)

    n_dense = (DEPTH + 1) // 2
    n_moe = DEPTH // 2
    x = nrm(0, (BATCH, SEQ, D_MODEL), 1.0)
    offsets = jax.random.randint(keys[1], (BATCH, 1), 0, 2048, dtype=jnp.int32)
    positions = offsets + jnp.arange(SEQ, dtype=jnp.int32)[None, :]
    return {
        "x": x,
        "positions": positions,
        "attn_norm_g": 1.0 + nrm(2, (DEPTH, D_MODEL), 0.02),
        "ffn_norm_g": 1.0 + nrm(3, (DEPTH, D_MODEL), 0.02),
        "w_in": nrm(4, (DEPTH, D_MODEL, IN_WIDTH), D_MODEL ** -0.5),
        "w_out": nrm(5, (DEPTH, MIX_WIDTH, D_MODEL), MIX_WIDTH ** -0.5),
        "q_norm_g": 1.0 + nrm(6, (DEPTH, HEAD_DIM), 0.02),
        "k_norm_g": 1.0 + nrm(7, (DEPTH, N_BRANCH, HEAD_DIM), 0.02),
        "cmp_pos_k": nrm(8, (DEPTH, CMP_LEN, HEAD_DIM), 0.1),
        "cmp_w1_k": nrm(9, (DEPTH, CMP_LEN * HEAD_DIM, CMP_HIDDEN), (CMP_LEN * HEAD_DIM) ** -0.5),
        "cmp_w2_k": nrm(10, (DEPTH, CMP_HIDDEN, HEAD_DIM), CMP_HIDDEN ** -0.5),
        "cmp_pos_v": nrm(11, (DEPTH, CMP_LEN, HEAD_DIM), 0.1),
        "cmp_w1_v": nrm(12, (DEPTH, CMP_LEN * HEAD_DIM, CMP_HIDDEN), (CMP_LEN * HEAD_DIM) ** -0.5),
        "cmp_w2_v": nrm(13, (DEPTH, CMP_HIDDEN, HEAD_DIM), CMP_HIDDEN ** -0.5),
        "conv_w": nrm(14, (DEPTH, CONV_KERNEL, CONV_WIDTH), CONV_KERNEL ** -0.5),
        "conv_b": nrm(15, (DEPTH, CONV_WIDTH), 0.02),
        "conv_ln_g": 1.0 + nrm(16, (DEPTH, CONV_WIDTH), 0.02),
        "conv_ln_b": nrm(17, (DEPTH, CONV_WIDTH), 0.02),
        "ffn_w_gate": nrm(18, (n_dense, D_MODEL, D_FF), D_MODEL ** -0.5),
        "ffn_w_up": nrm(19, (n_dense, D_MODEL, D_FF), D_MODEL ** -0.5),
        "ffn_w_down": nrm(20, (n_dense, D_FF, D_MODEL), D_FF ** -0.5),
        "moe_router": nrm(21, (n_moe, D_MODEL, N_EXPERTS), D_MODEL ** -0.5),
        "moe_w_gate": nrm(22, (n_moe, N_EXPERTS, D_MODEL, D_FF), D_MODEL ** -0.5),
        "moe_w_up": nrm(23, (n_moe, N_EXPERTS, D_MODEL, D_FF), D_MODEL ** -0.5),
        "moe_w_down": nrm(24, (n_moe, N_EXPERTS, D_FF, D_MODEL), D_FF ** -0.5),
    }

def first_block(x, positions, attn_norm_g, ffn_norm_g, w_in, w_out, q_norm_g, k_norm_g,
              cmp_pos_k, cmp_w1_k, cmp_w2_k, cmp_pos_v, cmp_w1_v, cmp_w2_v,
              conv_w, conv_b, conv_ln_g, conv_ln_b,
              ffn_w_gate, ffn_w_up, ffn_w_down,
              moe_router, moe_w_gate, moe_w_up, moe_w_down):
    b, s, _ = x.shape
    pos_cmp = positions[:, cmp_block_ends(s)]
    split_points = in_proj_split_points()
    for layer in range(DEPTH):
        h = rms_norm(x, attn_norm_g[layer])
        proj = jnp.einsum('bsd,de->bse', h, w_in[layer])
        q, k_c, v_c, k_s, v_s, k_w, v_w, g_logit, u = jnp.split(proj, split_points, axis=-1)
        q = rope_partial(rms_norm(q.reshape(b, s, N_HEADS, HEAD_DIM), q_norm_g[layer]), positions)
        kv_shape = (b, s, N_KV_HEADS, HEAD_DIM)
        k_cmp = compress_blocks(k_c.reshape(kv_shape), cmp_pos_k[layer], cmp_w1_k[layer], cmp_w2_k[layer])
        k_cmp = rope_partial(rms_norm(k_cmp, k_norm_g[layer, 0]), pos_cmp)
        v_cmp = compress_blocks(v_c.reshape(kv_shape), cmp_pos_v[layer], cmp_w1_v[layer], cmp_w2_v[layer])
        k_slc = rope_partial(rms_norm(k_s.reshape(kv_shape), k_norm_g[layer, 1]), positions)
        k_win = rope_partial(rms_norm(k_w.reshape(kv_shape), k_norm_g[layer, 2]), positions)
        gates = jax.nn.sigmoid(g_logit.astype(jnp.float32)).astype(x.dtype).reshape(b, s, N_HEADS, N_BRANCH)
        attn_out = nsa_attention(q, k_cmp, v_cmp, k_slc, v_s.reshape(kv_shape),
                                 k_win, v_w.reshape(kv_shape), gates)
        conv_out = conformer_conv(u, conv_w[layer], conv_b[layer], conv_ln_g[layer], conv_ln_b[layer])
        mixed = jnp.concatenate([attn_out, conv_out], axis=-1)
        x = x + jnp.einsum('bsm,md->bsd', mixed, w_out[layer])
        h = rms_norm(x, ffn_norm_g[layer])
        if layer % 2 == 0:
            i = layer // 2
            x = x + swiglu(h, ffn_w_gate[i], ffn_w_up[i], ffn_w_down[i])
        else:
            i = layer // 2
            x = x + moe_swiglu(h, moe_router[i], moe_w_gate[i], moe_w_up[i], moe_w_down[i])
    return x


GRID_W = 64
CTX_LEN = 256
N_MIXERS = 4
ROPE_THETA_2 = 10000.0
NEG_INF = -1e30
Q_BLOCK_2 = 128
D_FF_2 = -(-(8 * D_MODEL) // (3 * 256)) * 256
SWA_HEADS = D_MODEL // HEAD_DIM
SWA_KV_HEADS = 4
SWA_WINDOW = 128
NA_HEADS = D_MODEL // HEAD_DIM
NA_KH = 8
NA_KW = 16
NA_QCB = 16
NA_SLAB = 2 * NA_KW
POOL_WINDOWS = (2, 4, 8, 16)
POOL_GROUPS = len(POOL_WINDOWS)
POOL_DG = D_MODEL // POOL_GROUPS
MLA_HEADS = 16
MLA_NOPE = 64
MLA_ROPE = 32
MLA_V = 64
MLA_Q_RANK = 256
MLA_KV_RANK = 128


def n_layers_of(m):
    return len(range(m, DEPTH, N_MIXERS))

def rms_norm_2(x, g):
    xf = x.astype(jnp.float32)
    y = xf * lax.rsqrt(jnp.mean(xf * xf, axis=-1, keepdims=True) + EPS)
    return (y * g.astype(jnp.float32)).astype(x.dtype)

def modulate(x, g, shift, scale):
    return rms_norm_2(x, g) * (1 + scale) + shift

def rope_1d(x, pos):
    half = x.shape[-1] // 2
    freqs = ROPE_THETA_2 ** (-jnp.arange(half, dtype=jnp.float32) / half)
    ang = pos.astype(jnp.float32)[:, None] * freqs[None, :]
    cos = jnp.cos(ang)[:, None, :]
    sin = jnp.sin(ang)[:, None, :]
    xf = x.astype(jnp.float32)
    x1, x2 = xf[..., :half], xf[..., half:]
    return jnp.concatenate([x1 * cos - x2 * sin, x1 * sin + x2 * cos], -1).astype(x.dtype)

def rope_2d_axial(x, length):
    t = jnp.arange(length)
    d = x.shape[-1] // 2
    return jnp.concatenate([rope_1d(x[..., :d], t // GRID_W), rope_1d(x[..., d:], t % GRID_W)], -1)

def softmax_f32(s, sink=None):
    if sink is None:
        return jax.nn.softmax(s, axis=-1)
    sink = jnp.broadcast_to(sink, s.shape[:-1] + (1,))
    return jax.nn.softmax(jnp.concatenate([s, sink], -1), axis=-1)[..., :-1]

def swiglu_2(h, w_gu, w_down):
    gu = h @ w_gu
    return (jax.nn.silu(gu[..., :D_FF_2]) * gu[..., D_FF_2:]) @ w_down

def swa_mixer(a_lat, a_ctx, w_qkv, g_q, g_k, sink, w_o, need_ctx):
    B, L, _ = a_lat.shape
    Lc = a_ctx.shape[1]
    Hq, Hk, dh = SWA_HEADS, SWA_KV_HEADS, HEAD_DIM
    G = Hq // Hk
    nq, nk = Hq * dh, Hk * dh
    scale = dh ** -0.5
    qkv = a_lat @ w_qkv
    q = rope_2d_axial(rms_norm_2(qkv[..., :nq].reshape(B, L, Hq, dh), g_q), L)
    k = rope_2d_axial(rms_norm_2(qkv[..., nq:nq + nk].reshape(B, L, Hk, dh), g_k), L)
    v = qkv[..., nq + nk:].reshape(B, L, Hk, dh)
    kv_c = a_ctx @ w_qkv[:, nq:]
    k_c = rms_norm_2(kv_c[..., :nk].reshape(B, Lc, Hk, dh), g_k)
    v_c = kv_c[..., nk:].reshape(B, Lc, Hk, dh)
    sink_g = sink.astype(jnp.float32).reshape(Hk, G)[None, :, :, None, None]
    nb = L // Q_BLOCK_2
    span = Q_BLOCK_2 + 2 * SWA_WINDOW
    pad = ((0, 0), (SWA_WINDOW, SWA_WINDOW), (0, 0), (0, 0))
    k_p = jnp.pad(k, pad)
    v_p = jnp.pad(v, pad)
    q_blocks = jnp.moveaxis(q.reshape(B, nb, Q_BLOCK_2, Hk, G, dh), 1, 0)
    ctx_valid = jnp.ones((Q_BLOCK_2, Lc), bool)

    def block(args):
        b, q_b = args
        start = b * Q_BLOCK_2
        k_b = jnp.concatenate([lax.dynamic_slice_in_dim(k_p, start, span, 1), k_c], 1)
        v_b = jnp.concatenate([lax.dynamic_slice_in_dim(v_p, start, span, 1), v_c], 1)
        q_pos = start + jnp.arange(Q_BLOCK_2)
        k_pos = start - SWA_WINDOW + jnp.arange(span)
        valid = (jnp.abs(q_pos[:, None] - k_pos[None, :]) <= SWA_WINDOW) & (k_pos >= 0) & (k_pos < L)
        valid = jnp.concatenate([valid, ctx_valid], 1)
        s = jnp.einsum('bqhgd,bkhd->bhgqk', q_b, k_b, preferred_element_type=jnp.float32) * scale
        p = softmax_f32(jnp.where(valid, s, NEG_INF), sink_g).astype(v_b.dtype)
        return jnp.einsum('bhgqk,bkhd->bqhgd', p, v_b)

    o = lax.map(block, (jnp.arange(nb), q_blocks))
    y_lat = jnp.moveaxis(o, 0, 1).reshape(B, L, nq) @ w_o
    y_ctx = None
    if need_ctx:
        q_c = rms_norm_2((a_ctx @ w_qkv[:, :nq]).reshape(B, Lc, Hk, G, dh), g_q)
        s = jnp.einsum('bqhgd,bkhd->bhgqk', q_c, k_c, preferred_element_type=jnp.float32) * scale
        p = softmax_f32(s, sink_g).astype(v_c.dtype)
        y_ctx = jnp.einsum('bhgqk,bkhd->bqhgd', p, v_c).reshape(B, Lc, nq) @ w_o
    return y_lat, y_ctx

def na_mixer(a_lat, a_ctx, w_qkv, g_q, g_k, rpb, w_o, need_ctx):
    B, L, _ = a_lat.shape
    Lc = a_ctx.shape[1]
    H, dh = NA_HEADS, HEAD_DIM
    n = H * dh
    scale = dh ** -0.5
    rows = L // GRID_W
    kh = min(NA_KH, rows)
    qkv = a_lat @ w_qkv
    q = rms_norm_2(qkv[..., :n].reshape(B, rows, GRID_W, H, dh), g_q)
    k = rms_norm_2(qkv[..., n:2 * n].reshape(B, rows, GRID_W, H, dh), g_k)
    v = qkv[..., 2 * n:].reshape(B, rows, GRID_W, H, dh)
    kv_c = a_ctx @ w_qkv[:, n:]
    k_c = rms_norm_2(kv_c[..., :n].reshape(B, Lc, H, dh), g_k)
    v_c = kv_c[..., n:].reshape(B, Lc, H, dh)
    ncb = GRID_W // NA_QCB
    q_col = np.arange(GRID_W).reshape(ncb, NA_QCB)
    slab0 = [int(s) for s in np.clip(np.arange(ncb) * NA_QCB - NA_KW // 2, 0, GRID_W - NA_SLAB)]
    col_start = np.clip(q_col - NA_KW // 2, 0, GRID_W - NA_KW)
    key_col = np.asarray(slab0)[:, None] + np.arange(NA_SLAB)
    kc3 = key_col[:, None, :]
    col_valid = (kc3 >= col_start[..., None]) & (kc3 < col_start[..., None] + NA_KW)
    dc_idx = (np.clip(kc3 - q_col[..., None], -(NA_KW - 1), NA_KW - 1) + NA_KW - 1)[:, :, None, :]
    nkey = kh * NA_SLAB
    valid_lat = np.broadcast_to(col_valid[:, :, None, :], (ncb, NA_QCB, kh, NA_SLAB)).reshape(ncb, NA_QCB, nkey)
    valid = jnp.asarray(np.concatenate([valid_lat, np.ones((ncb, NA_QCB, Lc), bool)], -1))
    rpb_f = rpb.astype(jnp.float32)

    def slabs(t):
        return jnp.stack([t[:, :, s:s + NA_SLAB] for s in slab0], 1).reshape(B, ncb, nkey, H, dh)

    def row_step(args):
        r, q_r = args
        r0 = jnp.clip(r - kh // 2, 0, rows - kh)
        k_s = slabs(lax.dynamic_slice_in_dim(k, r0, kh, 1))
        v_s = slabs(lax.dynamic_slice_in_dim(v, r0, kh, 1))
        dr_idx = (r0 + jnp.arange(kh) - r + NA_KH - 1)[None, None, :, None]
        bias = rpb_f[:, dr_idx, dc_idx].reshape(H, ncb, NA_QCB, nkey)
        q_b = q_r.reshape(B, ncb, NA_QCB, H, dh)
        s_lat = jnp.einsum('bjqhd,bjkhd->bhjqk', q_b, k_s, preferred_element_type=jnp.float32) * scale + bias
        s_ctx = jnp.einsum('bjqhd,bkhd->bhjqk', q_b, k_c, preferred_element_type=jnp.float32) * scale
        p = softmax_f32(jnp.where(valid, jnp.concatenate([s_lat, s_ctx], -1), NEG_INF)).astype(v.dtype)
        o = (jnp.einsum('bhjqk,bjkhd->bjqhd', p[..., :nkey], v_s)
             + jnp.einsum('bhjqk,bkhd->bjqhd', p[..., nkey:], v_c))
        return o.reshape(B, GRID_W, H, dh)

    o = lax.map(row_step, (jnp.arange(rows), jnp.moveaxis(q, 1, 0)))
    y_lat = jnp.moveaxis(o, 0, 1).reshape(B, L, n) @ w_o
    y_ctx = None
    if need_ctx:
        q_c = rms_norm_2((a_ctx @ w_qkv[:, :n]).reshape(B, Lc, H, dh), g_q)
        s = jnp.einsum('bqhd,bkhd->bhqk', q_c, k_c, preferred_element_type=jnp.float32) * scale
        p = softmax_f32(s).astype(v_c.dtype)
        y_ctx = jnp.einsum('bhqk,bkhd->bqhd', p, v_c).reshape(B, Lc, n) @ w_o
    return y_lat, y_ctx

def multi_pool(h):
    B, L, _ = h.shape
    hf = h.astype(jnp.float32)
    cs = jnp.pad(lax.cumsum(hf, axis=1), ((0, 0), (1, 0), (0, 0)))
    t = jnp.arange(L)
    outs = []
    for g, w in enumerate(POOL_WINDOWS):
        lo = jnp.clip(t - w // 2, 0, L)
        hi = jnp.clip(t - w // 2 + w, 0, L)
        cg = cs[..., g * POOL_DG:(g + 1) * POOL_DG]
        outs.append((cg[:, hi] - cg[:, lo]) / (hi - lo).astype(jnp.float32)[None, :, None])
    return (jnp.concatenate(outs, -1) - hf).astype(h.dtype)

def pool_mixer(a_lat, a_ctx, w, b, scale, need_ctx):
    def mix(h):
        B, L, _ = h.shape
        p = multi_pool(h).reshape(B, L, POOL_GROUPS, POOL_DG)
        y = jnp.einsum('blgc,gcd->blgd', p, w) + b
        return y.reshape(B, L, D_MODEL) * scale
    return mix(a_lat), (mix(a_ctx) if need_ctx else None)

def mla_mixer(a_lat, a_ctx, w_a, g_cq, g_ckv, w_uq, w_ukv, g_q, g_k, w_o, need_ctx):
    H, dn, dr, dv = MLA_HEADS, MLA_NOPE, MLA_ROPE, MLA_V
    dqk = dn + dr
    qr = MLA_Q_RANK
    scale = dqk ** -0.5

    def queries(cq_raw):
        B_, L_, _ = cq_raw.shape
        c_q = rms_norm_2(cq_raw, g_cq)
        return rms_norm_2((c_q @ w_uq).reshape(B_, L_, H, dqk), g_q)

    def keys_values(kv_raw):
        B_, L_, _ = kv_raw.shape
        c_kv = rms_norm_2(kv_raw[..., :MLA_KV_RANK], g_ckv)
        k_r = jnp.broadcast_to(kv_raw[..., MLA_KV_RANK:][:, :, None, :], (B_, L_, H, dr))
        kv = (c_kv @ w_ukv).reshape(B_, L_, H, dn + dv)
        k = rms_norm_2(jnp.concatenate([kv[..., :dn], k_r], -1), g_k)
        return k, kv[..., dn:]

    def rope_part(t):
        return jnp.concatenate([t[..., :dn], rope_2d_axial(t[..., dn:], t.shape[1])], -1)

    B, L, _ = a_lat.shape
    Lc = a_ctx.shape[1]
    proj = a_lat @ w_a
    q = rope_part(queries(proj[..., :qr]))
    k, v = keys_values(proj[..., qr:])
    k = rope_part(k)
    if need_ctx:
        proj_c = a_ctx @ w_a
        q_c = queries(proj_c[..., :qr])
        kv_raw_c = proj_c[..., qr:]
    else:
        kv_raw_c = a_ctx @ w_a[:, qr:]
    k_c, v_c = keys_values(kv_raw_c)
    k_all = jnp.concatenate([k, k_c], 1)
    v_all = jnp.concatenate([v, v_c], 1)
    nb = L // Q_BLOCK_2
    q_blocks = jnp.moveaxis(q.reshape(B, nb, Q_BLOCK_2, H, dqk), 1, 0)

    def block(q_b):
        s = jnp.einsum('bqhd,bkhd->bhqk', q_b, k_all, preferred_element_type=jnp.float32) * scale
        p = softmax_f32(s).astype(v_all.dtype)
        return jnp.einsum('bhqk,bkhd->bqhd', p, v_all)

    o = lax.map(block, q_blocks)
    y_lat = jnp.moveaxis(o, 0, 1).reshape(B, L, H * dv) @ w_o
    y_ctx = None
    if need_ctx:
        s = jnp.einsum('bqhd,bkhd->bhqk', q_c, k_c, preferred_element_type=jnp.float32) * scale
        p = softmax_f32(s).astype(v_c.dtype)
        y_ctx = jnp.einsum('bhqk,bkhd->bqhd', p, v_c).reshape(B, Lc, H * dv) @ w_o
    return y_lat, y_ctx

def second_inputs(seed: int = 0) -> dict:
    key = jax.random.key(seed)
    ks = iter(jax.random.split(key, 48))
    f32 = jnp.float32

    def nrm(shape, fan_in, gain=1.0):
        return jax.random.normal(next(ks), shape, f32) * (gain * fan_in ** -0.5)

    def gains(shape):
        return 1.0 + 0.05 * jax.random.normal(next(ks), shape, f32)

    def small(shape, s=0.01):
        return s * jax.random.normal(next(ks), shape, f32)

    D = D_MODEL
    nA, nB, nC, nD = (n_layers_of(m) for m in range(N_MIXERS))
    dqk = MLA_NOPE + MLA_ROPE
    return {
        'x': jax.random.normal(next(ks), (BATCH, SEQ, D), f32),
        'c': jax.random.normal(next(ks), (BATCH, D), f32),
        'ctx': jax.random.normal(next(ks), (BATCH, CTX_LEN, D), f32),
        'c_ctx': jax.random.normal(next(ks), (D,), f32),
        'w_ada': nrm((DEPTH, D, 6 * D), D, 0.5),
        'b_ada': small((DEPTH, 6 * D)),
        'g_mix': gains((DEPTH, D)),
        'g_ffn': gains((DEPTH, D)),
        'w_gate_up': nrm((DEPTH, D, 2 * D_FF_2), D),
        'w_down': nrm((DEPTH, D_FF_2, D), D_FF_2),
        'swa_w_qkv': nrm((nA, D, (SWA_HEADS + 2 * SWA_KV_HEADS) * HEAD_DIM), D),
        'swa_g_q': gains((nA, HEAD_DIM)),
        'swa_g_k': gains((nA, HEAD_DIM)),
        'swa_sink': small((nA, SWA_HEADS), 0.5),
        'swa_w_o': nrm((nA, SWA_HEADS * HEAD_DIM, D), SWA_HEADS * HEAD_DIM),
        'na_w_qkv': nrm((nB, D, 3 * NA_HEADS * HEAD_DIM), D),
        'na_g_q': gains((nB, HEAD_DIM)),
        'na_g_k': gains((nB, HEAD_DIM)),
        'na_rpb': small((nB, NA_HEADS, 2 * NA_KH - 1, 2 * NA_KW - 1), 0.1),
        'na_w_o': nrm((nB, NA_HEADS * HEAD_DIM, D), NA_HEADS * HEAD_DIM),
        'pool_w': nrm((nC, POOL_GROUPS, POOL_DG, POOL_DG), POOL_DG),
        'pool_b': small((nC, POOL_GROUPS, POOL_DG)),
        'pool_scale': gains((nC, D)),
        'mla_w_a': nrm((nD, D, MLA_Q_RANK + MLA_KV_RANK + MLA_ROPE), D),
        'mla_g_cq': gains((nD, MLA_Q_RANK)),
        'mla_g_ckv': gains((nD, MLA_KV_RANK)),
        'mla_w_uq': nrm((nD, MLA_Q_RANK, MLA_HEADS * dqk), MLA_Q_RANK),
        'mla_w_ukv': nrm((nD, MLA_KV_RANK, MLA_HEADS * (MLA_NOPE + MLA_V)), MLA_KV_RANK),
        'mla_g_q': gains((nD, dqk)),
        'mla_g_k': gains((nD, dqk)),
        'mla_w_o': nrm((nD, MLA_HEADS * MLA_V, D), MLA_HEADS * MLA_V),
    }

def second_block(x, c, ctx, c_ctx, w_ada, b_ada, g_mix, g_ffn, w_gate_up, w_down,
              swa_w_qkv, swa_g_q, swa_g_k, swa_sink, swa_w_o,
              na_w_qkv, na_g_q, na_g_k, na_rpb, na_w_o,
              pool_w, pool_b, pool_scale,
              mla_w_a, mla_g_cq, mla_g_ckv, mla_w_uq, mla_w_ukv, mla_g_q, mla_g_k, mla_w_o):
    cond = jax.nn.silu(c)
    cond_c = jax.nn.silu(c_ctx)
    h, hc = x, ctx
    for i in range(DEPTH):
        m, j = i % N_MIXERS, i // N_MIXERS
        need_ctx = i < DEPTH - 1
        mod = (cond @ w_ada[i] + b_ada[i])[:, None, :]
        mod_c = cond_c @ w_ada[i] + b_ada[i]
        sh1, sc1, gt1, sh2, sc2, gt2 = jnp.split(mod, 6, axis=-1)
        sh1c, sc1c, gt1c, sh2c, sc2c, gt2c = jnp.split(mod_c, 6, axis=-1)
        a = modulate(h, g_mix[i], sh1, sc1)
        ac = modulate(hc, g_mix[i], sh1c, sc1c)
        if m == 0:
            y, yc = swa_mixer(a, ac, swa_w_qkv[j], swa_g_q[j], swa_g_k[j], swa_sink[j], swa_w_o[j], need_ctx)
        elif m == 1:
            y, yc = na_mixer(a, ac, na_w_qkv[j], na_g_q[j], na_g_k[j], na_rpb[j], na_w_o[j], need_ctx)
        elif m == 2:
            y, yc = pool_mixer(a, ac, pool_w[j], pool_b[j], pool_scale[j], need_ctx)
        else:
            y, yc = mla_mixer(a, ac, mla_w_a[j], mla_g_cq[j], mla_g_ckv[j], mla_w_uq[j], mla_w_ukv[j],
                              mla_g_q[j], mla_g_k[j], mla_w_o[j], need_ctx)
        h = h + gt1 * y
        h = h + gt2 * swiglu_2(modulate(h, g_ffn[i], sh2, sc2), w_gate_up[i], w_down[i])
        if need_ctx:
            hc = hc + gt1c * yc
            hc = hc + gt2c * swiglu_2(modulate(hc, g_ffn[i], sh2c, sc2c), w_gate_up[i], w_down[i])
    return h


def setup_inputs(seed=0):
    out = dict(first_inputs(seed))
    for name, value in second_inputs(seed + 1).items():
        if name != "x":
            out[name + "_2"] = value
    return out


def reference(
    x, positions, attn_norm_g, ffn_norm_g, w_in, w_out, q_norm_g, k_norm_g, cmp_pos_k, cmp_w1_k,
    cmp_w2_k, cmp_pos_v, cmp_w1_v, cmp_w2_v, conv_w, conv_b, conv_ln_g, conv_ln_b, ffn_w_gate,
    ffn_w_up, ffn_w_down, moe_router, moe_w_gate, moe_w_up, moe_w_down, c_2, ctx_2, c_ctx_2,
    w_ada_2, b_ada_2, g_mix_2, g_ffn_2, w_gate_up_2, w_down_2, swa_w_qkv_2, swa_g_q_2,
    swa_g_k_2, swa_sink_2, swa_w_o_2, na_w_qkv_2, na_g_q_2, na_g_k_2, na_rpb_2, na_w_o_2,
    pool_w_2, pool_b_2, pool_scale_2, mla_w_a_2, mla_g_cq_2, mla_g_ckv_2, mla_w_uq_2,
    mla_w_ukv_2, mla_g_q_2, mla_g_k_2, mla_w_o_2,
):
    x = first_block(
        x, positions, attn_norm_g, ffn_norm_g, w_in, w_out, q_norm_g, k_norm_g, cmp_pos_k,
        cmp_w1_k, cmp_w2_k, cmp_pos_v, cmp_w1_v, cmp_w2_v, conv_w, conv_b, conv_ln_g, conv_ln_b,
        ffn_w_gate, ffn_w_up, ffn_w_down, moe_router, moe_w_gate, moe_w_up, moe_w_down,
    )
    return second_block(
        x, c_2, ctx_2, c_ctx_2, w_ada_2, b_ada_2, g_mix_2, g_ffn_2, w_gate_up_2, w_down_2,
        swa_w_qkv_2, swa_g_q_2, swa_g_k_2, swa_sink_2, swa_w_o_2, na_w_qkv_2, na_g_q_2,
        na_g_k_2, na_rpb_2, na_w_o_2, pool_w_2, pool_b_2, pool_scale_2, mla_w_a_2, mla_g_cq_2,
        mla_g_ckv_2, mla_w_uq_2, mla_w_ukv_2, mla_g_q_2, mla_g_k_2, mla_w_o_2,
    )


_drawn_inputs = setup_inputs


def setup_inputs(seed=0):
    import zlib

    import numpy as np

    out = dict(_drawn_inputs(seed))
    spreads = {}
    factors = {'q_norm_g': 5.591,
     'k_norm_g': 4.055,
     'cmp_pos_k': 7.355,
     'conv_ln_b': 3.106,
     'b_ada_2': 6.117,
     'g_mix_2': 8.0,
     'g_ffn_2': 3.683,
     'swa_g_q_2': 8.0,
     'swa_g_k_2': 8.0,
     'swa_sink_2': 8.0,
     'na_g_q_2': 8.0,
     'na_g_k_2': 8.0,
     'na_rpb_2': 8.0}
    for name, (base, spread) in spreads.items():
        noise = np.random.default_rng([zlib.crc32(name.encode()), seed]).standard_normal(out[name].shape)
        drawn = base * np.exp(spread * noise) if base else spread * noise
        out[name] = jnp.asarray(drawn.astype(out[name].dtype))
    for name, factor in factors.items():
        out[name] = (out[name] * factor).astype(out[name].dtype)
    return out
```

```python
import math
from contextlib import ExitStack

import numpy as np
import concourse.bass as bass
from concourse import mybir

F32 = mybir.dt.float32
I32 = mybir.dt.int32
U32 = mybir.dt.uint32
ALU = mybir.AluOpType
ACT = mybir.ActivationFunctionType
AX = mybir.AxisListType

P = 128
S = 256
QT = S // P
D = 1024
KC = D // P
HD = 64
EPS = 1e-6
NEG = -1e30
TINY = float(np.finfo(np.float32).tiny)
NCMP = 15
TAPS = 31
CW = 512
CC = CW // P
AW = 512
COLW = 256
SLOTS = 6
FF1, FF2 = 3584, 2816
NE = 8
GW = 64
GROWS = S // GW
SKW = 127
NDR = 2 * GROWS - 1
MAGIC = 12582912.0
TWO_PI = (6.28125, 0.00193500518798828125, 3.01991598196e-7)



def constant_layout():
    at, out = 0, {}
    for name, n in (("ident", P), ("ones", P), ("causal", QT * S), ("cmp", QT * NCMP), ("swa", QT * S),
                    ("na", S), ("cos2", QT * 32), ("sin2", QT * 32), ("freq", 8), ("iota", P), ("before", P)):
        out[name] = (at, n)
        at += n
    return out, at


def shape_constants():
    layout, width = constant_layout()
    c = np.zeros((P, width), np.float32)

    def put(name, a):
        at, n = layout[name]
        c[:, at:at + n] = np.asarray(a, np.float32).reshape(P, n)

    p = np.arange(P)
    t = (np.arange(QT)[None, :] * P + p[:, None])[:, :, None]
    k = np.arange(S)[None, None, :]
    put("ident", np.eye(P))
    put("ones", np.ones((P, P)))
    put("causal", np.where(k <= t, 0.0, NEG))
    put("cmp", np.where(np.arange(NCMP)[None, None, :] * 16 + 31 <= t, 0.0, NEG))
    put("swa", np.where(np.abs(k - t) <= 128, 0.0, NEG))
    start = np.clip(p % GW - 8, 0, GW - 16)[:, None]
    col = (np.arange(S) % GW)[None, :]
    put("na", np.where((col >= start) & (col < start + 16), 0.0, NEG))
    f2 = np.float32(10000.0) ** (-np.arange(16, dtype=np.float32) / np.float32(16))
    tt = t[:, :, 0]
    ang = np.stack([(tt // GW)[..., None] * f2, (tt % GW)[..., None] * f2], 2).astype(np.float32)
    put("cos2", np.cos(ang))
    put("sin2", np.sin(ang))
    f1 = np.float32(500000.0) ** (np.float32(-2.0) * np.arange(8, dtype=np.float32) / np.float32(16))
    put("freq", np.broadcast_to(f1, (P, 8)))
    put("iota", np.broadcast_to(np.arange(P), (P, P)))
    put("before", p[:, None] < p[None, :])
    return c



def free(a, dims, off=0):
    return bass.AP(tensor=a.tensor, offset=a.offset + off, ap=[list(a.ap[0])] + dims)


def rows(a, off, dims):
    return bass.AP(tensor=a.tensor, offset=a.offset + off, ap=dims)



class Batch:

    def __init__(self, qt, heads, q, k, nk, kt, v, mask, **more):
        self.qt, self.heads, self.q, self.k, self.nk, self.kt, self.v, self.mask = qt, heads, q, k, nk, kt, v, mask
        self.gate = more.get("gate")
        self.sink = more.get("sink", False)
        self.bias = more.get("bias", False)


def pair_heads(h):
    return 4 * (h // 8) + h % 4, 64 * (h // 4 % 2)


def first_batches():
    out = []
    for qt in range(QT):
        for g in range(2):
            heads = [4 * g + j for j in range(4)]
            for br, nk in ((0, NCMP), (1, P * (qt + 1)), (2, P * (qt + 1))):
                out.append(Batch(qt, heads, [pair_heads(h) for h in heads], [(0, 64 * g)] * 4, nk,
                                 "cmp" if br == 0 else ("slc", "win")[br - 1], (br, [64 * g] * 4),
                                 "cmp" if br == 0 else "causal", gate=br))
    return out


def swa_batches(ctx):
    out = []
    for qt in range(QT):
        for g in range(4):
            heads = [4 * g + j for j in range(4)]
            out.append(Batch(qt, heads, [pair_heads(h) for h in heads], [(g // 2, 64 * (g % 2))] * 4,
                             S if ctx else 2 * S, "swa_ctx" if ctx else "all",
                             (None, [1280 + 64 * g] * 4), None if ctx else "swa", sink=True))
    return out


def na_batches():
    out = []
    for qt in range(QT):
        for g in range(4):
            heads = [4 * g + j for j in range(4)]
            where = [(h // 2, 64 * (h % 2)) for h in heads]
            out.append(Batch(qt, heads, where, where, 2 * S, "all", (None, [64 * h for h in heads]), None, bias=True))
    return out


def build(nc, a, out):
    ctx = ExitStack()
    with ctx:
        def sb(name, shape, dt=F32):
            return ctx.enter_context(nc.sbuf_tensor(name, shape, dt))

        def sem(name):
            return ctx.enter_context(nc.semaphore(name))

        ada_done = sem("ada_done")
        angles = sem("angles")
        attended = sem("attended")
        bias_used = sem("bias_used")
        blocks_ready = sem("blocks_ready")
        cond_raw = sem("cond_raw")
        cond_ready = sem("cond_ready")
        conv_gate = sem("conv_gate")
        conv_normed = sem("conv_normed")
        conv_ready = sem("conv_ready")
        denominators = sem("denominators")
        exp_main = sem("exp_main")
        exp_sink = sem("exp_sink")
        gate_logits = sem("gate_logits")
        gates_ready = sem("gates_ready")
        gates_sigmoid = sem("gates_sigmoid")
        hT_ready = sem("hT_ready")
        hidden_raw = sem("hidden_raw")
        hidden_ready = sem("hidden_ready")
        kcm_ready = sem("kcm_ready")
        mixed_attn = sem("mixed_attn")
        mixed_conv = sem("mixed_conv")
        normed = sem("normed")
        output_done = sem("output_done")
        output_taken = sem("output_taken")
        params = sem("params")
        pos_clear = sem("pos_clear")
        positions = sem("positions")
        probT_ready = sem("probT_ready")
        prob_ready = sem("prob_ready")
        qT_ready = sem("qT_ready")
        qk_ready = sem("qk_ready")
        root_in = sem("root_in")
        back_current = sem("back_current")
        picked = sem("picked")
        scatter_clear = sem("scatter_clear")
        y_taken = sem("y_taken")
        h_current = sem("h_current")
        routed = sem("routed")
        root_out = sem("root_out")
        rpb_clear = sem("rpb_clear")
        rpb_loaded = sem("rpb_loaded")
        scores_done = sem("scores_done")
        scores_taken = sem("scores_taken")
        shifted = sem("shifted")
        sines = sem("sines")
        skewed = sem("skewed")
        squares = sem("squares")
        stored = sem("stored")
        sum_done = sem("sum_done")
        tile_used = sem("tile_used")
        top_exp = sem("top_exp")
        top_shifted = sem("top_shifted")
        u_ready = sem("u_ready")
        vector_chain = sem("vector_chain")
        x_final = sem("x_final")
        x_ready = sem("x_ready")
        act_ready = [sem(f"act_ready{i}") for i in range(2)]
        bank_emptied = [sem(f"bank_emptied{i}") for i in range(2)]
        bank_filled = [sem(f"bank_filled{i}") for i in range(2)]
        bias_loaded = [sem(f"bias_loaded{i}") for i in range(2)]
        gate_up_done = [sem(f"gate_up_done{i}") for i in range(2)]
        silu_ready = [sem(f"silu_ready{i}") for i in range(2)]
        tile_loaded = [sem(f"tile_loaded{i}") for i in range(SLOTS)]
        weighed = [sem(f"weighed{i}") for i in range(2)]

        layout, cwidth = constant_layout()
        ring = sb("ring", [P, SLOTS * 2048])
        const = sb("const", [P, cwidth])
        x = sb("x", [P, QT * D])
        xc = sb("xc", [P, QT * D])
        hT = sb("hT", [P, KC * S])
        big = sb("big", [P, QT * 3072])
        bigc = sb("bigc", [P, QT * 2048])
        work = sb("work", [P, QT * D])
        prob = sb("prob", [P, 2 * 4 * 512])
        hTc = prob[:, 0:KC * S]
        probT = sb("probT", [P, 4 * 4 * P])
        qT = sb("qT", [P, 8 * S])
        kT = sb("kT", [P, 8 * 2 * S])
        biasb = sb("biasb", [P, 2 * 4 * S])
        gateb = sb("gateb", [P, D])
        chunks = sb("chunks", [P, 4 * S])
        silu = chunks[:, 0:2 * S]
        actb = chunks[:, 2 * S:4 * S]
        mod = sb("mod", [P, 2 * 48 * 2])
        gsc = sb("gsc", [P, KC])
        rowsA = probT[0:104, 0:128]
        rowsB = probT[0:96, 128:256]
        rowsC = probT[0:64, 256:384]
        rowsD = probT[0:2 * TAPS, 512:1024]
        colA = sb("colA", [P, 104])
        colB = sb("colB", [P, 96])
        colC = sb("colC", [P, 64])
        convw = sb("convw", [P, CC * 2 * TAPS])
        cond = sb("cond", [P, KC * 2])
        gain1 = sb("gain1", [P, 2 * 4 * HD])
        gain2 = sb("gain2", [P, 4 * HD])
        sink = sb("sink", [P, 16])
        w2 = sb("w2", [P, 2 * 2 * HD])
        router = sb("router", [P, KC * NE])
        posi = sb("posi", [P, 3], I32)
        posf = sb("posf", [P, 3])
        ang = sb("ang", [P, 4 * 24])
        cos1 = sb("cos1", [P, 24])
        sin1 = sb("sin1", [P, 24])
        rpb = biasb[0:16, 0:NDR * SKW]
        small = sb("small", [P, 256])
        hid = sb("hid", [P, 2 * 60])
        kcm = sb("kcm", [16, 2 * 128])
        kcT = sb("kcT", [P, 16])
        logit = sb("logit", [P, 6 * 16])
        top_i = sb("top_i", [P, 16], U32)
        route = sb("route", [P, 48])
        most = sb("most", [P, 1], I32)
        den = sb("den", [P, 4 * 8])
        ropet = chunks
        skew = nc.dram_tensor("skew_scratch", [16, GW, NDR * SKW], F32, kind="Internal").ap()

        pacc = ctx.enter_context(nc.psum_tensor("pacc", [P, 2048], F32))
        pt = [ctx.enter_context(nc.psum_tensor(f"pt{i}", [P, 512], F32)) for i in range(2)]
        po = ctx.enter_context(nc.psum_tensor("po", [P, 512], F32))
        pada = ctx.enter_context(nc.psum_tensor("pada", [P, 512], F32))

        def cst(name, n=P):
            at, w = layout[name]
            return const[0:n, at:at + w]

        ident = cst("ident")
        xv = x[:, :].rearrange("p (t n) -> p t n", t=QT)
        xcv = xc[:, :].rearrange("p (t n) -> p t n", t=QT)
        hTv = hT[:, :].rearrange("p (k t) -> p k t", k=KC)
        hTcv = hTc.rearrange("p (k t) -> p k t", k=KC)
        wv = work[:, :].rearrange("p (t n) -> p t n", t=QT)
        qTv = qT[:, :].rearrange("p (c t) -> p c t", c=8)
        gathered = big[:, 0:6 * D], bigc[:, 0:2 * D]
        pick = qT[:, :].rearrange("p (e t n) -> p e t n", e=NE, t=QT)
        weigh = probT[:, :].rearrange("p (e t n) -> p e t n", e=NE, t=QT)
        back = kT[:, 0:(NE + 1) * S]
        hcur = qT[:, 0:D]
        hcurv = hcur.rearrange("p (k t) -> p k t", k=KC)
        backcur = qT[:, D:D + S]
        gx = kT[:, 0:NE * S].rearrange("p (e t) -> p e t", e=NE)
        modv = mod[:, :].rearrange("p (l c s) -> p l c s", l=2, c=48)
        condv = cond[:, :].rearrange("p (k s) -> p k s", s=2)
        qkz = big[:, 0:QT * 12 * HD].rearrange("p (t h d) -> p t h d", t=QT, h=12)
        val1 = big[:, 1536:2048].rearrange("p (t n) -> p t n", t=QT)
        ug = big[:, 2048:4096].rearrange("p (c t) -> p c t", c=8)
        padded = big[:, 4096:4096 + CC * (S + TAPS - 1)].rearrange("p (c t) -> p c t", c=CC)
        kvp = bigc[:, 0:1024].rearrange("p (w v t) -> p w v t", w=2, v=2)
        blk = bigc[:, 1024:1984].rearrange("p (w i v n) -> p w i v n", w=2, i=16, v=2)
        y = bigc[:, 1984:3008].rearrange("p (c t) -> p c t", c=CC)
        y2 = bigc[:, 3008:4032].rearrange("p (c t) -> p c t", c=CC)
        spread = [pacc[:, 1024:1536], pacc[:, 1536:2048], po[:, :], pada[:, :]]
        glog = small[:, 0:QT * 24].rearrange("p (t n) -> p t n", t=QT)
        w2v = w2[:, :].rearrange("p (l w d) -> p l w d", l=2, w=2)
        convv = convw[:, :].rearrange("p (c n) -> p c n", c=CC)

        W = {n: a[n] for n in a}
        w_in = [W["w_in"][i] for i in range(2)]
        w_out = [W["w_out"][i] for i in range(2)]
        w_ada = [W["w_ada_2"][i] for i in range(2)]
        w_gu = [W["w_gate_up_2"][i] for i in range(2)]
        w_dn = [W["w_down_2"][i] for i in range(2)]

        def col_tile(w, c0, n=COLW):
            return w[:, c0:c0 + n].rearrange("(k p) n -> p k n", p=P), ("col", n)

        def row_tile(w, t):
            return w[256 * t:256 * t + 256, :].rearrange("(a p) n -> p a n", p=P), ("row", D)

        IN_TILES = [(0, 256), (256, 256), (512, 256), (768, 256), (1024, 256), (1280, 24)] + \
                   [(1304 + 256 * j, 256) for j in range(4)]
        stream = []
        ada = [(i, j) for i in range(2) for j in range(24)]
        ada_per = len(ada) // (2 * len(first_batches()))
        for l in range(2):
            stream += [("tile",) + col_tile(w_in[l], c, n) for c, n in IN_TILES]
            for w in ("cmp_w1_k", "cmp_w1_v"):
                stream.append(("tile", W[w][l].rearrange("(i p) h -> p i h", p=P), ("cmp", P)))
            for i, j in ada[l * 24:l * 24 + 24]:
                stream.append(("tile",) + col_tile(w_ada[i], 256 * j))
            stream += [("tile",) + row_tile(w_out[l], t) for t in range(4)]
            if l == 0:
                stream.append(("ffn", W["ffn_w_gate"][0], W["ffn_w_up"][0], 0, W["ffn_w_down"][0], FF1 // COLW))
            else:
                stream.append(("moe",))
        stream += [("tile",) + col_tile(W["swa_w_qkv_2"][0], 256 * j) for j in range(6)]
        swa_o = [("tile",) + row_tile(W["swa_w_o_2"][0], t) for t in range(4)]
        ffn2 = [("ffn", w_gu[i], w_gu[i], FF2, w_dn[i], FF2 // COLW) for i in range(2)]
        stream += swa_o + [ffn2[0]] + swa_o + [ffn2[0]]
        stream += [("tile",) + col_tile(W["na_w_qkv_2"][0], 256 * j) for j in range(12)]
        stream += [("tile",) + row_tile(W["na_w_o_2"][0], t) for t in range(4)] + [ffn2[1]]

        ffn_at, n = [], 0
        for item in stream:
            if item[0] != "tile":
                ffn_at.append(n)
            n += {"tile": 1, "ffn": 3 * item[-1] if item[0] == "ffn" else 0, "moe": 3 * NE * FF1 // COLW}[item[0]]

        def slot(n):
            return ring[:, (n % SLOTS) * 2048:(n % SLOTS + 1) * 2048]

        def slot_view(n, kind):
            what, w = kind
            if what == "col":
                return slot(n).rearrange("p (k n) -> p k n", k=KC)[:, :, 0:w]
            return slot(n).rearrange("p (k n) -> p k n", n=w)

        def bcast(w, off, n, rep=1):
            return rows(w, off, [[0, P]] + ([[0, rep]] if rep > 1 else []) + [[1, n]])

        loads = [(const[:, :], W["shape_constants"])]
        at = 0
        COL = {}
        for name in ("attn_norm_g", "ffn_norm_g", "conv_b", "conv_ln_g", "conv_ln_b", "g_mix_2", "g_ffn_2"):
            n = W[name].shape[0] * W[name].shape[1] // P
            loads.append((rowsA[at:at + n, :], W[name].rearrange("l (k p) -> (l k) p", p=P)))
            COL[name] = at
            at += n
        loads.append((rowsA[at:at + 8, :], W["c_2"].rearrange("b (k p) -> (b k) p", p=P)))
        loads.append((rowsA[at + 8:at + 16, :], W["c_ctx_2"].rearrange("(k p) -> k p", p=P)))
        COL["cond"] = at
        loads.append((rowsB[:, :], W["b_ada_2"].rearrange("l (k p) -> (l k) p", p=P)))
        loads.append((rowsC[0:32, :], W["cmp_pos_k"].rearrange("l (i a) d -> (l i) (a d)", a=2)))
        loads.append((rowsC[32:64, :], W["cmp_pos_v"].rearrange("l (i a) d -> (l i) (a d)", a=2)))
        loads.append((rowsD[:, :], W["conv_w"].rearrange("l k c -> (l k) c")))
        for l in range(2):
            loads.append((gain1[:, 256 * l:256 * l + 64], bcast(W["q_norm_g"], 64 * l, 64)))
            for j, br in enumerate((1, 2, 0)):
                loads.append((gain1[:, 256 * l + 64 * (j + 1):256 * l + 64 * (j + 2)],
                              bcast(W["k_norm_g"], 64 * (3 * l + br), 64)))
            loads.append((w2v[:, l, 0, :], W["cmp_w2_k"][l]))
            loads.append((w2v[:, l, 1, :], W["cmp_w2_v"][l]))
        for j, name in enumerate(("swa_g_q_2", "swa_g_k_2", "na_g_q_2", "na_g_k_2")):
            loads.append((gain2[:, 64 * j:64 * j + 64], bcast(W[name], 0, 64)))
        loads.append((sink[:, :], bcast(W["swa_sink_2"], 0, 16)))
        loads.append((router[:, :].rearrange("p (k e) -> p k e", k=KC),
                      W["moe_router"][0].rearrange("(k p) e -> p k e", p=P)))
        loads.append((xv, W["x"][0].rearrange("(t p) n -> p t n", p=P)))
        loads.append((xcv, W["ctx_2"][0].rearrange("(t p) n -> p t n", p=P)))
        pos_loads = [(posi[:, t:t + 1], rows(W["positions"], t * P, [[1, P], [1, 1]])) for t in range(QT)]
        pos_loads.append((posi[0:NCMP, 2:3], rows(W["positions"], 31, [[16, NCMP], [1, 1]])))

        block = ctx.enter_context(nc.Block())

        def counter():
            seen = {}

            def due(name, k=1):
                seen[name] = seen.get(name, 0) + k
                return seen[name]
            return due

        def attention_view(b, which):
            c, base = b.k[which]
            hi = base + HD
            if b.kt == "cmp":
                return kcT[base:hi, 0:NCMP]
            if b.kt in ("slc", "win"):
                o = S * (b.kt == "win")
                return kT[base:hi, o:o + b.nk]
            if b.kt == "swa_ctx":
                return kT[base:hi, c * 512 + S:c * 512 + 2 * S]
            return kT[base:hi, c * 512:c * 512 + 2 * S]

        def value_view(b, which, kc, layer1):
            br, cols = b.v
            c = cols[which]
            if br == 0:
                return kcm[0:NCMP, 128 + c:128 + c + HD]
            if br is not None:
                return val1[:, kc, (br - 1) * 128 + c:(br - 1) * 128 + c + HD]
            if layer1:
                if kc < QT:
                    return big[:, kc * 3072 + 2048 + c:kc * 3072 + 2048 + c + HD]
                o = (kc - QT) * 2048 + 1024 + c
                return bigc[:, o:o + HD]
            if b.kt == "swa_ctx":
                kc += QT
            src, o = (big, kc * 1536) if kc < QT else (bigc, (kc - QT) * 1536)
            return src[:, o + c:o + c + HD]

        @block.sync
        def _(sp):
            n = 0

            def load(n, src, kind, it=None, base=None):
                if it is not None:
                    sp.wait_ge(tile_used, it * 6 + (base - SLOTS + 1))
                elif n >= SLOTS:
                    sp.wait_ge(tile_used, n - SLOTS + 1)
                sp.dma_start(slot_view(n, kind), src).then_inc(tile_loaded[n % SLOTS], 16)

            def group_src(wg, wu, uoff, wd, g):
                c = g * COLW
                return ((wg[:, bass.ds(c, COLW)].rearrange("(k p) n -> p k n", p=P), ("col", COLW)),
                        (wu[:, bass.ds(c + uoff, COLW)].rearrange("(k p) n -> p k n", p=P), ("col", COLW)),
                        (wd[bass.ds(c, COLW), :].rearrange("(a p) n -> p a n", p=P), ("row", D)))

            for item in stream:
                if item[0] == "tile":
                    load(n, item[1], item[2])
                    n += 1
                elif item[0] == "ffn":
                    _, wg, wu, uoff, wd, groups = item
                    with sp.Fori(0, groups // 2) as it:
                        for u in range(2):
                            for j, (src, kind) in enumerate(group_src(wg, wu, uoff, wd, it * 2 + u)):
                                load(n + 3 * u + j, src, kind, it, n + 3 * u + j)
                    n += 6 * (groups // 2)
                    if groups % 2:
                        for src, kind in group_src(wg, wu, uoff, wd, groups - 1):
                            load(n, src, kind)
                            n += 1
                else:
                    wg = W["moe_w_gate"][0].rearrange("e k f -> (e k) f")
                    wu = W["moe_w_up"][0].rearrange("e k f -> (e k) f")
                    wd = W["moe_w_down"][0].rearrange("e f n -> (e f) n")
                    per = FF1 // COLW // 2
                    with sp.Fori(0, NE) as e:
                        with sp.Fori(0, per) as j:
                            for u in range(2):
                                c = j * (2 * COLW) + u * COLW
                                for k, (src, kind) in enumerate((
                                        (wg[bass.ds(e * D, D), bass.ds(c, COLW)].rearrange("(k p) n -> p k n", p=P), ("col", COLW)),
                                        (wu[bass.ds(e * D, D), bass.ds(c, COLW)].rearrange("(k p) n -> p k n", p=P), ("col", COLW)),
                                        (wd[bass.ds(e * FF1 + c, COLW), :].rearrange("(a p) n -> p a n", p=P), ("row", D)))):
                                    load(n + 3 * u + k, src, kind, e * per + j, n + 3 * u + k)
                    n += 6 * per * NE
            sp.wait_ge(x_final, 1)
            sp.dma_start(out[0].rearrange("(t p) n -> p t n", p=P), xv).then_inc(stored, 16)
            sp.wait_ge(stored, 16)

        @block.gpsimd
        def _(pool):
            pool.memset(rpb[:, :], 0.0).then_inc(rpb_clear, 1)
            pool.wait_ge(rpb_clear, 1)
            rv = rpb[:, :].rearrange("h (r n) -> h r n", r=NDR)
            pool.dma_start(rv[:, :, 48:79], W["na_rpb_2"][0, :, 4:4 + NDR, :]).then_inc(rpb_loaded, 16)
            pool.wait_ge(rpb_loaded, 16)
            pool.dma_start(skew, free(rpb[:, :], [[0, GW], [1, NDR * SKW]])).then_inc(skewed, 16)
            pool.wait_ge(skewed, 16)
            pitch = NDR * SKW
            for i, b in enumerate(na_batches()):
                if i >= 2:
                    pool.wait_ge(bias_used, i - 1)
                for rr in range(2):
                    r = 2 * b.qt + rr
                    for j in range(4):
                        src = rows(skew, (b.heads[j] * GW) * pitch + (GROWS - 1 - r) * SKW + GW - 1,
                                   [[pitch - 1, GW], [SKW, GROWS], [1, GW]])
                        dst = biasb[64 * rr:64 * rr + 64, (i % 2) * 1024 + j * S:(i % 2) * 1024 + j * S + S]
                        pool.dma_start(dst.rearrange("p (r c) -> p r c", r=GROWS), src)\
                            .then_inc(bias_loaded[i % 2], 16)

        @block.tensor
        def _(pe):
            due = counter()
            pos = {"tile": 0, "t": 0}

            def tile(kind):
                n = pos["tile"]
                pos["tile"] += 1
                pe.wait_ge(tile_loaded[n % SLOTS], 16 * (n // SLOTS + 1))
                return slot_view(n, kind)

            def bank():
                n = pos["t"]
                pos["t"] += 1
                return pt[n % 2], bank_filled[n % 2], n // 2 + 1, bank_emptied[n % 2]

            def transpose(dst, src, n=P):
                return pe.transpose(dst, src, ident[0:n, 0:n])

            def turn_tokens(src):
                for j in range(KC // 2):
                    t, filled, uses, emptied = bank()
                    pe.wait_ge(emptied, uses)
                    for k in range(2):
                        for q in range(QT):
                            o = (2 * j + k) * P
                            ins = transpose(t[:, k * S + q * P:k * S + q * P + P], src[:, q, o:o + P])
                    ins.then_inc(filled, 1)

            def token_tile(w, n, src, used=True):
                t, filled, uses, emptied = bank()
                pe.wait_ge(emptied, uses)
                for q in range(QT):
                    for k in range(KC):
                        ins = pe.matmul(t[:, q * 256:q * 256 + n], src[:, k, q * P:q * P + P], w[:, k, 0:n],
                                        start=(k == 0), stop=(k == KC - 1))
                ins.then_inc(filled, 1)
                return ins

            def mark_used():
                pe.drain().then_inc(tile_used, 1)

            def attention(batches, layer1=False, after=None):
                def scores(b):
                    if pos.get("sb", 0):
                        pe.wait_ge(scores_taken, due("scores_taken"))
                    pos["sb"] = 1
                    for j in range(4):
                        qc, base = b.q[j]
                        ins = pe.matmul(pacc[:, j * 512:j * 512 + b.nk],
                                        qTv[base:base + HD, qc, b.qt * P:b.qt * P + P], attention_view(b, j),
                                        start=True, stop=True)
                    ins.then_inc(scores_done, 1)

                def output(b, i):
                    pe.wait_ge(prob_ready, due("prob_ready"))
                    nkc = -(-b.nk // P)
                    for kc in range(nkc):
                        w = min(P, b.nk - kc * P)
                        t, filled, uses, emptied = bank()
                        pe.wait_ge(emptied, uses)
                        for j in range(4):
                            o = (i % 2) * 2048 + j * 512 + kc * P
                            ins = transpose(t[0:w, j * P:j * P + P], prob[:, o:o + w])
                        ins.then_inc(filled, 1)
                    pe.wait_ge(probT_ready, due("probT_ready"))
                    if pos.get("ob", 0):
                        pe.wait_ge(output_taken, due("output_taken"))
                    pos["ob"] = 1
                    for j in range(4):
                        for kc in range(nkc):
                            w = min(P, b.nk - kc * P)
                            ins = pe.matmul(po[:, j * HD:j * HD + HD],
                                            probT[0:w, kc * 512 + j * P:kc * 512 + j * P + P],
                                            value_view(b, j, kc, layer1), start=(kc == 0), stop=(kc == nkc - 1))
                    ins.then_inc(output_done, 1)

                for i in range(len(batches) + 1):
                    if i < len(batches):
                        scores(batches[i])
                        if after:
                            after()
                    if i:
                        output(batches[i - 1], i - 1)
                pe.wait_ge(scores_taken, due("scores_taken"))
                pe.wait_ge(output_taken, due("output_taken"))
                pos["sb"] = pos["ob"] = 0

            def project_out(src):
                for t in range(4):
                    w = tile(("row", D))
                    for k in range(2):
                        kc = 2 * t + k
                        for q in range(QT):
                            for h in range(2):
                                o = (2 * q + h) * 512
                                ins = pe.matmul(pacc[:, o:o + 512], src[:, kc, q * P:q * P + P],
                                                w[:, k, h * 512:h * 512 + 512], start=(kc == 0), stop=(kc == KC - 1))
                    ins.then_inc(tile_used, 1)
                pe.drain().then_inc(sum_done, 1)

            group0 = [0]

            def ffn(src, groups, experts=0, first_wait=True):
                n0, g0 = pos["tile"], group0[0]
                if first_wait:
                    for b in range(2):
                        pe.wait_ge(bank_emptied[b], (pos["t"] - b + 1) // 2 + 1)

                def group(n, u, it, first, last, tokens=S, hidden=None):
                    g = g0 + u + it * 2
                    tiles = [slot_view(n + j, kind) for j, kind in enumerate((("col", COLW), ("col", COLW), ("row", D)))]

                    def arrived(j):
                        pe.wait_ge(tile_loaded[(n + j) % SLOTS], it * 16 + 16 * ((n + j) // SLOTS + 1))

                    for cc in range(2):
                        if hidden or not first or g > 0:
                            pe.wait_ge(act_ready[cc], g)
                        for j in range(2):
                            if cc == 0:
                                arrived(j)
                            for k in range(KC):
                                ins = pe.matmul(pt[cc][:, j * S:j * S + tokens], tiles[j][:, k, cc * P:cc * P + P],
                                                src[:, k, :], start=(k == 0), stop=(k == KC - 1))
                            if cc == 1 and j == 0:
                                ins.then_inc(tile_used, 1)
                        ins.then_inc(gate_up_done[cc], 1)
                    if first and hidden:
                        hidden()
                    arrived(2)
                    for cc in range(2):
                        pe.wait_ge(act_ready[cc], g + 1)
                        for q in range(tokens // P):
                            for h in range(2):
                                o = (2 * q + h) * 512
                                ins = pe.matmul(pacc[:, o:o + 512], actb[:, cc * S + q * P:cc * S + q * P + P],
                                                tiles[2][:, cc, h * 512:h * 512 + 512],
                                                start=(first and cc == 0), stop=(last and cc == 1),
                                                skip_group_check=True)
                                if cc == 0 and q == 0 and h == 0:
                                    ins.then_inc(tile_used, 1)
                    ins.then_inc(tile_used, 1)

                if experts:
                    per = groups // 2

                    def scatter(e):
                        pe.wait_ge(y_taken, e + 1)
                        for q in range(QT):
                            for h in range(2):
                                ins = pe.matmul(spread[2 * q + h], backcur[:, q * P:q * P + P],
                                                work[:, h * 512:h * 512 + 512], start=False, stop=True,
                                                skip_group_check=True)
                        return ins

                    with pe.Fori(0, experts) as e:
                        pe.wait_ge(h_current, e + 1)
                        group(n0, 0, e * per, True, False, P, lambda: scatter(e))
                        group(n0 + 3, 1, e * per, False, False, P, True)
                        with pe.Fori(1, per) as it:
                            group(n0, 0, e * per + it, False, False, P, True)
                            group(n0 + 3, 1, e * per + it, False, True, P, True)
                    scatter(experts).then_inc(sum_done, 1)
                    pos["tile"] += 3 * groups * experts
                    group0[0] += groups * experts
                    return
                group(n0, 0, 0, True, False)
                group(n0 + 3, 1, 0, False, False)
                with pe.Fori(1, groups // 2) as it:
                    group(n0, 0, it, False, False)
                    group(n0 + 3, 1, it, False, groups % 2 == 0)
                if groups % 2:
                    n = n0 + 6 * (groups // 2)
                    g0_ = g0 + groups - 1
                    tail(n, g0_, group, g0)
                pos["tile"] += 3 * groups
                group0[0] += groups
                pe.wait_ge(tile_used, pos["tile"])
                pe.sem_inc(sum_done, 1)

            def tail(n, g, group, g0):
                group(n, g - g0, 0, False, True)

            def moe_sparse():
                for e in range(NE):
                    pe.wait_ge(picked, e + 1)
                    if e == 0:
                        for bank_ in spread:
                            pe.matmul(bank_, ident, gateb[:, 0:512], start=True, stop=True)
                    for k4 in range(2):
                        t, filled, uses, emptied = bank()
                        pe.wait_ge(emptied, uses)
                        for k in range(4):
                            o = (4 * k4 + k) * P
                            for q in range(QT):
                                ins = pe.matmul(t[:, k * P:k * P + P], wv[:, q, o:o + P], pick[:, e, q, :],
                                                start=(q == 0), stop=(q == QT - 1))
                        ins.then_inc(filled, 1)
                    if e % 2:
                        t, filled, uses, emptied = bank()
                        pe.wait_ge(emptied, uses)
                        for k in range(4):
                            ins = transpose(t[:, k * P:k * P + P], weigh[:, e - 1 + k // 2, k % 2, :])
                        ins.then_inc(filled, 1)
                ffn(hcurv, FF1 // COLW, NE)

            def moe_dense():
                for e in range(0, NE, 2):
                    t, filled, uses, emptied = bank()
                    pe.wait_ge(emptied, uses)
                    for i in range(2):
                        for q in range(QT):
                            g = logit[:, 80 + q * NE + e + i:81 + q * NE + e + i]
                            ins = pe.matmul(t[:, i * S + q * P:i * S + q * P + P], free(g, [[0, P]]), ident,
                                            start=True, stop=True)
                    ins.then_inc(filled, 1)
                for b in range(2):
                    pe.wait_ge(bank_emptied[b], (pos["t"] - b + 1) // 2 + 1)
                    pe.sem_inc(bank_filled[b], 8)
                ffn(hTv, NE * FF1 // COLW, first_wait=False)
                pos["t"] += 16

            pe.wait_ge(params, due("params", 16 * len(loads)))
            for src, n in ((rowsA, 104), (rowsB, 96), (rowsC, 64)):
                t, filled, uses, emptied = bank()
                pe.wait_ge(emptied, uses)
                transpose(t[:, 0:n], src[:, :], n).then_inc(filled, 1)
            t, filled, uses, emptied = bank()
            pe.wait_ge(emptied, uses)
            for cc in range(CC):
                ins = transpose(t[:, cc * P:cc * P + 2 * TAPS], rowsD[:, cc * P:cc * P + P], 2 * TAPS)
            ins.then_inc(filled, 1)
            pe.wait_ge(cond_ready, due("cond_ready"))

            ada_at = [0]

            def ada_tiles():
                for _ in range(ada_per):
                    i, j = ada[ada_at[0]]
                    ada_at[0] += 1
                    w = tile(("col", COLW))
                    for h in range(2):
                        o = (i * 48 + 2 * j + h) * 2
                        for k in range(KC):
                            ins = pe.matmul(pada[:, o:o + 2], w[:, k, h * P:h * P + P], condv[:, k, :],
                                            start=(k == 0), stop=(k == KC - 1))
                    ins.then_inc(tile_used, 1)

            for l in range(2):
                pe.wait_ge(normed, due("normed", QT))
                turn_tokens(wv)
                pe.wait_ge(hT_ready, due("hT_ready"))
                for n_tile, (c0, n) in enumerate(IN_TILES):
                    w = tile(("col", n))
                    if n_tile == 2:
                        for which in range(2):
                            t, filled, uses, emptied = bank()
                            pe.wait_ge(emptied, uses)
                            for v in range(2):
                                o = which * P + v * HD
                                for half in range(2):
                                    for k in range(KC):
                                        ins = pe.matmul(t[half * HD:half * HD + HD, v * S:v * S + S],
                                                        w[:, k, o:o + HD], hTv[:, k, :],
                                                        start=(k == 0), stop=(k == KC - 1))
                            ins.then_inc(filled, 1)
                    elif n_tile < 6:
                        token_tile(w, n, hTv)
                    else:
                        t, filled, uses, emptied = bank()
                        pe.wait_ge(emptied, uses)
                        for h in range(2):
                            for k in range(KC):
                                ins = pe.matmul(t[:, h * S:h * S + S], w[:, k, h * P:h * P + P], hTv[:, k, :],
                                                start=(k == 0), stop=(k == KC - 1))
                        ins.then_inc(filled, 1)
                    mark_used()
                pe.wait_ge(blocks_ready, due("blocks_ready"))
                for which in range(2):
                    w = tile(("cmp", P))
                    t, filled, uses, emptied = bank()
                    pe.wait_ge(emptied, uses)
                    for i in range(16):
                        ins = pe.matmul(t[:, 0:30], w[:, i, :], blk[:, which, i, :, :], start=(i == 0), stop=(i == 15))
                    ins.then_inc(filled, 1)
                    mark_used()
                pe.wait_ge(hidden_ready, due("hidden_ready"))
                t, filled, uses, emptied = bank()
                pe.wait_ge(emptied, uses)
                for which in range(2):
                    for v in range(2):
                        o = which * P + v * HD
                        ins = pe.matmul(t[0:NCMP, o:o + HD], hid[:, 60 + which * 30 + v * 15:60 + which * 30 + v * 15 + 15],
                                        w2v[:, l, which, :], start=True, stop=True)
                ins.then_inc(filled, 1)
                pe.wait_ge(qk_ready, due("qk_ready"))
                for q in range(QT):
                    t, filled, uses, emptied = bank()
                    pe.wait_ge(emptied, uses)
                    for cc in range(4):
                        ins = transpose(t[:, cc * P:cc * P + P], qkz[:, q, 2 * cc:2 * cc + 2, :])
                    ins.then_inc(filled, 1)
                t, filled, uses, emptied = bank()
                pe.wait_ge(emptied, uses)
                for br in range(2):
                    for q in range(QT):
                        ins = transpose(t[:, br * S + q * P:br * S + q * P + P], qkz[:, q, 8 + 2 * br:10 + 2 * br, :])
                ins.then_inc(filled, 1)
                pe.wait_ge(kcm_ready, due("kcm_ready"))
                t, filled, uses, emptied = bank()
                pe.wait_ge(emptied, uses)
                transpose(t[:, 0:NCMP], kcm[0:NCMP, 0:P], NCMP).then_inc(filled, 1)
                for _ in range(2):
                    pe.wait_ge(conv_ready, due("conv_ready"))
                    t, filled, uses, emptied = bank()
                    pe.wait_ge(emptied, uses)
                    src = y if _ == 0 else y2
                    for cc in range(CC):
                        ins = pe.matmul(t[:, 0:S], cst("ones"), src[:, cc, :], start=(cc == 0), stop=(cc == CC - 1))
                    ins.then_inc(filled, 1)
                pe.wait_ge(qT_ready, due("qT_ready"))
                attention(first_batches(), after=ada_tiles)
                if l == 1:
                    pe.drain().then_inc(ada_done, 1)
                pe.wait_ge(attended, due("attended"))
                for j in range(2):
                    t, filled, uses, emptied = bank()
                    pe.wait_ge(emptied, uses)
                    for k in range(2):
                        for q in range(QT):
                            o = (2 * j + k) * P
                            ins = transpose(t[:, k * S + q * P:k * S + q * P + P], work[:, q * AW + o:q * AW + o + P])
                    ins.then_inc(filled, 1)
                pe.wait_ge(mixed_attn, due("mixed_attn"))
                pe.wait_ge(mixed_conv, due("mixed_conv"))
                project_out(hTv)
                pe.wait_ge(normed, due("normed", QT))
                turn_tokens(wv)
                pe.wait_ge(hT_ready, due("hT_ready"))
                if l == 0:
                    ffn(hTv, FF1 // COLW)
                else:
                    t, filled, uses, emptied = bank()
                    pe.wait_ge(emptied, uses)
                    for q in range(QT):
                        for k in range(KC):
                            ins = pe.matmul(t[:, q * NE:q * NE + NE], hTv[:, k, q * P:q * P + P],
                                            router[:, k * NE:k * NE + NE], start=(k == 0), stop=(k == KC - 1))
                    ins.then_inc(filled, 1)
                    pe.wait_ge(gates_ready, due("gates_ready"))
                    t, filled, uses, emptied = bank()
                    pe.wait_ge(emptied, uses)
                    for o, left, right in ((0, ("before",), (0,)), (8, ("ones", "before"), (0, 1)),
                                           (16, ("ones", "ones"), (0, 1))):
                        for m, (name, q) in enumerate(zip(left, right)):
                            ins = pe.matmul(t[:, o:o + NE], cst(name), route[:, q * NE:q * NE + NE],
                                            start=(m == 0), stop=(m == len(left) - 1))
                    ins.then_inc(filled, 1)
                    pe.wait_ge(routed, 1)
                    fullest = pe.value_load(most[0:1, 0:1], min_val=0, max_val=S)
                    state = dict(pos), group0[0]
                    with pe.If(fullest <= P):
                        moe_sparse()
                    pos.update(state[0])
                    group0[0] = state[1]
                    with pe.If(fullest > P):
                        moe_dense()

            def gate_rows(i, j, s):
                for h in range(2):
                    t, filled, uses, emptied = bank()
                    pe.wait_ge(emptied, uses)
                    for k in range(4):
                        ins = pe.matmul(t[:, k * P:k * P + P],
                                        free(modv[:, i, 8 * j + 4 * h + k, s:s + 1], [[0, P]]), ident,
                                        start=True, stop=True)
                    ins.then_inc(filled, 1)

            def turn_heads(src, width, first, nheads):
                for q in range(QT):
                    for c4 in range(0, nheads // 2, 4):
                        t, filled, uses, emptied = bank()
                        pe.wait_ge(emptied, uses)
                        m = min(4, nheads // 2 - c4)
                        for k in range(m):
                            cc = c4 + k
                            o = q * width + first + cc * P
                            ins = transpose(t[:, k * P:k * P + P], src[:, o:o + P])
                        ins.then_inc(filled, 1)

            def mixer_end(i, s, src):
                pe.wait_ge(attended, due("attended"))
                turn_tokens(wv)
                pe.wait_ge(mixed_attn, due("mixed_attn"))
                project_out(src)
                gate_rows(i, 2, s)
                pe.wait_ge(normed, due("normed", QT))
                turn_tokens(wv)
                pe.wait_ge(hT_ready, due("hT_ready"))
                ffn(src, FF2 // COLW)
                gate_rows(i, 5, s)

            for i in range(2):
                for s in range(2):
                    pe.wait_ge(normed, due("normed", QT))
                    turn_tokens(wv)
                pe.wait_ge(hT_ready, due("hT_ready", 2))
                ntiles = 6 if i == 0 else 12
                for n in range(ntiles):
                    w = tile(("col", COLW))
                    token_tile(w, COLW, hTv)
                    if i == 0 or n >= 4:
                        token_tile(w, COLW, hTcv)
                    mark_used()
                pe.wait_ge(qk_ready, due("qk_ready"))
                if i == 0:
                    turn_heads(big, 1536, 0, 16)
                    turn_heads(big, 1536, 1024, 4)
                    turn_heads(bigc, 1536, 1024, 4)
                else:
                    turn_heads(big, 3072, 0, 16)
                    turn_heads(big, 3072, 1024, 16)
                    turn_heads(bigc, 2048, 0, 16)
                pe.wait_ge(qT_ready, due("qT_ready"))
                attention(swa_batches(False) if i == 0 else na_batches(), layer1=(i == 1))
                mixer_end(i, 0, hTv)
                if i == 0:
                    turn_heads(bigc, 1536, 0, 16)
                    pe.wait_ge(qT_ready, due("qT_ready"))
                    attention(swa_batches(True))
                    mixer_end(0, 1, hTv)

        @block.scalar
        def _(act):
            due = counter()
            for dst, src in loads:
                act.dma_start(dst, src).then_inc(params, 16)
            act.wait_ge(pos_clear, 1)
            for dst, src in pos_loads:
                act.dma_start(dst, src, allow_slow_non_contiguous=True).then_inc(positions, 16)

            def norm_stats(src):
                act.wait_ge(x_ready, due("x_ready"))
                for q in range(QT):
                    act.activation(prob[:, 2048 + q * D:2048 + q * D + D], src[:, q, :], ACT.Square,
                                   accum_out=den[:, q:q + 1]).then_inc(squares, 1)
                root(den[:, 2:2 + QT])

            def root(v):
                act.wait_ge(root_in, due("root_in"))
                act.activation(v, v, ACT.Sqrt).then_inc(root_out, 1)

            def exps(batches):
                for i, b in enumerate(batches):
                    act.wait_ge(shifted, due("shifted"))
                    for j in range(4):
                        o = (i % 2) * 2048 + j * 512
                        ins = act.activation(prob[:, o:o + b.nk], prob[:, o:o + b.nk], ACT.Exp,
                                             bias=den[:, 8 + (i % 2) * 4 + j:9 + (i % 2) * 4 + j],
                                             accum_out=den[:, 16 + (i % 2) * 4 + j:17 + (i % 2) * 4 + j])
                    if b.sink:
                        ins.then_inc(exp_main, 1)
                        v = den[:, 24 + (i % 2) * 4:28 + (i % 2) * 4]
                        act.activation(v, v, ACT.Exp).then_inc(exp_sink, 1)
                        act.wait_ge(exp_main, due("exp_main"))
                        act.wait_ge(exp_sink, due("exp_sink"))
                        act.sem_inc(prob_ready, 1)
                        act.sem_inc(denominators, 1)
                    else:
                        ins.then_inc(exp_main, 1)
                        act.wait_ge(exp_main, due("exp_main"))
                        act.sem_inc(prob_ready, 1)
                        act.sem_inc(denominators, 1)

            group0 = [0]

            def ffn(groups):
                g0 = group0[0]

                def one(g, before=True):
                    for cc in range(2):
                        act.wait_ge(gate_up_done[cc], g + 1)
                        if before:
                            act.wait_ge(act_ready[cc], g)
                        act.activation(silu[:, cc * S:cc * S + S], pt[cc][:, 0:S], ACT.Silu)\
                           .then_inc(silu_ready[cc], 1)

                one(g0, before=g0 > 0)
                with act.Fori(1, groups) as it:
                    one(it + g0)
                group0[0] += groups

            act.wait_ge(cond_raw, due("cond_raw"))
            act.activation(condv, condv, ACT.Silu).then_inc(cond_ready, 1)
            act.wait_ge(angles, due("angles"))
            act.activation(ang[:, 24:72], ang[:, 24:72], ACT.Sin).then_inc(sines, 1)

            for l in range(2):
                norm_stats(xv)
                act.wait_ge(gate_logits, due("gate_logits"))
                act.activation(glog, glog, ACT.Sigmoid).then_inc(gates_sigmoid, 1)
                act.wait_ge(u_ready, due("u_ready"))
                act.activation(ug[:, 4:8, :], ug[:, 4:8, :], ACT.Sigmoid).then_inc(conv_gate, 1)
                act.wait_ge(hidden_raw, due("hidden_raw"))
                act.activation(hid[:, 60:120], hid[:, 0:60], ACT.Gelu_apprx_tanh).then_inc(hidden_ready, 1)
                root(small[:, 64:88])
                root(small[0:NCMP, 96:98])
                root(y2[:, 0, :])
                act.wait_ge(conv_normed, due("conv_normed"))
                for cc in range(CC):
                    ins = act.activation(hTv[:, CC + cc, :], y[:, cc, :], ACT.Silu,
                                         scale=colA[:, COL["conv_ln_g"] + CC * l + cc:COL["conv_ln_g"] + CC * l + cc + 1],
                                         bias=colA[:, COL["conv_ln_b"] + CC * l + cc:COL["conv_ln_b"] + CC * l + cc + 1])
                ins.then_inc(mixed_conv, 1)
                exps(first_batches())
                norm_stats(xv)
                if l == 0:
                    ffn(FF1 // COLW)
                else:
                    act.wait_ge(top_shifted, due("top_shifted"))
                    act.activation(logit[:, 64:66], logit[:, 64:66], ACT.Exp).then_inc(top_exp, 1)
                    ffn(NE * FF1 // COLW)
            for i in range(2):
                norm_stats(xv)
                norm_stats(xcv)
                root(small[:, 0:(80, 96)[i]])
                exps(swa_batches(False) if i == 0 else na_batches())
                norm_stats(xv)
                ffn(FF2 // COLW)
                if i == 0:
                    exps(swa_batches(True))
                    norm_stats(xcv)
                    ffn(FF2 // COLW)

        @block.vector
        def _(ve):
            due = counter()
            pos = {"t": 0}
            chain = [0]

            def link(ins):
                chain[0] += 1
                ins.then_inc(vector_chain, 1)
                ve.wait_ge(vector_chain, chain[0])

            def go(ins):
                chain[0] += 1
                ins.then_inc(vector_chain, 1)

            def settle():
                ve.wait_ge(vector_chain, chain[0])

            def tell(name, k=1):
                settle()
                ve.sem_inc(name, k)

            def bank():
                n = pos["t"]
                pos["t"] += 1
                return pt[n % 2], bank_filled[n % 2], n // 2 + 1, bank_emptied[n % 2]

            def root():
                tell(root_in)
                ve.wait_ge(root_out, due("root_out"))

            def norm(src, gain, shift, dst, ms_only=False):
                ve.wait_ge(squares, due("squares", QT))
                link(ve.tensor_scalar(den[:, 0:QT], den[:, 0:QT], 1.0 / D, EPS, ALU.mult, ALU.add))
                link(ve.reciprocal(den[:, 2:2 + QT], den[:, 0:QT]))
                root()
                for q in range(QT):
                    ve.tensor_scalar(wv[:, q, :], src[:, q, :], den[:, 2 + q:3 + q], None, ALU.mult)\
                      .then_inc(normed, 1)
                for j in range(KC // 2):
                    t, filled, uses, emptied = bank()
                    ve.wait_ge(filled, uses)
                    for k in range(2):
                        kc = 2 * j + k
                        if shift is None:
                            go(ve.tensor_scalar(dst[:, kc, :], t[:, k * S:k * S + S], gain[:, kc:kc + 1], None, ALU.mult))
                        else:
                            go(ve.tensor_scalar(dst[:, kc, :], t[:, k * S:k * S + S], gain[:, kc:kc + 1],
                                                shift(kc), ALU.mult, ALU.add))
                    tell(emptied)
                tell(hT_ready)

            def head_norm(z, n, gains, at, sq):
                link(ve.tensor_tensor(sq, z, z, ALU.mult))
                r = small[0:z.shape[0], at:at + n]
                link(ve.tensor_reduce(r, sq, AX.X, ALU.add))
                link(ve.tensor_scalar(r, r, 1.0 / HD, EPS, ALU.mult, ALU.add))
                link(ve.reciprocal(r, r))

            def head_scale(z, n, at):
                r = small[0:z.shape[0], at:at + n]
                link(ve.tensor_tensor(z, z, free(r, [[1, n], [0, HD]]), ALU.mult))

            def rotate(x1, x2, cos, sin, shape):
                np_ = x1.shape[0]
                dims, k = [], 1
                for n in reversed(shape):
                    dims.insert(0, [k, n])
                    k *= n
                t = [free(ropet[0:np_, 256 * j:256 * j + 1], dims) for j in range(4)]
                go(ve.tensor_tensor(t[0], x1, cos, ALU.mult))
                go(ve.tensor_tensor(t[1], x2, sin, ALU.mult))
                go(ve.tensor_tensor(t[2], x2, cos, ALU.mult))
                go(ve.tensor_tensor(t[3], x1, sin, ALU.mult))
                settle()
                go(ve.tensor_tensor(x1, t[0], t[1], ALU.subtract))
                go(ve.tensor_tensor(x2, t[2], t[3], ALU.add))
                settle()

            def attention(batches, glog_=None):
                def softmax(b, i):
                    ve.wait_ge(scores_done, due("scores_done"))
                    o = (i % 2) * 2048
                    raw = pacc[:, :].rearrange("p (j k) -> p j k", j=4)
                    st = prob[:, o:o + 2048].rearrange("p (j k) -> p j k", j=4)
                    lat = min(b.nk, S)
                    if b.bias:
                        ve.wait_ge(bias_loaded[i % 2], 128 * (i // 2 + 1))
                        bb = biasb[:, (i % 2) * 1024:(i % 2) * 1024 + 1024].rearrange("p (j k) -> p j k", j=4)
                        m = cst("na")
                        link(ve.tensor_tensor(bb, bb, free(m, [[0, 4], [1, S]]), ALU.add))
                    elif b.mask:
                        w = {"cmp": NCMP, "causal": S, "swa": S}[b.mask]
                        m = cst(b.mask)[:, b.qt * w:b.qt * w + lat]
                        bb = free(m, [[0, 4], [1, lat]])
                    if b.mask or b.bias:
                        go(ve.scalar_tensor_tensor(out=st[:, :, 0:lat], in0=raw[:, :, 0:lat], scalar=HD ** -0.5, in1=bb,
                                                   op0=ALU.mult, op1=ALU.add))
                        if b.nk > S:
                            go(ve.tensor_scalar(st[:, :, S:b.nk], raw[:, :, S:b.nk], HD ** -0.5, None, ALU.mult))
                    else:
                        go(ve.tensor_scalar(st[:, :, 0:b.nk], raw[:, :, 0:b.nk], HD ** -0.5, None, ALU.mult))
                    settle()
                    ve.sem_inc(scores_taken, 1)
                    if b.bias:
                        ve.sem_inc(bias_used, 1)
                    top = den[:, 8 + (i % 2) * 4:12 + (i % 2) * 4]
                    sk = den[:, 24 + (i % 2) * 4:28 + (i % 2) * 4]
                    link(ve.tensor_reduce(top, st[:, :, 0:b.nk], AX.X, ALU.max))
                    if b.sink:
                        s4 = sink[:, b.heads[0]:b.heads[0] + 4]
                        link(ve.tensor_tensor(top, top, s4, ALU.max))
                        link(ve.tensor_tensor(sk, s4, top, ALU.subtract))
                    if b.mask == "cmp":
                        link(ve.scalar_tensor_tensor(out=top, in0=top, scalar=-1e29, in1=top, op0=ALU.is_gt, op1=ALU.mult))
                    link(ve.tensor_scalar(top, top, -1.0, None, ALU.mult))
                    ve.sem_inc(shifted, 1)

                def output(b, i):
                    nkc = -(-b.nk // P)
                    for kc in range(nkc):
                        w = min(P, b.nk - kc * P)
                        t, filled, uses, emptied = bank()
                        ve.wait_ge(filled, uses)
                        go(ve.tensor_copy(probT[0:w, kc * 512:kc * 512 + 512], t[0:w, :]))
                        tell(emptied)
                    tell(probT_ready)
                    ve.wait_ge(denominators, due("denominators"))
                    den_ = den[:, 16 + (i % 2) * 4:20 + (i % 2) * 4]
                    if b.sink:
                        link(ve.tensor_tensor(den_, den_, den[:, 24 + (i % 2) * 4:28 + (i % 2) * 4], ALU.add))
                    link(ve.tensor_scalar(den_, den_, TINY, None, ALU.max))
                    link(ve.reciprocal(den_, den_))
                    h0 = b.heads[0]
                    if b.gate is not None:
                        g = free(glog[:, b.qt, 3 * h0 + b.gate:3 * h0 + b.gate + 1], [[3, 4]])
                        link(ve.tensor_tensor(den_, den_, g, ALU.mult))
                        width = AW
                    else:
                        width = D
                    dst = work[:, b.qt * width + h0 * HD:b.qt * width + h0 * HD + 4 * HD].rearrange("p (j d) -> p j d", j=4)
                    r = free(den_, [[1, 4], [0, HD]])
                    ve.wait_ge(output_done, due("output_done"))
                    src = po[:, 0:4 * HD].rearrange("p (j d) -> p j d", j=4)
                    if b.gate:
                        tmp = ropet[:, 0:4 * HD].rearrange("p (j d) -> p j d", j=4)
                        link(ve.tensor_tensor(tmp, src, r, ALU.mult))
                        link(ve.tensor_tensor(dst, dst, tmp, ALU.add))
                    else:
                        link(ve.tensor_tensor(dst, src, r, ALU.mult))
                    ve.sem_inc(output_taken, 1)

                for i in range(len(batches) + 1):
                    if i < len(batches):
                        softmax(batches[i], i)
                    if i:
                        output(batches[i - 1], i - 1)

            group0 = [0]
            ffn_tiles = list(ffn_at)

            def ffn(experts, groups, sparse=False):
                g0, n0 = group0[0], ffn_tiles.pop(0)

                def one(g, e, tokens=S):
                    for cc in range(2):
                        ve.wait_ge(silu_ready[cc], g + 1)
                        sl = silu[:, cc * S:cc * S + tokens]
                        ve.wait_ge(tile_used, g * 3 + (n0 - 3 * g0))
                        if e is not None:
                            ve.tensor_tensor(sl, sl, kT[:, bass.ds(e * S, S)], ALU.mult).then_inc(weighed[cc], 1)
                            ve.wait_ge(weighed[cc], g + (1 - g0))
                        ve.tensor_tensor(actb[:, cc * S:cc * S + tokens], sl, pt[cc][:, S:S + tokens], ALU.mult)\
                          .then_inc(act_ready[cc], 1)

                if sparse:
                    def current(e, src, off):
                        ve.wait_ge(gate_up_done[1], e * groups + g0)
                        ve.tensor_copy(hcur, src[:, bass.ds(off, D)]).then_inc(h_current, 1)

                    def taken(e):
                        ve.wait_ge(tile_used, e * (3 * groups) + n0)
                        ve.tensor_copy(backcur, back[:, bass.ds(e * S, S)]).then_inc(back_current, 1)
                        ve.wait_ge(back_current, e + 1)
                        ve.tensor_copy(work[:, 0:D], pacc[:, 0:D]).then_inc(y_taken, 1)

                    for e0, e1, src in ((0, 6, gathered[0]), (6, 8, gathered[1])):
                        with ve.Fori(e0, e1) as e:
                            current(e, src, e * D - e0 * D)
                            taken(e)
                            with ve.Fori(0, groups) as it:
                                one(e * groups + it + g0, None, P)
                    ve.wait_ge(tile_used, experts * 3 * groups + n0)
                    ve.tensor_copy(backcur, back[:, experts * S:(experts + 1) * S]).then_inc(back_current, 1)
                    ve.wait_ge(back_current, experts + 1)
                    ve.tensor_copy(work[:, 0:D], pacc[:, 0:D]).then_inc(y_taken, 1)
                    group0[0] += groups * experts
                    return
                if experts:
                    with ve.Fori(0, experts) as e:
                        with ve.Fori(0, groups) as it:
                            one(e * groups + it + g0, e)
                    groups *= experts
                else:
                    with ve.Fori(0, groups) as it:
                        one(it + g0, None)
                group0[0] += groups

            def moe_sparse():
                go(ve.memset(gateb[:, 0:512], 0.0))
                go(ve.memset(back[:, 0:S], 0.0))
                g = colA[:, COL["ffn_norm_g"] + KC:COL["ffn_norm_g"] + 2 * KC]
                for e in range(NE):
                    for q in range(QT):
                        r = route[:, 16 + q * NE + e:17 + q * NE + e]
                        go(ve.tensor_scalar(pick[:, e, q, :], cst("iota"), r, None, ALU.is_equal))
                        go(ve.tensor_scalar(weigh[:, e, q, :], cst("iota"), r,
                                            logit[:, 80 + q * NE + e:81 + q * NE + e], ALU.is_equal, ALU.mult))
                    tell(picked)
                    if e:
                        take_gathered(e - 1, g)
                take_gathered(NE - 1, g)
                ffn(NE, FF1 // COLW, sparse=True)
                ve.wait_ge(sum_done, due("sum_done"))
                for i in range(4):
                    go(ve.tensor_tensor(x[:, 512 * i:512 * i + 512], x[:, 512 * i:512 * i + 512], spread[i], ALU.add))
                settle()

            def take_gathered(e, g):
                buf, o = (gathered[0], e * D) if e < 6 else (gathered[1], (e - 6) * D)
                for k4 in range(2):
                    t, filled, uses, emptied = bank()
                    ve.wait_ge(filled, uses)
                    go(ve.tensor_tensor(buf[:, o + 512 * k4:o + 512 * k4 + 512].rearrange("p (k t) -> p k t", k=4),
                                        t[:, :].rearrange("p (k t) -> p k t", k=4),
                                        free(g[:, 4 * k4:4 * k4 + 1], [[1, 4], [0, P]]), ALU.mult))
                    tell(emptied)
                if e % 2:
                    t, filled, uses, emptied = bank()
                    ve.wait_ge(filled, uses)
                    go(ve.tensor_copy(back[:, e * S:(e + 2) * S], t[:, :]))
                    tell(emptied)

            def moe_dense(after):
                for e in range(0, NE, 2):
                    t, filled, uses, emptied = bank()
                    ve.wait_ge(filled, uses)
                    go(ve.tensor_copy(kT[:, e * S:(e + 2) * S], t[:, :]))
                    tell(emptied)
                for b in range(2):
                    ve.sem_inc(bank_emptied[b], 8)
                pos["t"] += 16
                ffn(NE, FF1 // COLW)
                ve.wait_ge(sum_done, due("sum_done", 0))
                link(ve.tensor_tensor(x[:, :], x[:, :], pacc[:, :], ALU.add))
                ve.sem_inc(vector_chain, after - chain[0])
                chain[0] = after
                settle()

            def add_sum(dst):
                ve.wait_ge(sum_done, due("sum_done"))
                link(ve.tensor_tensor(dst[:, :], dst[:, :], pacc[:, :], ALU.add))

            def add_gated(dst):
                for h in range(2):
                    t, filled, uses, emptied = bank()
                    ve.wait_ge(filled, uses)
                    go(ve.tensor_copy(gateb[:, 512 * h:512 * h + 512], t[:, :]))
                    tell(emptied)
                ve.wait_ge(sum_done, due("sum_done"))
                for q in range(QT):
                    go(ve.tensor_tensor(wv[:, q, :], pacc[:, q * D:q * D + D], gateb[:, :], ALU.mult))
                settle()
                link(ve.tensor_tensor(dst[:, :], dst[:, :], work[:, :], ALU.add))

            def attn_to_mix(n, dst):
                ve.sem_inc(attended, 1)
                for j in range(n // 2):
                    t, filled, uses, emptied = bank()
                    ve.wait_ge(filled, uses)
                    go(ve.tensor_copy(dst[:, 2 * j:2 * j + 2, :], t[:, :].rearrange("p (k t) -> p k t", k=2)))
                    tell(emptied)
                tell(mixed_attn)

            for b in range(2):
                ve.sem_inc(bank_emptied[b], 1)
            link(ve.memset(posi[:, :], 0))
            ve.sem_inc(pos_clear, 1)
            t, filled, uses, emptied = bank()
            ve.wait_ge(filled, uses)
            go(ve.tensor_copy(colA[:, :], t[:, 0:104]))
            go(ve.tensor_copy(free(condv[:, 0, 0:1], [[1, 2], [2, KC]]),
                              t[:, COL["cond"]:COL["cond"] + 16].rearrange("p (s k) -> p s k", s=2)))
            tell(emptied)
            tell(cond_raw)
            t, filled, uses, emptied = bank()
            ve.wait_ge(filled, uses)
            go(ve.tensor_copy(colB[:, :], t[:, 0:96]))
            tell(emptied)
            t, filled, uses, emptied = bank()
            ve.wait_ge(filled, uses)
            go(ve.tensor_copy(colC[:, :], t[:, 0:64]))
            tell(emptied)
            t, filled, uses, emptied = bank()
            ve.wait_ge(filled, uses)
            go(ve.tensor_copy(convv, t[:, :].rearrange("p (c n) -> p c n", c=CC)[:, :, 0:2 * TAPS]))
            tell(emptied)
            ve.wait_ge(positions, 16 * len(pos_loads))
            ve.wait_ge(params, 16 * len(loads))
            ve.sem_inc(x_ready, 1)
            link(ve.tensor_copy(posf[:, :], posi[:, :]))
            an, kk = ang[:, 0:24], ang[:, 72:96]
            for s in range(3):
                go(ve.tensor_scalar(an[:, 8 * s:8 * s + 8], cst("freq"), posf[:, s:s + 1], None, ALU.mult))
            settle()
            link(ve.tensor_scalar(kk, an, 1.0 / (2 * math.pi), MAGIC, ALU.mult, ALU.add))
            link(ve.tensor_scalar(kk, kk, -MAGIC, None, ALU.add))
            for part in TWO_PI:
                link(ve.scalar_tensor_tensor(out=an, in0=kk, scalar=-part, in1=an, op0=ALU.mult, op1=ALU.add))
            link(ve.tensor_scalar(an, an, 3.1415925, -3.1415925, ALU.min, ALU.max))
            go(ve.tensor_copy(ang[:, 24:48], an))
            go(ve.tensor_scalar(ang[:, 48:72], an, 0.5, None, ALU.mult))
            tell(angles)
            ve.wait_ge(sines, due("sines"))
            go(ve.tensor_copy(sin1[:, :], ang[:, 24:48]))
            link(ve.tensor_tensor(kk, ang[:, 48:72], ang[:, 48:72], ALU.mult))
            link(ve.tensor_scalar(cos1[:, :], kk, -2.0, 1.0, ALU.mult, ALU.add))
            link(ve.memset(padded[:, :, 0:TAPS - 1], 0.0))

            def gains(name, l):
                o = COL[name] + KC * l
                return colA[:, o:o + KC]

            for l in range(2):
                norm(xv, gains("attn_norm_g", l), None, hTv)
                for j in range(2):
                    t, filled, uses, emptied = bank()
                    ve.wait_ge(filled, uses)
                    go(ve.tensor_copy(qkz[:, :, j:j + 7:2, :], t[:, :].rearrange("p (t h d) -> p t h d", t=QT, h=4)))
                    tell(emptied)
                for which in range(2):
                    t, filled, uses, emptied = bank()
                    ve.wait_ge(filled, uses)
                    go(ve.tensor_copy(kvp[0:64, which, :, :], t[0:64, :].rearrange("p (v t) -> p v t", v=2)))
                    go(ve.tensor_copy(kvp[64:128, which, :, 0:S - 1],
                                      t[64:128, :].rearrange("p (v t) -> p v t", v=2)[:, :, 1:S]))
                    tell(emptied)
                    for v in range(2):
                        src = free(kvp[:, which, v, 0:1], [[2, 16], [16, NCMP]])
                        pe_ = free(colC[:, 32 * which + 16 * l:32 * which + 16 * l + 1], [[1, 16], [0, NCMP]])
                        go(ve.tensor_tensor(blk[:, which, :, v, :], src, pe_, ALU.add))
                tell(blocks_ready)
                for br in range(2):
                    t, filled, uses, emptied = bank()
                    ve.wait_ge(filled, uses)
                    go(ve.tensor_copy(qkz[:, :, 8 + 2 * br:10 + 2 * br, :],
                                      t[:, :].rearrange("p (t h d) -> p t h d", t=QT, h=4)[:, :, 0:2, :]))
                    go(ve.tensor_copy(val1[:, :, 128 * br:128 * br + 128],
                                      t[:, :].rearrange("p (t n) -> p t n", t=QT)[:, :, 128:256]))
                    tell(emptied)
                t, filled, uses, emptied = bank()
                ve.wait_ge(filled, uses)
                go(ve.tensor_copy(glog, t[:, :].rearrange("p (t n) -> p t n", t=QT)[:, :, 0:24]))
                tell(emptied)
                tell(gate_logits)
                for j in range(4):
                    t, filled, uses, emptied = bank()
                    ve.wait_ge(filled, uses)
                    go(ve.tensor_copy(ug[:, 2 * j:2 * j + 2, :], t[:, :].rearrange("p (k t) -> p k t", k=2)))
                    tell(emptied)
                tell(u_ready)
                for which in range(2):
                    t, filled, uses, emptied = bank()
                    ve.wait_ge(filled, uses)
                    go(ve.tensor_copy(hid[:, 30 * which:30 * which + 30], t[:, 0:30]))
                    tell(emptied)
                tell(hidden_raw)
                z = big[:, 0:QT * 12 * HD].rearrange("p (h d) -> p h d", d=HD)
                sq = work[:, 0:QT * 12 * HD].rearrange("p (h d) -> p h d", d=HD)
                head_norm(z, 24, None, 64, sq)
                root()
                head_scale(z, 24, 64)
                for q in range(QT):
                    for h0, nh, g in ((0, 8, 0), (8, 2, 1), (10, 2, 2)):
                        v = qkz[:, q, h0:h0 + nh, :]
                        go(ve.tensor_tensor(v, v, free(gain1[:, 256 * l + 64 * g:256 * l + 64 * g + 1], [[0, nh], [1, HD]]), ALU.mult))
                settle()
                for q in range(QT):
                    rotate(qkz[:, q, :, 0:8], qkz[:, q, :, 8:16], free(cos1[:, 8 * q:8 * q + 1], [[0, 12], [1, 8]]),
                           free(sin1[:, 8 * q:8 * q + 1], [[0, 12], [1, 8]]), (12, 8))
                ve.sem_inc(qk_ready, 1)
                t, filled, uses, emptied = bank()
                ve.wait_ge(filled, uses)
                go(ve.tensor_copy(kcm[0:NCMP, :], t[0:NCMP, 0:256]))
                tell(emptied)
                for q in range(QT):
                    t, filled, uses, emptied = bank()
                    ve.wait_ge(filled, uses)
                    go(ve.tensor_copy(qTv[:, 0:4, q * P:q * P + P], t[:, :].rearrange("p (c t) -> p c t", c=4)))
                    tell(emptied)
                t, filled, uses, emptied = bank()
                ve.wait_ge(filled, uses)
                go(ve.tensor_copy(kT[:, 0:512], t[:, :]))
                tell(emptied)
                z = kcm[0:NCMP, 0:128].rearrange("p (h d) -> p h d", d=HD)
                head_norm(z, 2, None, 96, work[0:NCMP, 0:128].rearrange("p (h d) -> p h d", d=HD))
                root()
                head_scale(z, 2, 96)
                link(ve.tensor_tensor(z, z, free(gain1[0:NCMP, 256 * l + 192:256 * l + 193], [[0, 2], [1, HD]]), ALU.mult))
                rotate(z[:, :, 0:8], z[:, :, 8:16], free(cos1[0:NCMP, 16:17], [[0, 2], [1, 8]]),
                       free(sin1[0:NCMP, 16:17], [[0, 2], [1, 8]]), (2, 8))
                ve.sem_inc(kcm_ready, 1)
                t, filled, uses, emptied = bank()
                ve.wait_ge(filled, uses)
                go(ve.tensor_copy(kcT[:, 0:NCMP], t[:, 0:NCMP]))
                tell(emptied)
                ve.wait_ge(conv_gate, due("conv_gate"))
                link(ve.tensor_tensor(padded[:, :, TAPS - 1:], ug[:, 0:4, :], ug[:, 4:8, :], ALU.mult))
                for k in range(TAPS):
                    for cc in range(CC):
                        wk = convv[:, cc, l * TAPS + k:l * TAPS + k + 1]
                        src = padded[:, cc, k:k + S]
                        if k == 0:
                            o = COL["conv_b"] + CC * l + cc
                            go(ve.tensor_scalar(y[:, cc, :], src, wk, colA[:, o:o + 1], ALU.mult, ALU.add))
                        else:
                            go(ve.scalar_tensor_tensor(out=y[:, cc, :], in0=src, scalar=wk, in1=y[:, cc, :],
                                                       op0=ALU.mult, op1=ALU.add))
                    settle()
                ve.sem_inc(conv_ready, 1)
                t, filled, uses, emptied = bank()
                ve.wait_ge(filled, uses)
                link(ve.scalar_tensor_tensor(out=y, in0=free(t[:, 0:1], [[0, CC], [1, S]]), scalar=-1.0 / CW, in1=y,
                                             op0=ALU.mult, op1=ALU.add))
                ve.sem_inc(emptied, 1)
                link(ve.tensor_tensor(y2, y, y, ALU.mult))
                ve.sem_inc(conv_ready, 1)
                t, filled, uses, emptied = bank()
                ve.wait_ge(filled, uses)
                link(ve.tensor_scalar(y2[:, 0, :], t[:, 0:S], 1.0 / CW, EPS, ALU.mult, ALU.add))
                ve.sem_inc(emptied, 1)
                link(ve.reciprocal(y2[:, 0, :], y2[:, 0, :]))
                root()
                link(ve.tensor_tensor(y, y, free(y2[:, 0, 0:1], [[0, CC], [1, S]]), ALU.mult))
                ve.sem_inc(conv_normed, 1)
                ve.wait_ge(gates_sigmoid, due("gates_sigmoid"))
                ve.sem_inc(qT_ready, 1)
                attention(first_batches())
                attn_to_mix(4, hTv)
                if l == 1:
                    ve.wait_ge(ada_done, 1)
                    src = pada[:, 0:192].rearrange("p (l c s) -> p l c s", l=2, c=48)
                    for i in range(2):
                        go(ve.tensor_tensor(modv[:, i, :, :], src[:, i, :, :],
                                            free(colB[:, 48 * i:48 * i + 1], [[1, 48], [0, 2]]), ALU.add))
                    settle()
                add_sum(x)
                ve.sem_inc(x_ready, 1)
                norm(xv, gains("ffn_norm_g", l), None, hTv)
                if l == 0:
                    ffn(0, FF1 // COLW)
                else:
                    lg = logit[:, 0:16].rearrange("p (t e) -> p t e", t=QT)
                    t, filled, uses, emptied = bank()
                    ve.wait_ge(filled, uses)
                    go(ve.tensor_copy(logit[:, 0:16], t[:, 0:16]))
                    tell(emptied)
                    for q in range(QT):
                        link(ve.max(logit[:, 16 + 8 * q:24 + 8 * q], logit[:, 8 * q:8 * q + 8]))
                        link(ve.max_index(top_i[:, 8 * q:8 * q + 8], logit[:, 16 + 8 * q:24 + 8 * q], logit[:, 8 * q:8 * q + 8]))
                    link(ve.tensor_copy(logit[:, 32:48], top_i[:, :]))
                    for q in range(QT):
                        link(ve.tensor_tensor(logit[:, 64 + q:65 + q], logit[:, 17 + 8 * q:18 + 8 * q],
                                              logit[:, 16 + 8 * q:17 + 8 * q], ALU.subtract))
                    ve.sem_inc(top_shifted, 1)
                    ve.wait_ge(top_exp, due("top_exp"))
                    link(ve.tensor_scalar(logit[:, 66:68], logit[:, 64:66], 1.0, None, ALU.add))
                    link(ve.reciprocal(logit[:, 66:68], logit[:, 66:68]))
                    link(ve.tensor_tensor(logit[:, 68:70], logit[:, 64:66], logit[:, 66:68], ALU.mult))
                    for q in range(QT):
                        link(ve.tensor_scalar(logit[:, 48:56], cst("iota")[:, 0:NE], logit[:, 32 + 8 * q:33 + 8 * q],
                                              logit[:, 66 + q:67 + q], ALU.is_equal, ALU.mult))
                        link(ve.tensor_scalar(logit[:, 56:64], cst("iota")[:, 0:NE], logit[:, 33 + 8 * q:34 + 8 * q],
                                              logit[:, 68 + q:69 + q], ALU.is_equal, ALU.mult))
                        link(ve.tensor_tensor(logit[:, 80 + 8 * q:88 + 8 * q], logit[:, 48:56], logit[:, 56:64], ALU.add))
                        link(ve.tensor_scalar(logit[:, 48:56], cst("iota")[:, 0:NE], logit[:, 32 + 8 * q:33 + 8 * q],
                                              None, ALU.is_equal))
                        link(ve.tensor_scalar(logit[:, 56:64], cst("iota")[:, 0:NE], logit[:, 33 + 8 * q:34 + 8 * q],
                                              None, ALU.is_equal))
                        link(ve.tensor_tensor(route[:, 8 * q:8 * q + 8], logit[:, 48:56], logit[:, 56:64], ALU.add))
                    ve.sem_inc(gates_ready, 1)
                    t, filled, uses, emptied = bank()
                    ve.wait_ge(filled, uses)
                    link(ve.scalar_tensor_tensor(out=route[:, 16:32], in0=t[:, 0:16], scalar=1.0, in1=route[:, 0:16],
                                                 op0=ALU.add, op1=ALU.mult))
                    link(ve.tensor_scalar(route[:, 16:32], route[:, 16:32], -1.0, None, ALU.add))
                    link(ve.tensor_reduce(route[:, 40:41], t[:, 16:24], AX.X, ALU.max))
                    ve.sem_inc(emptied, 1)
                    link(ve.tensor_copy(most[:, :], route[:, 40:41]))
                    ve.sem_inc(routed, 1)
                    fullest = ve.value_load(most[0:1, 0:1], min_val=0, max_val=S)
                    state = dict(pos), group0[0], list(ffn_tiles), chain[0]
                    with ve.If(fullest <= P):
                        moe_sparse()
                    after = chain[0]
                    pos.update(state[0])
                    group0[0] = state[1]
                    ffn_tiles[:] = state[2]
                    chain[0] = state[3]
                    with ve.If(fullest > P):
                        moe_dense(after)
                    ve.sem_inc(x_ready, 1)
                    continue
                add_sum(x)
                ve.sem_inc(x_ready, 1)

            def modulated(src, i, which, s, name, dst):
                sc = modv[:, i, 8 * (3 * which + 1):8 * (3 * which + 2), s]
                link(ve.scalar_tensor_tensor(out=gsc[:, :], in0=sc, scalar=1.0, in1=gains(name, i),
                                             op0=ALU.add, op1=ALU.mult))
                norm(src, gsc, lambda kc: modv[:, i, 8 * 3 * which + kc, s:s + 1], dst)

            def project_evac(i):
                for n in range(6 if i == 0 else 12):
                    w = (1536, 3072)[i]
                    def place(buf, w, m):
                        if i == 0 and m < 4:
                            v = buf[:, 0:QT * w].rearrange("p (t h d) -> p t h d", t=QT, d=HD)
                            o = 8 * (m // 2) + m % 2
                            t, filled, uses, emptied = bank()
                            ve.wait_ge(filled, uses)
                            go(ve.tensor_copy(v[:, :, o:o + 7:2, :],
                                              t[:, :].rearrange("p (t h d) -> p t h d", t=QT, d=HD)))
                            tell(emptied)
                        else:
                            v = buf[:, 0:QT * w].rearrange("p (t n) -> p t n", t=QT)
                            t, filled, uses, emptied = bank()
                            ve.wait_ge(filled, uses)
                            go(ve.tensor_copy(v[:, :, 256 * m:256 * m + 256],
                                              t[:, :].rearrange("p (t n) -> p t n", t=QT)))
                            tell(emptied)

                    place(big, w, n)
                    if i == 0 or n >= 4:
                        place(bigc, (1536, 2048)[i], n - 4 * i)

            def heads_of(src, width, first, n, q):
                return src[:, q * width + first:q * width + first + n * HD].rearrange("p (h d) -> p h d", d=HD)

            def heads_norm_all(parts):
                at = 0
                for z, n, g in parts:
                    r = norms[:, at:at + n]
                    sq = work[:, 0:n * HD].rearrange("p (h d) -> p h d", d=HD)
                    link(ve.tensor_tensor(sq, z, z, ALU.mult))
                    link(ve.tensor_reduce(r, sq, AX.X, ALU.add))
                    at += n
                r = norms[:, 0:at]
                link(ve.tensor_scalar(r, r, 1.0 / HD, EPS, ALU.mult, ALU.add))
                link(ve.reciprocal(r, r))
                root()
                at = 0
                for z, n, g in parts:
                    go(ve.tensor_tensor(z, z, free(norms[:, at:at + 1], [[1, n], [0, HD]]), ALU.mult))
                    at += n
                settle()
                for z, n, g in parts:
                    go(ve.tensor_tensor(z, z, free(gain2[:, 64 * g:64 * g + 1], [[0, n], [1, HD]]), ALU.mult))
                settle()

            norms = small[:, 0:160]

            def heads_evac(nheads, dst, off=0):
                for q in range(QT):
                    for c4 in range(0, nheads // 2, 4):
                        m = min(4, nheads // 2 - c4)
                        t, filled, uses, emptied = bank()
                        ve.wait_ge(filled, uses)
                        go(ve.tensor_copy(dst[:, c4:c4 + m, off + q * P:off + q * P + P],
                                          t[:, 0:m * P].rearrange("p (c t) -> p c t", c=m)))
                        tell(emptied)

            kTv = kT[:, :].rearrange("p (c t) -> p c t", c=8)

            def mixer_end(i, s, res, resv, dst, last=False):
                attn_to_mix(8, dst)
                add_gated(res)
                ve.sem_inc(x_ready, 1)
                modulated(resv, i, 1, s, "g_ffn_2", dst)
                ffn(0, FF2 // COLW)
                add_gated(res)

            for i in range(2):
                if i == 1:
                    ve.sem_inc(x_ready, 1)
                modulated(xv, i, 0, 0, "g_mix_2", hTv)
                ve.sem_inc(x_ready, 1)
                modulated(xcv, i, 0, 1, "g_mix_2", hTcv)
                project_evac(i)
                if i == 0:
                    heads_norm_all([(heads_of(s_, 1536, f, n, q), n, g) for s_ in (big, bigc) for q in range(QT)
                                    for f, n, g in ((0, 16, 0), (1024, 4, 1))])
                    for q in range(QT):
                        for f, n in ((0, 16), (1024, 4)):
                            v = big[:, q * 1536 + f:q * 1536 + f + n * HD].rearrange("p (h d) -> p h d", d=HD)
                            for axis in range(2):
                                o = 32 * axis
                                rotate(v[:, :, o:o + 16], v[:, :, o + 16:o + 32],
                                       free(cst("cos2")[:, 32 * q + 16 * axis:32 * q + 16 * axis + 1], [[0, n], [1, 16]]),
                                       free(cst("sin2")[:, 32 * q + 16 * axis:32 * q + 16 * axis + 1], [[0, n], [1, 16]]), (n, 16))
                    ve.sem_inc(qk_ready, 1)
                    heads_evac(16, qTv)
                    heads_evac(4, kTv)
                    heads_evac(4, kTv, S)
                    tell(qT_ready)
                    attention(swa_batches(False))
                    mixer_end(0, 0, x, xv, hTv)
                    heads_evac(16, qTv)
                    tell(qT_ready)
                    attention(swa_batches(True))
                    mixer_end(0, 1, xc, xcv, hTv)
                else:
                    heads_norm_all([(heads_of(big, 3072, f, 16, q), 16, g) for q in range(QT) for f, g in ((0, 2), (1024, 3))]
                                   + [(heads_of(bigc, 2048, 0, 16, q), 16, 3) for q in range(QT)])
                    ve.sem_inc(qk_ready, 1)
                    heads_evac(16, qTv)
                    heads_evac(16, kTv)
                    heads_evac(16, kTv, S)
                    tell(qT_ready)
                    attention(na_batches())
                    mixer_end(1, 0, x, xv, hTv)
            ve.sem_inc(x_final, 1)


UNUSED = ("pool_", "mla_")


def kernel(**inputs):
    import concourse.bacc as bacc
    from concourse.bass_utils import run_bass_kernel_spmd

    nc = bacc.Bacc("TRN2", target_bir_lowering=False, num_devices=1)
    arrays, args = {}, {}
    laid = {n: np.ascontiguousarray(v) for n, v in inputs.items() if not n.startswith(UNUSED)}
    laid["shape_constants"] = shape_constants()
    for name, v in laid.items():
        arrays[f"in_{name}"] = v
        args[name] = nc.dram_tensor(f"in_{name}", v.shape, mybir.dt.from_np(v.dtype), kind="ExternalInput").ap()
    out = nc.dram_tensor("out_0", (1, S, D), F32, kind="ExternalOutput").ap()
    build(nc, args, out)
    r = run_bass_kernel_spmd(nc, [arrays], core_ids=[0])
    return r.results[0]["out_0"]
```

```python
import math
from contextlib import ExitStack

import numpy as np
import concourse.bass as bass
from concourse import mybir

F32 = mybir.dt.float32
I32 = mybir.dt.int32
U32 = mybir.dt.uint32
ALU = mybir.AluOpType
ACT = mybir.ActivationFunctionType
AX = mybir.AxisListType

P = 128
S = 256
QT = S // P
D = 1024
KC = D // P
HD = 64
EPS = 1e-6
NEG = -1e30
TINY = float(np.finfo(np.float32).tiny)
NCMP = 15
TAPS = 31
CW = 512
CC = CW // P
AW = 512
COLW = 256
SLOTS = 6
FF1, FF2 = 3584, 2816
NE = 8
MODS_EARLY = 16
GW = 64
GROWS = S // GW
SKW = 127
NDR = 2 * GROWS - 1
MAGIC = 12582912.0
TWO_PI = (6.28125, 0.00193500518798828125, 3.01991598196e-7)



def constant_layout():
    at, out = 0, {}
    for name, n in (("ident", P), ("ones", P), ("causal", QT * S), ("cmp", QT * NCMP), ("swa", QT * S),
                    ("na", S), ("cos2", QT * 32), ("sin2", QT * 32), ("freq", 8), ("iota", P), ("before", P)):
        out[name] = (at, n)
        at += n
    return out, at


def shape_constants():
    layout, width = constant_layout()
    c = np.zeros((P, width), np.float32)

    def put(name, a):
        at, n = layout[name]
        c[:, at:at + n] = np.asarray(a, np.float32).reshape(P, n)

    p = np.arange(P)
    t = (np.arange(QT)[None, :] * P + p[:, None])[:, :, None]
    k = np.arange(S)[None, None, :]
    put("ident", np.eye(P))
    put("ones", np.ones((P, P)))
    put("causal", np.where(k <= t, 0.0, NEG))
    put("cmp", np.where(np.arange(NCMP)[None, None, :] * 16 + 31 <= t, 0.0, NEG))
    put("swa", np.where(np.abs(k - t) <= 128, 0.0, NEG))
    start = np.clip(p % GW - 8, 0, GW - 16)[:, None]
    col = (np.arange(S) % GW)[None, :]
    put("na", np.where((col >= start) & (col < start + 16), 0.0, NEG))
    f2 = np.float32(10000.0) ** (-np.arange(16, dtype=np.float32) / np.float32(16))
    tt = t[:, :, 0]
    ang = np.stack([(tt // GW)[..., None] * f2, (tt % GW)[..., None] * f2], 2).astype(np.float32)
    put("cos2", np.cos(ang))
    put("sin2", np.sin(ang))
    f1 = np.float32(500000.0) ** (np.float32(-2.0) * np.arange(8, dtype=np.float32) / np.float32(16))
    put("freq", np.broadcast_to(f1, (P, 8)))
    put("iota", np.broadcast_to(np.arange(P), (P, P)))
    put("before", p[:, None] < p[None, :])
    return c



def free(a, dims, off=0):
    return bass.AP(tensor=a.tensor, offset=a.offset + off, ap=[list(a.ap[0])] + dims)


def rows(a, off, dims):
    return bass.AP(tensor=a.tensor, offset=a.offset + off, ap=dims)



class Batch:

    def __init__(self, qt, heads, q, k, nk, kt, v, mask, **more):
        self.qt, self.heads, self.q, self.k, self.nk, self.kt, self.v, self.mask = qt, heads, q, k, nk, kt, v, mask
        self.gate = more.get("gate")
        self.sink = more.get("sink", False)
        self.bias = more.get("bias", False)


def pair_heads(h):
    return 4 * (h // 8) + h % 4, 64 * (h // 4 % 2)


def first_batches():
    out = []
    for qt in range(QT):
        for g in range(2):
            heads = [4 * g + j for j in range(4)]
            for br, nk in ((0, NCMP), (1, P * (qt + 1)), (2, P * (qt + 1))):
                out.append(Batch(qt, heads, [pair_heads(h) for h in heads], [(0, 64 * g)] * 4, nk,
                                 "cmp" if br == 0 else ("slc", "win")[br - 1], (br, [64 * g] * 4),
                                 "cmp" if br == 0 else "causal", gate=br))
    return out


def swa_batches(ctx):
    out = []
    for qt in range(QT):
        for g in range(4):
            heads = [4 * g + j for j in range(4)]
            out.append(Batch(qt, heads, [pair_heads(h) for h in heads], [(g // 2, 64 * (g % 2))] * 4,
                             S if ctx else 2 * S, "swa_ctx" if ctx else "all",
                             (None, [1280 + 64 * g] * 4), None if ctx else "swa", sink=True))
    return out


def na_batches():
    out = []
    for qt in range(QT):
        for g in range(4):
            heads = [4 * g + j for j in range(4)]
            where = [(h // 2, 64 * (h % 2)) for h in heads]
            out.append(Batch(qt, heads, where, where, 2 * S, "all", (None, [64 * h for h in heads]), None, bias=True))
    return out


def scalar_banks():
    out, n = [], 0

    def vector(count):
        nonlocal n
        n += count

    def scalar(count=1):
        nonlocal n
        for _ in range(count):
            out.append(n % 2)
            n += 1

    def attend(batches, mods=0):
        for i, b in enumerate(batches):
            for kc in range(-(-b.nk // P)):
                scalar() if kc % 2 else vector(1)
            if i < mods:
                scalar()

    vector(4)
    for l in range(2):
        vector(4 + 2 + 2 + 2 + 1 + 4 + 2 + 1)
        vector(2 + 1 + 1)
        scalar(MODS_EARLY)
        vector(2)
        attend(first_batches(), 24 - MODS_EARLY)
        vector(4)
    vector(2 + 20)
    for i in range(2):
        vector(8 + (12, 20)[i])
        vector((4 + 2 + 2, 4 + 4 + 4)[i])
        attend(swa_batches(False) if i == 0 else na_batches())
        vector(2 + 4 + 2)
        if i == 0:
            vector(4)
            attend(swa_batches(True))
            vector(2 + 4 + 2)
    return out


def build(nc, a, out):
    ctx = ExitStack()
    with ctx:
        def sb(name, shape, dt=F32):
            return ctx.enter_context(nc.sbuf_tensor(name, shape, dt))

        def sem(name):
            return ctx.enter_context(nc.semaphore(name))

        ada_done = sem("ada_done")
        angles = sem("angles")
        bias_used = sem("bias_used")
        blocks_ready = sem("blocks_ready")
        cond_raw = sem("cond_raw")
        cond_ready = sem("cond_ready")
        conv_gate = sem("conv_gate")
        conv_normed = sem("conv_normed")
        conv_ready = sem("conv_ready")
        gate_logits = sem("gate_logits")
        gates_ready = sem("gates_ready")
        gates_sigmoid = sem("gates_sigmoid")
        hT_ready = sem("hT_ready")
        hidden_raw = sem("hidden_raw")
        hidden_ready = sem("hidden_ready")
        kcm_ready = sem("kcm_ready")
        mixed_attn = sem("mixed_attn")
        mixed_conv = sem("mixed_conv")
        normed = sem("normed")
        output_done = sem("output_done")
        output_taken = sem("output_taken")
        params = sem("params")
        params_pool = sem("params_pool")
        pos_clear = sem("pos_clear")
        positions = sem("positions")
        probT_ready = sem("probT_ready")
        prob_ready = sem("prob_ready")
        odd_copied = sem("odd_copied")
        exp_done = sem("exp_done")
        probT_odd = sem("probT_odd")
        odd_filled = sem("odd_filled")
        mod_filled = sem("mod_filled")
        mod_row = sem("mod_row")
        qT_ready = sem("qT_ready")
        qk_ready = sem("qk_ready")
        root_in = sem("root_in")
        back_current = sem("back_current")
        picked = sem("picked")
        scatter_clear = sem("scatter_clear")
        y_taken = sem("y_taken")
        h_current = sem("h_current")
        routed = sem("routed")
        root_out = sem("root_out")
        rpb_clear = sem("rpb_clear")
        rpb_loaded = sem("rpb_loaded")
        scores_done = sem("scores_done")
        scores_taken = sem("scores_taken")
        shifted = sem("shifted")
        sines = sem("sines")
        skewed = sem("skewed")
        squares = sem("squares")
        stored = sem("stored")
        sum_done = sem("sum_done")
        tile_used = sem("tile_used")
        top_exp = sem("top_exp")
        top_shifted = sem("top_shifted")
        u_ready = sem("u_ready")
        vector_chain = sem("vector_chain")
        x_final = sem("x_final")
        x_ready = sem("x_ready")
        act_ready = [sem(f"act_ready{i}") for i in range(2)]
        bank_emptied = [sem(f"bank_emptied{i}") for i in range(2)]
        bank_filled = [sem(f"bank_filled{i}") for i in range(2)]
        bias_loaded = [sem(f"bias_loaded{i}") for i in range(2)]
        gate_up_done = [sem(f"gate_up_done{i}") for i in range(2)]
        silu_ready = [sem(f"silu_ready{i}") for i in range(2)]
        tile_loaded = [sem(f"tile_loaded{i}") for i in range(SLOTS)]
        weighed = [sem(f"weighed{i}") for i in range(2)]

        layout, cwidth = constant_layout()
        ring = sb("ring", [P, SLOTS * 2048])
        const = sb("const", [P, cwidth])
        x = sb("x", [P, QT * D])
        xc = sb("xc", [P, QT * D])
        hT = sb("hT", [P, KC * S])
        big = sb("big", [P, QT * 3072])
        bigc = sb("bigc", [P, QT * 2048])
        work = sb("work", [P, QT * D])
        prob = sb("prob", [P, 2 * 4 * 512])
        hTc = prob[:, 0:KC * S]
        probT = sb("probT", [P, 4 * 4 * P])
        qT = sb("qT", [P, 8 * S])
        kT = sb("kT", [P, 8 * 2 * S])
        biasb = sb("biasb", [P, 2 * 4 * S])
        gateb = sb("gateb", [P, D])
        chunks = sb("chunks", [P, 4 * S])
        silu = chunks[:, 0:2 * S]
        actb = chunks[:, 2 * S:4 * S]
        mod = sb("mod", [P, 2 * 48 * 2])
        gsc = sb("gsc", [P, KC])
        rowsA = probT[0:104, 0:128]
        rowsB = probT[0:96, 128:256]
        rowsC = probT[0:64, 256:384]
        rowsD = probT[0:2 * TAPS, 512:1024]
        colA = sb("colA", [P, 104])
        colB = sb("colB", [P, 96])
        colC = sb("colC", [P, 64])
        convw = sb("convw", [P, CC * 2 * TAPS])
        cond = sb("cond", [P, KC * 2])
        gain1 = sb("gain1", [P, 2 * 4 * HD])
        gain2 = sb("gain2", [P, 4 * HD])
        sink = sb("sink", [P, 16])
        w2 = sb("w2", [P, 2 * 2 * HD])
        router = sb("router", [P, KC * NE])
        posi = sb("posi", [P, 3], I32)
        posf = sb("posf", [P, 3])
        ang = sb("ang", [P, 4 * 24])
        cos1 = sb("cos1", [P, 24])
        sin1 = sb("sin1", [P, 24])
        rpb = biasb[0:16, 0:NDR * SKW]
        small = sb("small", [P, 256])
        hid = sb("hid", [P, 2 * 60])
        kcm = sb("kcm", [16, 2 * 128])
        kcT = sb("kcT", [P, 16])
        logit = sb("logit", [P, 6 * 16])
        top_i = sb("top_i", [P, 16], U32)
        route = sb("route", [P, 48])
        most = sb("most", [P, 1], I32)
        modrow = sb("modrow", [2, 2 * COLW])
        den = sb("den", [P, 4 * 8])
        ropet = chunks
        skew = nc.dram_tensor("skew_scratch", [16, GW, NDR * SKW], F32, kind="Internal").ap()

        pacc = ctx.enter_context(nc.psum_tensor("pacc", [P, 2048], F32))
        pt = [ctx.enter_context(nc.psum_tensor(f"pt{i}", [P, 512], F32)) for i in range(2)]
        po = ctx.enter_context(nc.psum_tensor("po", [P, 512], F32))
        pada = ctx.enter_context(nc.psum_tensor("pada", [P, 512], F32))

        def cst(name, n=P):
            at, w = layout[name]
            return const[0:n, at:at + w]

        ident = cst("ident")
        xv = x[:, :].rearrange("p (t n) -> p t n", t=QT)
        xcv = xc[:, :].rearrange("p (t n) -> p t n", t=QT)
        hTv = hT[:, :].rearrange("p (k t) -> p k t", k=KC)
        hTcv = hTc.rearrange("p (k t) -> p k t", k=KC)
        wv = work[:, :].rearrange("p (t n) -> p t n", t=QT)
        qTv = qT[:, :].rearrange("p (c t) -> p c t", c=8)
        gathered = big[:, 0:6 * D], bigc[:, 0:2 * D]
        pick = qT[:, :].rearrange("p (e t n) -> p e t n", e=NE, t=QT)
        weigh = probT[:, :].rearrange("p (e t n) -> p e t n", e=NE, t=QT)
        back = kT[:, 0:(NE + 1) * S]
        hcur = qT[:, 0:D]
        hcurv = hcur.rearrange("p (k t) -> p k t", k=KC)
        backcur = qT[:, D:D + S]
        gx = kT[:, 0:NE * S].rearrange("p (e t) -> p e t", e=NE)
        modv = mod[:, :].rearrange("p (l c s) -> p l c s", l=2, c=48)
        condv = cond[:, :].rearrange("p (k s) -> p k s", s=2)
        qkz = big[:, 0:QT * 12 * HD].rearrange("p (t h d) -> p t h d", t=QT, h=12)
        val1 = big[:, 1536:2048].rearrange("p (t n) -> p t n", t=QT)
        ug = big[:, 2048:4096].rearrange("p (c t) -> p c t", c=8)
        padded = big[:, 4096:4096 + CC * (S + TAPS - 1)].rearrange("p (c t) -> p c t", c=CC)
        kvp = bigc[:, 0:1024].rearrange("p (w v t) -> p w v t", w=2, v=2)
        blk = bigc[:, 1024:1984].rearrange("p (w i v n) -> p w i v n", w=2, i=16, v=2)
        y = bigc[:, 1984:3008].rearrange("p (c t) -> p c t", c=CC)
        y2 = bigc[:, 3008:4032].rearrange("p (c t) -> p c t", c=CC)
        spread = [pacc[:, 1024:1536], pacc[:, 1536:2048], po[:, :], pada[:, :]]
        glog = small[:, 0:QT * 24].rearrange("p (t n) -> p t n", t=QT)
        w2v = w2[:, :].rearrange("p (l w d) -> p l w d", l=2, w=2)
        convv = convw[:, :].rearrange("p (c n) -> p c n", c=CC)

        W = {n: a[n] for n in a}
        w_in = [W["w_in"][i] for i in range(2)]
        w_out = [W["w_out"][i] for i in range(2)]
        w_ada = [W["w_ada_2"][i] for i in range(2)]
        w_gu = [W["w_gate_up_2"][i] for i in range(2)]
        w_dn = [W["w_down_2"][i] for i in range(2)]

        def col_tile(w, c0, n=COLW):
            return w[:, c0:c0 + n].rearrange("(k p) n -> p k n", p=P), ("col", n)

        def row_tile(w, t):
            return w[256 * t:256 * t + 256, :].rearrange("(a p) n -> p a n", p=P), ("row", D)

        IN_TILES = [(0, 256), (256, 256), (512, 256), (768, 256), (1024, 256), (1280, 24)] + \
                   [(1304 + 256 * j, 256) for j in range(4)]
        stream = []
        ada = [(i, j) for i in range(2) for j in range(24)]
        for l in range(2):
            stream += [("tile",) + col_tile(w_in[l], c, n) for c, n in IN_TILES]
            for w in ("cmp_w1_k", "cmp_w1_v"):
                stream.append(("tile", W[w][l].rearrange("(i p) h -> p i h", p=P), ("cmp", P)))
            for i, j in ada[l * 24:l * 24 + 24]:
                stream.append(("tile",) + col_tile(w_ada[i], 256 * j))
            stream += [("tile",) + row_tile(w_out[l], t) for t in range(4)]
            if l == 0:
                stream.append(("ffn", W["ffn_w_gate"][0], W["ffn_w_up"][0], 0, W["ffn_w_down"][0], FF1 // COLW))
            else:
                stream.append(("moe",))
        stream += [("tile",) + col_tile(W["swa_w_qkv_2"][0], 256 * j) for j in range(6)]
        swa_o = [("tile",) + row_tile(W["swa_w_o_2"][0], t) for t in range(4)]
        ffn2 = [("ffn", w_gu[i], w_gu[i], FF2, w_dn[i], FF2 // COLW) for i in range(2)]
        stream += swa_o + [ffn2[0]] + swa_o + [ffn2[0]]
        stream += [("tile",) + col_tile(W["na_w_qkv_2"][0], 256 * j) for j in range(12)]
        stream += [("tile",) + row_tile(W["na_w_o_2"][0], t) for t in range(4)] + [ffn2[1]]

        ffn_at, n = [], 0
        for item in stream:
            if item[0] != "tile":
                ffn_at.append(n)
            n += {"tile": 1, "ffn": 3 * item[-1] if item[0] == "ffn" else 0, "moe": 3 * NE * FF1 // COLW}[item[0]]

        def slot(n):
            return ring[:, (n % SLOTS) * 2048:(n % SLOTS + 1) * 2048]

        def slot_view(n, kind):
            what, w = kind
            if what == "col":
                return slot(n).rearrange("p (k n) -> p k n", k=KC)[:, :, 0:w]
            return slot(n).rearrange("p (k n) -> p k n", n=w)

        def bcast(w, off, n, rep=1):
            return rows(w, off, [[0, P]] + ([[0, rep]] if rep > 1 else []) + [[1, n]])

        loads = [(const[:, :], W["shape_constants"])]
        at = 0
        COL = {}
        for name in ("attn_norm_g", "ffn_norm_g", "conv_b", "conv_ln_g", "conv_ln_b", "g_mix_2", "g_ffn_2"):
            n = W[name].shape[0] * W[name].shape[1] // P
            loads.append((rowsA[at:at + n, :], W[name].rearrange("l (k p) -> (l k) p", p=P)))
            COL[name] = at
            at += n
        loads.append((rowsA[at:at + 8, :], W["c_2"].rearrange("b (k p) -> (b k) p", p=P)))
        loads.append((rowsA[at + 8:at + 16, :], W["c_ctx_2"].rearrange("(k p) -> k p", p=P)))
        COL["cond"] = at
        loads.append((rowsB[:, :], W["b_ada_2"].rearrange("l (k p) -> (l k) p", p=P)))
        loads.append((rowsC[0:32, :], W["cmp_pos_k"].rearrange("l (i a) d -> (l i) (a d)", a=2)))
        loads.append((rowsC[32:64, :], W["cmp_pos_v"].rearrange("l (i a) d -> (l i) (a d)", a=2)))
        loads.append((rowsD[:, :], W["conv_w"].rearrange("l k c -> (l k) c")))
        for l in range(2):
            loads.append((gain1[:, 256 * l:256 * l + 64], bcast(W["q_norm_g"], 64 * l, 64)))
            for j, br in enumerate((1, 2, 0)):
                loads.append((gain1[:, 256 * l + 64 * (j + 1):256 * l + 64 * (j + 2)],
                              bcast(W["k_norm_g"], 64 * (3 * l + br), 64)))
            loads.append((w2v[:, l, 0, :], W["cmp_w2_k"][l]))
            loads.append((w2v[:, l, 1, :], W["cmp_w2_v"][l]))
        for j, name in enumerate(("swa_g_q_2", "swa_g_k_2", "na_g_q_2", "na_g_k_2")):
            loads.append((gain2[:, 64 * j:64 * j + 64], bcast(W[name], 0, 64)))
        loads.append((sink[:, :], bcast(W["swa_sink_2"], 0, 16)))
        loads.append((router[:, :].rearrange("p (k e) -> p k e", k=KC),
                      W["moe_router"][0].rearrange("(k p) e -> p k e", p=P)))
        loads.append((xv, W["x"][0].rearrange("(t p) n -> p t n", p=P)))
        loads.append((xcv, W["ctx_2"][0].rearrange("(t p) n -> p t n", p=P)))
        pos_loads = [(posi[:, t:t + 1], rows(W["positions"], t * P, [[1, P], [1, 1]])) for t in range(QT)]
        pos_loads.append((posi[0:NCMP, 2:3], rows(W["positions"], 31, [[16, NCMP], [1, 1]])))

        bank_order = scalar_banks()

        block = ctx.enter_context(nc.Block())

        def counter():
            seen = {}

            def due(name, k=1):
                seen[name] = seen.get(name, 0) + k
                return seen[name]
            return due

        def attention_view(b, which):
            c, base = b.k[which]
            hi = base + HD
            if b.kt == "cmp":
                return kcT[base:hi, 0:NCMP]
            if b.kt in ("slc", "win"):
                o = S * (b.kt == "win")
                return kT[base:hi, o:o + b.nk]
            if b.kt == "swa_ctx":
                return kT[base:hi, c * 512 + S:c * 512 + 2 * S]
            return kT[base:hi, c * 512:c * 512 + 2 * S]

        def value_view(b, which, kc, layer1):
            br, cols = b.v
            c = cols[which]
            if br == 0:
                return kcm[0:NCMP, 128 + c:128 + c + HD]
            if br is not None:
                return val1[:, kc, (br - 1) * 128 + c:(br - 1) * 128 + c + HD]
            if layer1:
                if kc < QT:
                    return big[:, kc * 3072 + 2048 + c:kc * 3072 + 2048 + c + HD]
                o = (kc - QT) * 2048 + 1024 + c
                return bigc[:, o:o + HD]
            if b.kt == "swa_ctx":
                kc += QT
            src, o = (big, kc * 1536) if kc < QT else (bigc, (kc - QT) * 1536)
            return src[:, o + c:o + c + HD]

        @block.sync
        def _(sp):
            n = 0

            def load(n, src, kind, it=None, base=None):
                if it is not None:
                    sp.wait_ge(tile_used, it * 6 + (base - SLOTS + 1))
                elif n >= SLOTS:
                    sp.wait_ge(tile_used, n - SLOTS + 1)
                sp.dma_start(slot_view(n, kind), src).then_inc(tile_loaded[n % SLOTS], 16)

            def group_src(wg, wu, uoff, wd, g):
                c = g * COLW
                return ((wg[:, bass.ds(c, COLW)].rearrange("(k p) n -> p k n", p=P), ("col", COLW)),
                        (wu[:, bass.ds(c + uoff, COLW)].rearrange("(k p) n -> p k n", p=P), ("col", COLW)),
                        (wd[bass.ds(c, COLW), :].rearrange("(a p) n -> p a n", p=P), ("row", D)))

            for item in stream:
                if item[0] == "tile":
                    load(n, item[1], item[2])
                    n += 1
                elif item[0] == "ffn":
                    _, wg, wu, uoff, wd, groups = item
                    with sp.Fori(0, groups // 2) as it:
                        for u in range(2):
                            for j, (src, kind) in enumerate(group_src(wg, wu, uoff, wd, it * 2 + u)):
                                load(n + 3 * u + j, src, kind, it, n + 3 * u + j)
                    n += 6 * (groups // 2)
                    if groups % 2:
                        for src, kind in group_src(wg, wu, uoff, wd, groups - 1):
                            load(n, src, kind)
                            n += 1
                else:
                    wg = W["moe_w_gate"][0].rearrange("e k f -> (e k) f")
                    wu = W["moe_w_up"][0].rearrange("e k f -> (e k) f")
                    wd = W["moe_w_down"][0].rearrange("e f n -> (e f) n")
                    per = FF1 // COLW // 2
                    with sp.Fori(0, NE) as e:
                        with sp.Fori(0, per) as j:
                            for u in range(2):
                                c = j * (2 * COLW) + u * COLW
                                for k, (src, kind) in enumerate((
                                        (wg[bass.ds(e * D, D), bass.ds(c, COLW)].rearrange("(k p) n -> p k n", p=P), ("col", COLW)),
                                        (wu[bass.ds(e * D, D), bass.ds(c, COLW)].rearrange("(k p) n -> p k n", p=P), ("col", COLW)),
                                        (wd[bass.ds(e * FF1 + c, COLW), :].rearrange("(a p) n -> p a n", p=P), ("row", D)))):
                                    load(n + 3 * u + k, src, kind, e * per + j, n + 3 * u + k)
                    n += 6 * per * NE
            sp.wait_ge(x_final, 1)
            sp.dma_start(out[0].rearrange("(t p) n -> p t n", p=P), xv).then_inc(stored, 16)
            sp.wait_ge(stored, 16)

        @block.gpsimd
        def _(pool):
            for dst, src in loads[1::2]:
                pool.dma_start(dst, src).then_inc(params_pool, 16)
            pool.memset(rpb[:, :], 0.0).then_inc(rpb_clear, 1)
            pool.wait_ge(rpb_clear, 1)
            rv = rpb[:, :].rearrange("h (r n) -> h r n", r=NDR)
            pool.dma_start(rv[:, :, 48:79], W["na_rpb_2"][0, :, 4:4 + NDR, :]).then_inc(rpb_loaded, 16)
            pool.wait_ge(rpb_loaded, 16)
            pool.dma_start(skew, free(rpb[:, :], [[0, GW], [1, NDR * SKW]])).then_inc(skewed, 16)
            pool.wait_ge(skewed, 16)
            pitch = NDR * SKW
            for i, b in enumerate(na_batches()):
                if i >= 2:
                    pool.wait_ge(bias_used, i - 1)
                for rr in range(2):
                    r = 2 * b.qt + rr
                    for j in range(4):
                        src = rows(skew, (b.heads[j] * GW) * pitch + (GROWS - 1 - r) * SKW + GW - 1,
                                   [[pitch - 1, GW], [SKW, GROWS], [1, GW]])
                        dst = biasb[64 * rr:64 * rr + 64, (i % 2) * 1024 + j * S:(i % 2) * 1024 + j * S + S]
                        pool.dma_start(dst.rearrange("p (r c) -> p r c", r=GROWS), src)\
                            .then_inc(bias_loaded[i % 2], 16)

        @block.tensor
        def _(pe):
            due = counter()
            pos = {"tile": 0, "t": 0}

            def tile(kind):
                n = pos["tile"]
                pos["tile"] += 1
                pe.wait_ge(tile_loaded[n % SLOTS], 16 * (n // SLOTS + 1))
                return slot_view(n, kind)

            def bank():
                n = pos["t"]
                pos["t"] += 1
                return pt[n % 2], bank_filled[n % 2], n // 2 + 1, bank_emptied[n % 2]

            ada_at = [0]

            def ada_tiles(count):
                for _ in range(count):
                    w = tile(("col", COLW))
                    t, filled, uses, emptied = bank()
                    pe.wait_ge(emptied, uses)
                    for k in range(KC):
                        ins = pe.matmul(t[0:2, 0:COLW], condv[:, k, :], w[:, k, :], start=(k == 0), stop=(k == KC - 1))
                    ins.then_inc(mod_filled, 1)
                    mark_used()
                    if ada_at[0]:
                        turn_mod(ada_at[0] - 1)
                    ada_at[0] += 1

            def turn_mod(n):
                pe.wait_ge(mod_row, n + 1)
                for h in range(2):
                    ins = pe.transpose(pada[:, (2 * n + h) * 2:(2 * n + h) * 2 + 2],
                                       modrow[0:2, (n % 2) * COLW + h * P:(n % 2) * COLW + h * P + P], ident[0:2, 0:2])
                return ins

            def transpose(dst, src, n=P):
                return pe.transpose(dst, src, ident[0:n, 0:n])

            def turn_tokens(src):
                for j in range(KC // 2):
                    t, filled, uses, emptied = bank()
                    pe.wait_ge(emptied, uses)
                    for k in range(2):
                        for q in range(QT):
                            o = (2 * j + k) * P
                            ins = transpose(t[:, k * S + q * P:k * S + q * P + P], src[:, q, o:o + P])
                    ins.then_inc(filled, 1)

            def token_tile(w, n, src, used=True):
                t, filled, uses, emptied = bank()
                pe.wait_ge(emptied, uses)
                for q in range(QT):
                    for k in range(KC):
                        ins = pe.matmul(t[:, q * 256:q * 256 + n], src[:, k, q * P:q * P + P], w[:, k, 0:n],
                                        start=(k == 0), stop=(k == KC - 1))
                ins.then_inc(filled, 1)
                return ins

            def mark_used():
                pe.drain().then_inc(tile_used, 1)

            def attention(batches, layer1=False, mods=0):
                def scores(b):
                    if pos.get("sb", 0):
                        pe.wait_ge(scores_taken, due("scores_taken"))
                    pos["sb"] = 1
                    for j in range(4):
                        qc, base = b.q[j]
                        ins = pe.matmul(pacc[:, j * 512:j * 512 + b.nk],
                                        qTv[base:base + HD, qc, b.qt * P:b.qt * P + P], attention_view(b, j),
                                        start=True, stop=True)
                    ins.then_inc(scores_done, 1)

                def turn(b, i):
                    pe.wait_ge(prob_ready, due("prob_ready"))
                    nkc = -(-b.nk // P)
                    for kc in range(nkc):
                        w = min(P, b.nk - kc * P)
                        t, filled, uses, emptied = bank()
                        pe.wait_ge(emptied, uses)
                        for j in range(4):
                            o = (i % 2) * 2048 + j * 512 + kc * P
                            ins = transpose(t[0:w, j * P:j * P + P], prob[:, o:o + w])
                        ins.then_inc(odd_filled if kc % 2 else filled, 1)

                def output(b, i):
                    nkc = -(-b.nk // P)
                    pe.wait_ge(probT_ready, due("probT_ready"))
                    if nkc > 1:
                        pe.wait_ge(probT_odd, due("probT_odd"))
                    if not b.gate:
                        if pos.get("ob", 0):
                            pe.wait_ge(output_taken, due("output_taken"))
                        pos["ob"] = 1
                    heads = [(0, 4)] if b.k[0] == b.k[3] else [(j, 1) for j in range(4)]
                    for j, m in heads:
                        for kc in range(nkc):
                            w = min(P, b.nk - kc * P)
                            ins = pe.matmul(po[0:HD, j * P:(j + m) * P], value_view(b, j, kc, layer1),
                                            probT[0:w, kc * 512 + j * P:kc * 512 + (j + m) * P],
                                            start=(kc == 0 and not b.gate),
                                            stop=(kc == nkc - 1 and b.gate in (None, 2)))
                    if b.gate in (None, 2):
                        ins.then_inc(output_done, 1)

                scores(batches[0])
                scores(batches[1])
                for i, b in enumerate(batches):
                    turn(b, i)
                    if i + 2 < len(batches):
                        scores(batches[i + 2])
                    if i < mods:
                        ada_tiles(1)
                    output(b, i)
                pe.wait_ge(scores_taken, due("scores_taken"))
                pe.wait_ge(output_taken, due("output_taken"))
                pos["sb"] = pos["ob"] = 0

            def project_out(src):
                for t in range(4):
                    w = tile(("row", D))
                    for k in range(2):
                        kc = 2 * t + k
                        for q in range(QT):
                            for h in range(2):
                                o = (2 * q + h) * 512
                                ins = pe.matmul(pacc[:, o:o + 512], src[:, kc, q * P:q * P + P],
                                                w[:, k, h * 512:h * 512 + 512], start=(kc == 0), stop=(kc == KC - 1))
                    ins.then_inc(tile_used, 1)
                pe.drain().then_inc(sum_done, 1)

            group0 = [0]

            def ffn(src, groups, experts=0, first_wait=True):
                n0, g0 = pos["tile"], group0[0]
                if first_wait:
                    for b in range(2):
                        pe.wait_ge(bank_emptied[b], (pos["t"] - b + 1) // 2 + 1)

                def group(n, u, it, first, last, tokens=S, hidden=None):
                    g = g0 + u + it * 2
                    tiles = [slot_view(n + j, kind) for j, kind in enumerate((("col", COLW), ("col", COLW), ("row", D)))]

                    def arrived(j):
                        pe.wait_ge(tile_loaded[(n + j) % SLOTS], it * 16 + 16 * ((n + j) // SLOTS + 1))

                    for cc in range(2):
                        if hidden or not first or g > 0:
                            pe.wait_ge(act_ready[cc], g)
                        for j in range(2):
                            if cc == 0:
                                arrived(j)
                            for k in range(KC):
                                ins = pe.matmul(pt[cc][:, j * S:j * S + tokens], tiles[j][:, k, cc * P:cc * P + P],
                                                src[:, k, :], start=(k == 0), stop=(k == KC - 1))
                            if cc == 1 and j == 0:
                                ins.then_inc(tile_used, 1)
                        ins.then_inc(gate_up_done[cc], 1)
                    if first and hidden:
                        hidden()
                    arrived(2)
                    for cc in range(2):
                        pe.wait_ge(act_ready[cc], g + 1)
                        for q in range(tokens // P):
                            for h in range(2):
                                o = (2 * q + h) * 512
                                ins = pe.matmul(pacc[:, o:o + 512], actb[:, cc * S + q * P:cc * S + q * P + P],
                                                tiles[2][:, cc, h * 512:h * 512 + 512],
                                                start=(first and cc == 0), stop=(last and cc == 1),
                                                skip_group_check=True)
                                if cc == 0 and q == 0 and h == 0:
                                    ins.then_inc(tile_used, 1)
                    ins.then_inc(tile_used, 1)

                if experts:
                    per = groups // 2

                    def scatter(e):
                        pe.wait_ge(y_taken, e + 1)
                        for q in range(QT):
                            for h in range(2):
                                ins = pe.matmul(spread[2 * q + h], backcur[:, q * P:q * P + P],
                                                work[:, h * 512:h * 512 + 512], start=False, stop=True,
                                                skip_group_check=True)
                        return ins

                    with pe.Fori(0, experts) as e:
                        pe.wait_ge(h_current, e + 1)
                        group(n0, 0, e * per, True, False, P, lambda: scatter(e))
                        group(n0 + 3, 1, e * per, False, False, P, True)
                        with pe.Fori(1, per) as it:
                            group(n0, 0, e * per + it, False, False, P, True)
                            group(n0 + 3, 1, e * per + it, False, True, P, True)
                    scatter(experts).then_inc(sum_done, 1)
                    pos["tile"] += 3 * groups * experts
                    group0[0] += groups * experts
                    return
                group(n0, 0, 0, True, False)
                group(n0 + 3, 1, 0, False, False)
                with pe.Fori(1, groups // 2) as it:
                    group(n0, 0, it, False, False)
                    group(n0 + 3, 1, it, False, groups % 2 == 0)
                if groups % 2:
                    n = n0 + 6 * (groups // 2)
                    g0_ = g0 + groups - 1
                    tail(n, g0_, group, g0)
                pos["tile"] += 3 * groups
                group0[0] += groups
                pe.wait_ge(tile_used, pos["tile"])
                pe.sem_inc(sum_done, 1)

            def tail(n, g, group, g0):
                group(n, g - g0, 0, False, True)

            def moe_sparse():
                for e in range(NE):
                    pe.wait_ge(picked, e + 1)
                    if e == 0:
                        for bank_ in spread:
                            pe.matmul(bank_, ident, gateb[:, 0:512], start=True, stop=True)
                    for k4 in range(2):
                        t, filled, uses, emptied = bank()
                        pe.wait_ge(emptied, uses)
                        for k in range(4):
                            o = (4 * k4 + k) * P
                            for q in range(QT):
                                ins = pe.matmul(t[:, k * P:k * P + P], wv[:, q, o:o + P], pick[:, e, q, :],
                                                start=(q == 0), stop=(q == QT - 1))
                        ins.then_inc(filled, 1)
                    if e % 2:
                        t, filled, uses, emptied = bank()
                        pe.wait_ge(emptied, uses)
                        for k in range(4):
                            ins = transpose(t[:, k * P:k * P + P], weigh[:, e - 1 + k // 2, k % 2, :])
                        ins.then_inc(filled, 1)
                ffn(hcurv, FF1 // COLW, NE)

            def moe_dense():
                for e in range(0, NE, 2):
                    t, filled, uses, emptied = bank()
                    pe.wait_ge(emptied, uses)
                    for i in range(2):
                        for q in range(QT):
                            g = logit[:, 80 + q * NE + e + i:81 + q * NE + e + i]
                            ins = pe.matmul(t[:, i * S + q * P:i * S + q * P + P], free(g, [[0, P]]), ident,
                                            start=True, stop=True)
                    ins.then_inc(filled, 1)
                for b in range(2):
                    pe.wait_ge(bank_emptied[b], (pos["t"] - b + 1) // 2 + 1)
                    pe.sem_inc(bank_filled[b], 8)
                ffn(hTv, NE * FF1 // COLW, first_wait=False)
                pos["t"] += 16

            pe.wait_ge(params, 16 * len(loads[0::2]))
            pe.wait_ge(params_pool, 16 * len(loads[1::2]))
            for src, n in ((rowsA, 104), (rowsB, 96), (rowsC, 64)):
                t, filled, uses, emptied = bank()
                pe.wait_ge(emptied, uses)
                transpose(t[:, 0:n], src[:, :], n).then_inc(filled, 1)
            t, filled, uses, emptied = bank()
            pe.wait_ge(emptied, uses)
            for cc in range(CC):
                ins = transpose(t[:, cc * P:cc * P + 2 * TAPS], rowsD[:, cc * P:cc * P + P], 2 * TAPS)
            ins.then_inc(filled, 1)
            pe.wait_ge(cond_ready, due("cond_ready"))

            for l in range(2):
                pe.wait_ge(normed, due("normed", QT))
                turn_tokens(wv)
                pe.wait_ge(hT_ready, due("hT_ready"))
                for n_tile, (c0, n) in enumerate(IN_TILES):
                    w = tile(("col", n))
                    if n_tile == 2:
                        for which in range(2):
                            t, filled, uses, emptied = bank()
                            pe.wait_ge(emptied, uses)
                            for k in range(KC):
                                ins = pe.matmul(t[:, 0:S], w[:, k, which * P:which * P + P], hTv[:, k, :],
                                                start=(k == 0), stop=(k == KC - 1))
                            ins.then_inc(filled, 1)
                    elif n_tile < 6:
                        token_tile(w, n, hTv)
                    else:
                        t, filled, uses, emptied = bank()
                        pe.wait_ge(emptied, uses)
                        for h in range(2):
                            for k in range(KC):
                                ins = pe.matmul(t[:, h * S:h * S + S], w[:, k, h * P:h * P + P], hTv[:, k, :],
                                                start=(k == 0), stop=(k == KC - 1))
                        ins.then_inc(filled, 1)
                    mark_used()
                pe.wait_ge(blocks_ready, due("blocks_ready"))
                for which in range(2):
                    w = tile(("cmp", P))
                    t, filled, uses, emptied = bank()
                    pe.wait_ge(emptied, uses)
                    for i in range(16):
                        ins = pe.matmul(t[:, 0:30], w[:, i, :], blk[:, which, i, :, :], start=(i == 0), stop=(i == 15))
                    ins.then_inc(filled, 1)
                    mark_used()
                pe.wait_ge(hidden_ready, due("hidden_ready"))
                t, filled, uses, emptied = bank()
                pe.wait_ge(emptied, uses)
                for which in range(2):
                    for v in range(2):
                        o = which * P + v * HD
                        ins = pe.matmul(t[0:NCMP, o:o + HD], hid[:, 60 + which * 30 + v * 15:60 + which * 30 + v * 15 + 15],
                                        w2v[:, l, which, :], start=True, stop=True)
                ins.then_inc(filled, 1)
                pe.wait_ge(qk_ready, due("qk_ready"))
                for q in range(QT):
                    t, filled, uses, emptied = bank()
                    pe.wait_ge(emptied, uses)
                    for cc in range(4):
                        ins = transpose(t[:, cc * P:cc * P + P], qkz[:, q, 2 * cc:2 * cc + 2, :])
                    ins.then_inc(filled, 1)
                t, filled, uses, emptied = bank()
                pe.wait_ge(emptied, uses)
                for br in range(2):
                    for q in range(QT):
                        ins = transpose(t[:, br * S + q * P:br * S + q * P + P], qkz[:, q, 8 + 2 * br:10 + 2 * br, :])
                ins.then_inc(filled, 1)
                pe.wait_ge(kcm_ready, due("kcm_ready"))
                t, filled, uses, emptied = bank()
                pe.wait_ge(emptied, uses)
                transpose(t[:, 0:NCMP], kcm[0:NCMP, 0:P], NCMP).then_inc(filled, 1)
                ada_tiles(MODS_EARLY)
                for _ in range(2):
                    pe.wait_ge(conv_ready, due("conv_ready"))
                    t, filled, uses, emptied = bank()
                    pe.wait_ge(emptied, uses)
                    src = y if _ == 0 else y2
                    for cc in range(CC):
                        ins = pe.matmul(t[:, 0:S], cst("ones"), src[:, cc, :], start=(cc == 0), stop=(cc == CC - 1))
                    ins.then_inc(filled, 1)
                pe.wait_ge(qT_ready, due("qT_ready"))
                attention(first_batches(), mods=24 - MODS_EARLY)
                if l == 1:
                    turn_mod(ada_at[0] - 1).then_inc(ada_done, 1)
                pe.wait_ge(mixed_attn, due("mixed_attn"))
                pe.wait_ge(mixed_conv, due("mixed_conv"))
                project_out(hTv)
                pe.wait_ge(normed, due("normed", QT))
                turn_tokens(wv)
                pe.wait_ge(hT_ready, due("hT_ready"))
                if l == 0:
                    ffn(hTv, FF1 // COLW)
                else:
                    t, filled, uses, emptied = bank()
                    pe.wait_ge(emptied, uses)
                    for q in range(QT):
                        for k in range(KC):
                            ins = pe.matmul(t[:, q * NE:q * NE + NE], hTv[:, k, q * P:q * P + P],
                                            router[:, k * NE:k * NE + NE], start=(k == 0), stop=(k == KC - 1))
                    ins.then_inc(filled, 1)
                    pe.wait_ge(gates_ready, due("gates_ready"))
                    t, filled, uses, emptied = bank()
                    pe.wait_ge(emptied, uses)
                    for o, left, right in ((0, ("before",), (0,)), (8, ("ones", "before"), (0, 1)),
                                           (16, ("ones", "ones"), (0, 1))):
                        for m, (name, q) in enumerate(zip(left, right)):
                            ins = pe.matmul(t[:, o:o + NE], cst(name), route[:, q * NE:q * NE + NE],
                                            start=(m == 0), stop=(m == len(left) - 1))
                    ins.then_inc(filled, 1)
                    pe.wait_ge(routed, 1)
                    fullest = pe.value_load(most[0:1, 0:1], min_val=0, max_val=S)
                    state = dict(pos), group0[0]
                    with pe.If(fullest <= P):
                        moe_sparse()
                    pos.update(state[0])
                    group0[0] = state[1]
                    with pe.If(fullest > P):
                        moe_dense()

            def gate_rows(i, j, s):
                for h in range(2):
                    t, filled, uses, emptied = bank()
                    pe.wait_ge(emptied, uses)
                    for k in range(4):
                        ins = pe.matmul(t[:, k * P:k * P + P],
                                        free(modv[:, i, 8 * j + 4 * h + k, s:s + 1], [[0, P]]), ident,
                                        start=True, stop=True)
                    ins.then_inc(filled, 1)

            def turn_heads(src, width, first, nheads):
                for q in range(QT):
                    for c4 in range(0, nheads // 2, 4):
                        t, filled, uses, emptied = bank()
                        pe.wait_ge(emptied, uses)
                        m = min(4, nheads // 2 - c4)
                        for k in range(m):
                            cc = c4 + k
                            o = q * width + first + cc * P
                            ins = transpose(t[:, k * P:k * P + P], src[:, o:o + P])
                        ins.then_inc(filled, 1)

            def mixer_end(i, s, src):
                pe.wait_ge(mixed_attn, due("mixed_attn"))
                project_out(src)
                gate_rows(i, 2, s)
                pe.wait_ge(normed, due("normed", QT))
                turn_tokens(wv)
                pe.wait_ge(hT_ready, due("hT_ready"))
                ffn(src, FF2 // COLW)
                gate_rows(i, 5, s)

            for i in range(2):
                for s in range(2):
                    pe.wait_ge(normed, due("normed", QT))
                    turn_tokens(wv)
                pe.wait_ge(hT_ready, due("hT_ready", 2))
                ntiles = 6 if i == 0 else 12
                for n in range(ntiles):
                    w = tile(("col", COLW))
                    token_tile(w, COLW, hTv)
                    if i == 0 or n >= 4:
                        token_tile(w, COLW, hTcv)
                    mark_used()
                pe.wait_ge(qk_ready, due("qk_ready"))
                if i == 0:
                    turn_heads(big, 1536, 0, 16)
                    turn_heads(big, 1536, 1024, 4)
                    turn_heads(bigc, 1536, 1024, 4)
                else:
                    turn_heads(big, 3072, 0, 16)
                    turn_heads(big, 3072, 1024, 16)
                    turn_heads(bigc, 2048, 0, 16)
                pe.wait_ge(qT_ready, due("qT_ready"))
                attention(swa_batches(False) if i == 0 else na_batches(), layer1=(i == 1))
                mixer_end(i, 0, hTv)
                if i == 0:
                    turn_heads(bigc, 1536, 0, 16)
                    pe.wait_ge(qT_ready, due("qT_ready"))
                    attention(swa_batches(True))
                    mixer_end(0, 1, hTv)

        @block.scalar
        def _(act):
            due = counter()
            for dst, src in loads[0::2]:
                act.dma_start(dst, src).then_inc(params, 16)
            act.wait_ge(pos_clear, 1)
            for dst, src in pos_loads:
                act.dma_start(dst, src, allow_slow_non_contiguous=True).then_inc(positions, 16)

            def norm_stats(src):
                act.wait_ge(x_ready, due("x_ready"))
                for q in range(QT):
                    act.activation(prob[:, 2048 + q * D:2048 + q * D + D], src[:, q, :], ACT.Square,
                                   accum_out=den[:, q:q + 1]).then_inc(squares, 1)
                root(den[:, 2:2 + QT])

            def root(v):
                act.wait_ge(root_in, due("root_in"))
                act.activation(v, v, ACT.Sqrt).then_inc(root_out, 1)

            mods = [0]

            def mod_rows(count):
                for _ in range(count):
                    n = mods[0]
                    mods[0] += 1
                    act.wait_ge(mod_filled, n + 1)
                    b = passing_bank()
                    act.activation(modrow[0:2, (n % 2) * COLW:(n % 2) * COLW + COLW], pt[b][0:2, 0:COLW], ACT.Copy)\
                       .then_inc(mod_row, 1)
                    act.wait_ge(mod_row, n + 1)
                    act.sem_inc(bank_emptied[b], 1)

            def passing_bank():
                return bank_order.pop(0)

            def exps(batches, mods_beside=0):
                def odd_turned(b):
                    for kc in range(1, -(-b.nk // P), 2):
                        act.wait_ge(odd_filled, due("odd_filled"))
                        bk = passing_bank()
                        w = min(P, b.nk - kc * P)
                        act.activation(probT[0:w, kc * 512:kc * 512 + 512], pt[bk][0:w, :], ACT.Copy)\
                           .then_inc(odd_copied, 1)
                        act.wait_ge(odd_copied, due("odd_copied"))
                        act.sem_inc(bank_emptied[bk], 1)
                    if b.nk > P:
                        act.sem_inc(probT_odd, 1)

                def exp(b, i):
                    act.wait_ge(shifted, due("shifted"))
                    for j in range(4):
                        o = (i % 2) * 2048 + j * 512
                        ins = act.activation(prob[:, o:o + b.nk], prob[:, o:o + b.nk], ACT.Exp,
                                             bias=den[:, 8 + (i % 2) * 4 + j:9 + (i % 2) * 4 + j],
                                             accum_out=den[:, 16 + (i % 2) * 4 + j:17 + (i % 2) * 4 + j])
                    ins.then_inc(exp_done, 1)
                    if b.sink:
                        v = den[:, 24 + (i % 2) * 4:28 + (i % 2) * 4]
                        act.activation(v, v, ACT.Exp).then_inc(exp_done, 1)

                exp(batches[0], 0)
                exp(batches[1], 1)
                for i, b in enumerate(batches):
                    odd_turned(b)
                    if i < mods_beside:
                        mod_rows(1)
                    if i + 2 < len(batches):
                        exp(batches[i + 2], i + 2)

            group0 = [0]

            def ffn(groups):
                g0 = group0[0]

                def one(g, before=True):
                    for cc in range(2):
                        act.wait_ge(gate_up_done[cc], g + 1)
                        if before:
                            act.wait_ge(act_ready[cc], g)
                        act.activation(silu[:, cc * S:cc * S + S], pt[cc][:, 0:S], ACT.Silu)\
                           .then_inc(silu_ready[cc], 1)

                one(g0, before=g0 > 0)
                with act.Fori(1, groups) as it:
                    one(it + g0)
                group0[0] += groups

            act.wait_ge(cond_raw, due("cond_raw"))
            act.activation(condv, condv, ACT.Silu).then_inc(cond_ready, 1)
            act.wait_ge(angles, due("angles"))
            act.activation(ang[:, 24:72], ang[:, 24:72], ACT.Sin).then_inc(sines, 1)

            for l in range(2):
                norm_stats(xv)
                act.wait_ge(gate_logits, due("gate_logits"))
                act.activation(glog, glog, ACT.Sigmoid).then_inc(gates_sigmoid, 1)
                act.wait_ge(u_ready, due("u_ready"))
                act.activation(ug[:, 4:8, :], ug[:, 4:8, :], ACT.Sigmoid).then_inc(conv_gate, 1)
                act.wait_ge(hidden_raw, due("hidden_raw"))
                act.activation(hid[:, 60:120], hid[:, 0:60], ACT.Gelu_apprx_tanh).then_inc(hidden_ready, 1)
                root(small[:, 64:88])
                root(small[0:NCMP, 96:98])
                mod_rows(MODS_EARLY)
                root(y2[:, 0, :])
                act.wait_ge(conv_normed, due("conv_normed"))
                for cc in range(CC):
                    ins = act.activation(hTv[:, CC + cc, :], y[:, cc, :], ACT.Silu,
                                         scale=colA[:, COL["conv_ln_g"] + CC * l + cc:COL["conv_ln_g"] + CC * l + cc + 1],
                                         bias=colA[:, COL["conv_ln_b"] + CC * l + cc:COL["conv_ln_b"] + CC * l + cc + 1])
                ins.then_inc(mixed_conv, 1)
                exps(first_batches(), 24 - MODS_EARLY)
                norm_stats(xv)
                if l == 0:
                    ffn(FF1 // COLW)
                else:
                    act.wait_ge(top_shifted, due("top_shifted"))
                    act.activation(logit[:, 64:66], logit[:, 64:66], ACT.Exp).then_inc(top_exp, 1)
                    ffn(NE * FF1 // COLW)
            for i in range(2):
                norm_stats(xv)
                norm_stats(xcv)
                root(small[:, 0:(80, 96)[i]])
                exps(swa_batches(False) if i == 0 else na_batches())
                norm_stats(xv)
                ffn(FF2 // COLW)
                if i == 0:
                    exps(swa_batches(True))
                    norm_stats(xcv)
                    ffn(FF2 // COLW)

        @block.vector
        def _(ve):
            due = counter()
            pos = {"t": 0}
            bank_log = []
            chain = [0]

            def link(ins):
                chain[0] += 1
                ins.then_inc(vector_chain, 1)
                ve.wait_ge(vector_chain, chain[0])

            def go(ins):
                chain[0] += 1
                ins.then_inc(vector_chain, 1)

            def settle():
                ve.wait_ge(vector_chain, chain[0])

            def tell(name, k=1):
                settle()
                ve.sem_inc(name, k)

            def bank():
                n = pos["t"]
                pos["t"] += 1
                fills[n % 2] += 1
                return pt[n % 2], bank_filled[n % 2], fills[n % 2], bank_emptied[n % 2]

            def leave_bank(count=1):
                for _ in range(count):
                    bank_log.append(pos["t"] % 2)
                    pos["t"] += 1

            fills = [0, 0]

            def root():
                tell(root_in)
                ve.wait_ge(root_out, due("root_out"))

            def norm(src, gain, shift, dst, ms_only=False):
                ve.wait_ge(squares, due("squares", QT))
                link(ve.tensor_scalar(den[:, 0:QT], den[:, 0:QT], 1.0 / D, EPS, ALU.mult, ALU.add))
                link(ve.reciprocal(den[:, 2:2 + QT], den[:, 0:QT]))
                root()
                for q in range(QT):
                    ve.tensor_scalar(wv[:, q, :], src[:, q, :], den[:, 2 + q:3 + q], None, ALU.mult)\
                      .then_inc(normed, 1)
                for j in range(KC // 2):
                    t, filled, uses, emptied = bank()
                    ve.wait_ge(filled, uses)
                    for k in range(2):
                        kc = 2 * j + k
                        if shift is None:
                            go(ve.tensor_scalar(dst[:, kc, :], t[:, k * S:k * S + S], gain[:, kc:kc + 1], None, ALU.mult))
                        else:
                            go(ve.tensor_scalar(dst[:, kc, :], t[:, k * S:k * S + S], gain[:, kc:kc + 1],
                                                shift(kc), ALU.mult, ALU.add))
                    tell(emptied)
                tell(hT_ready)

            def head_norm(z, n, gains, at, sq):
                link(ve.tensor_tensor(sq, z, z, ALU.mult))
                r = small[0:z.shape[0], at:at + n]
                link(ve.tensor_reduce(r, sq, AX.X, ALU.add))
                link(ve.tensor_scalar(r, r, 1.0 / HD, EPS, ALU.mult, ALU.add))
                link(ve.reciprocal(r, r))

            def head_scale(z, n, at):
                r = small[0:z.shape[0], at:at + n]
                link(ve.tensor_tensor(z, z, free(r, [[1, n], [0, HD]]), ALU.mult))

            def rotate(x1, x2, cos, sin, shape):
                np_ = x1.shape[0]
                dims, k = [], 1
                for n in reversed(shape):
                    dims.insert(0, [k, n])
                    k *= n
                t = [free(ropet[0:np_, 256 * j:256 * j + 1], dims) for j in range(4)]
                go(ve.tensor_tensor(t[0], x1, cos, ALU.mult))
                go(ve.tensor_tensor(t[1], x2, sin, ALU.mult))
                go(ve.tensor_tensor(t[2], x2, cos, ALU.mult))
                go(ve.tensor_tensor(t[3], x1, sin, ALU.mult))
                settle()
                go(ve.tensor_tensor(x1, t[0], t[1], ALU.subtract))
                go(ve.tensor_tensor(x2, t[2], t[3], ALU.add))
                settle()

            def attention(batches, mods=0):
                def softmax(b, i):
                    ve.wait_ge(scores_done, due("scores_done"))
                    o = (i % 2) * 2048
                    raw = pacc[:, :].rearrange("p (j k) -> p j k", j=4)
                    st = prob[:, o:o + 2048].rearrange("p (j k) -> p j k", j=4)
                    lat = min(b.nk, S)
                    if b.bias:
                        ve.wait_ge(bias_loaded[i % 2], 128 * (i // 2 + 1))
                        bb = biasb[:, (i % 2) * 1024:(i % 2) * 1024 + 1024].rearrange("p (j k) -> p j k", j=4)
                        m = cst("na")
                        link(ve.tensor_tensor(bb, bb, free(m, [[0, 4], [1, S]]), ALU.add))
                    elif b.mask:
                        w = {"cmp": NCMP, "causal": S, "swa": S}[b.mask]
                        m = cst(b.mask)[:, b.qt * w:b.qt * w + lat]
                        bb = free(m, [[0, 4], [1, lat]])
                    if b.mask or b.bias:
                        go(ve.scalar_tensor_tensor(out=st[:, :, 0:lat], in0=raw[:, :, 0:lat], scalar=HD ** -0.5, in1=bb,
                                                   op0=ALU.mult, op1=ALU.add))
                        if b.nk > S:
                            go(ve.tensor_scalar(st[:, :, S:b.nk], raw[:, :, S:b.nk], HD ** -0.5, None, ALU.mult))
                    else:
                        go(ve.tensor_scalar(st[:, :, 0:b.nk], raw[:, :, 0:b.nk], HD ** -0.5, None, ALU.mult))
                    settle()
                    ve.sem_inc(scores_taken, 1)
                    if b.bias:
                        ve.sem_inc(bias_used, 1)
                    top = den[:, 8 + (i % 2) * 4:12 + (i % 2) * 4]
                    sk = den[:, 24 + (i % 2) * 4:28 + (i % 2) * 4]
                    link(ve.tensor_reduce(top, st[:, :, 0:b.nk], AX.X, ALU.max))
                    if b.sink:
                        s4 = sink[:, b.heads[0]:b.heads[0] + 4]
                        link(ve.tensor_tensor(top, top, s4, ALU.max))
                        link(ve.tensor_tensor(sk, s4, top, ALU.subtract))
                    if b.mask == "cmp":
                        link(ve.scalar_tensor_tensor(out=top, in0=top, scalar=-1e29, in1=top, op0=ALU.is_gt, op1=ALU.mult))
                    link(ve.tensor_scalar(top, top, -1.0, None, ALU.mult))
                    ve.sem_inc(shifted, 1)

                def normalise(b, i):
                    den_ = den[:, 16 + (i % 2) * 4:20 + (i % 2) * 4]
                    if b.sink:
                        ve.wait_ge(exp_done, due("exp_done", 2))
                        link(ve.tensor_tensor(den_, den_, den[:, 24 + (i % 2) * 4:28 + (i % 2) * 4], ALU.add))
                    else:
                        ve.wait_ge(exp_done, due("exp_done"))
                    link(ve.tensor_scalar(den_, den_, TINY, None, ALU.max))
                    link(ve.reciprocal(den_, den_))
                    if b.gate is not None:
                        h0 = b.heads[0]
                        g = free(glog[:, b.qt, 3 * h0 + b.gate:3 * h0 + b.gate + 1], [[3, 4]])
                        link(ve.tensor_tensor(den_, den_, g, ALU.mult))
                    for j in range(4):
                        o = (i % 2) * 2048 + j * 512
                        go(ve.tensor_scalar(prob[:, o:o + b.nk], prob[:, o:o + b.nk], den_[:, j:j + 1], None, ALU.mult))
                    tell(prob_ready)

                def output(b, i):
                    nkc = -(-b.nk // P)
                    for kc in range(0, nkc, 2):
                        w = min(P, b.nk - kc * P)
                        t, filled, uses, emptied = bank()
                        ve.wait_ge(filled, uses)
                        go(ve.tensor_copy(probT[0:w, kc * 512:kc * 512 + 512], t[0:w, :]))
                        tell(emptied)
                        if kc + 1 < nkc:
                            leave_bank()
                    ve.sem_inc(probT_ready, 1)

                def result(b):
                    ve.wait_ge(output_done, due("output_done"))
                    src = po[0:HD, :].rearrange("p (j t) -> p j t", j=4)
                    c0 = b.heads[0] // 2
                    for half in range(2):
                        go(ve.tensor_copy(hTv[half * HD:half * HD + HD, c0:c0 + 2, b.qt * P:b.qt * P + P],
                                          src[:, half:4:2, :]))
                    tell(output_taken)

                softmax(batches[0], 0)
                softmax(batches[1], 1)
                normalise(batches[0], 0)
                waiting = []
                for i, b in enumerate(batches):
                    if waiting:
                        result(waiting.pop())
                    output(b, i)
                    if i < mods:
                        leave_bank()
                    if b.gate in (None, 2):
                        waiting.append(b)
                    if i + 1 < len(batches):
                        normalise(batches[i + 1], i + 1)
                    if i + 2 < len(batches):
                        softmax(batches[i + 2], i + 2)
                result(waiting.pop())
                ve.sem_inc(mixed_attn, 1)

            group0 = [0]
            ffn_tiles = list(ffn_at)

            def ffn(experts, groups, sparse=False):
                g0, n0 = group0[0], ffn_tiles.pop(0)

                def one(g, e, tokens=S):
                    for cc in range(2):
                        ve.wait_ge(silu_ready[cc], g + 1)
                        sl = silu[:, cc * S:cc * S + tokens]
                        ve.wait_ge(tile_used, g * 3 + (n0 - 3 * g0))
                        if e is not None:
                            ve.tensor_tensor(sl, sl, kT[:, bass.ds(e * S, S)], ALU.mult).then_inc(weighed[cc], 1)
                            ve.wait_ge(weighed[cc], g + (1 - g0))
                        ve.tensor_tensor(actb[:, cc * S:cc * S + tokens], sl, pt[cc][:, S:S + tokens], ALU.mult)\
                          .then_inc(act_ready[cc], 1)

                if sparse:
                    def current(e, src, off):
                        ve.wait_ge(gate_up_done[1], e * groups + g0)
                        ve.tensor_copy(hcur, src[:, bass.ds(off, D)]).then_inc(h_current, 1)

                    def taken(e):
                        ve.wait_ge(tile_used, e * (3 * groups) + n0)
                        ve.tensor_copy(backcur, back[:, bass.ds(e * S, S)]).then_inc(back_current, 1)
                        ve.wait_ge(back_current, e + 1)
                        ve.tensor_copy(work[:, 0:D], pacc[:, 0:D]).then_inc(y_taken, 1)

                    for e0, e1, src in ((0, 6, gathered[0]), (6, 8, gathered[1])):
                        with ve.Fori(e0, e1) as e:
                            current(e, src, e * D - e0 * D)
                            taken(e)
                            with ve.Fori(0, groups) as it:
                                one(e * groups + it + g0, None, P)
                    ve.wait_ge(tile_used, experts * 3 * groups + n0)
                    ve.tensor_copy(backcur, back[:, experts * S:(experts + 1) * S]).then_inc(back_current, 1)
                    ve.wait_ge(back_current, experts + 1)
                    ve.tensor_copy(work[:, 0:D], pacc[:, 0:D]).then_inc(y_taken, 1)
                    group0[0] += groups * experts
                    return
                if experts:
                    with ve.Fori(0, experts) as e:
                        with ve.Fori(0, groups) as it:
                            one(e * groups + it + g0, e)
                    groups *= experts
                else:
                    with ve.Fori(0, groups) as it:
                        one(it + g0, None)
                group0[0] += groups

            def moe_sparse():
                go(ve.memset(gateb[:, 0:512], 0.0))
                go(ve.memset(back[:, 0:S], 0.0))
                g = colA[:, COL["ffn_norm_g"] + KC:COL["ffn_norm_g"] + 2 * KC]
                for e in range(NE):
                    for q in range(QT):
                        r = route[:, 16 + q * NE + e:17 + q * NE + e]
                        go(ve.tensor_scalar(pick[:, e, q, :], cst("iota"), r, None, ALU.is_equal))
                        go(ve.tensor_scalar(weigh[:, e, q, :], cst("iota"), r,
                                            logit[:, 80 + q * NE + e:81 + q * NE + e], ALU.is_equal, ALU.mult))
                    tell(picked)
                    if e:
                        take_gathered(e - 1, g)
                take_gathered(NE - 1, g)
                ffn(NE, FF1 // COLW, sparse=True)
                ve.wait_ge(sum_done, due("sum_done"))
                for i in range(4):
                    go(ve.tensor_tensor(x[:, 512 * i:512 * i + 512], x[:, 512 * i:512 * i + 512], spread[i], ALU.add))
                settle()

            def take_gathered(e, g):
                buf, o = (gathered[0], e * D) if e < 6 else (gathered[1], (e - 6) * D)
                for k4 in range(2):
                    t, filled, uses, emptied = bank()
                    ve.wait_ge(filled, uses)
                    go(ve.tensor_tensor(buf[:, o + 512 * k4:o + 512 * k4 + 512].rearrange("p (k t) -> p k t", k=4),
                                        t[:, :].rearrange("p (k t) -> p k t", k=4),
                                        free(g[:, 4 * k4:4 * k4 + 1], [[1, 4], [0, P]]), ALU.mult))
                    tell(emptied)
                if e % 2:
                    t, filled, uses, emptied = bank()
                    ve.wait_ge(filled, uses)
                    go(ve.tensor_copy(back[:, e * S:(e + 2) * S], t[:, :]))
                    tell(emptied)

            def moe_dense(after):
                for e in range(0, NE, 2):
                    t, filled, uses, emptied = bank()
                    ve.wait_ge(filled, uses)
                    go(ve.tensor_copy(kT[:, e * S:(e + 2) * S], t[:, :]))
                    tell(emptied)
                for b in range(2):
                    ve.sem_inc(bank_emptied[b], 8)
                pos["t"] += 16
                for b in range(2):
                    fills[b] += 8
                ffn(NE, FF1 // COLW)
                ve.wait_ge(sum_done, due("sum_done", 0))
                link(ve.tensor_tensor(x[:, :], x[:, :], pacc[:, :], ALU.add))
                ve.sem_inc(vector_chain, after - chain[0])
                chain[0] = after
                settle()

            def add_sum(dst):
                ve.wait_ge(sum_done, due("sum_done"))
                link(ve.tensor_tensor(dst[:, :], dst[:, :], pacc[:, :], ALU.add))

            def add_gated(dst):
                for h in range(2):
                    t, filled, uses, emptied = bank()
                    ve.wait_ge(filled, uses)
                    go(ve.tensor_copy(gateb[:, 512 * h:512 * h + 512], t[:, :]))
                    tell(emptied)
                ve.wait_ge(sum_done, due("sum_done"))
                for q in range(QT):
                    go(ve.tensor_tensor(wv[:, q, :], pacc[:, q * D:q * D + D], gateb[:, :], ALU.mult))
                settle()
                link(ve.tensor_tensor(dst[:, :], dst[:, :], work[:, :], ALU.add))

            for b in range(2):
                ve.sem_inc(bank_emptied[b], 1)
            link(ve.memset(posi[:, :], 0))
            ve.sem_inc(pos_clear, 1)
            t, filled, uses, emptied = bank()
            ve.wait_ge(filled, uses)
            go(ve.tensor_copy(colA[:, :], t[:, 0:104]))
            go(ve.tensor_copy(free(condv[:, 0, 0:1], [[1, 2], [2, KC]]),
                              t[:, COL["cond"]:COL["cond"] + 16].rearrange("p (s k) -> p s k", s=2)))
            tell(emptied)
            tell(cond_raw)
            t, filled, uses, emptied = bank()
            ve.wait_ge(filled, uses)
            go(ve.tensor_copy(colB[:, :], t[:, 0:96]))
            tell(emptied)
            t, filled, uses, emptied = bank()
            ve.wait_ge(filled, uses)
            go(ve.tensor_copy(colC[:, :], t[:, 0:64]))
            tell(emptied)
            t, filled, uses, emptied = bank()
            ve.wait_ge(filled, uses)
            go(ve.tensor_copy(convv, t[:, :].rearrange("p (c n) -> p c n", c=CC)[:, :, 0:2 * TAPS]))
            tell(emptied)
            ve.wait_ge(positions, 16 * len(pos_loads))
            ve.wait_ge(params, 16 * len(loads[0::2]))
            ve.wait_ge(params_pool, 16 * len(loads[1::2]))
            ve.sem_inc(x_ready, 1)
            link(ve.tensor_copy(posf[:, :], posi[:, :]))
            an, kk = ang[:, 0:24], ang[:, 72:96]
            for s in range(3):
                go(ve.tensor_scalar(an[:, 8 * s:8 * s + 8], cst("freq"), posf[:, s:s + 1], None, ALU.mult))
            settle()
            link(ve.tensor_scalar(kk, an, 1.0 / (2 * math.pi), MAGIC, ALU.mult, ALU.add))
            link(ve.tensor_scalar(kk, kk, -MAGIC, None, ALU.add))
            for part in TWO_PI:
                link(ve.scalar_tensor_tensor(out=an, in0=kk, scalar=-part, in1=an, op0=ALU.mult, op1=ALU.add))
            link(ve.tensor_scalar(an, an, 3.1415925, -3.1415925, ALU.min, ALU.max))
            go(ve.tensor_copy(ang[:, 24:48], an))
            go(ve.tensor_scalar(ang[:, 48:72], an, 0.5, None, ALU.mult))
            tell(angles)
            ve.wait_ge(sines, due("sines"))
            go(ve.tensor_copy(sin1[:, :], ang[:, 24:48]))
            link(ve.tensor_tensor(kk, ang[:, 48:72], ang[:, 48:72], ALU.mult))
            link(ve.tensor_scalar(cos1[:, :], kk, -2.0, 1.0, ALU.mult, ALU.add))
            link(ve.memset(padded[:, :, 0:TAPS - 1], 0.0))

            def gains(name, l):
                o = COL[name] + KC * l
                return colA[:, o:o + KC]

            for l in range(2):
                norm(xv, gains("attn_norm_g", l), None, hTv)
                for j in range(2):
                    t, filled, uses, emptied = bank()
                    ve.wait_ge(filled, uses)
                    go(ve.tensor_copy(qkz[:, :, j:j + 7:2, :], t[:, :].rearrange("p (t h d) -> p t h d", t=QT, h=4)))
                    tell(emptied)
                for which in range(2):
                    t, filled, uses, emptied = bank()
                    ve.wait_ge(filled, uses)
                    for v in range(2):
                        head = t[v * HD:v * HD + HD, 0:S]
                        go(ve.tensor_copy(kvp[0:64, which, v, :], head))
                        go(ve.tensor_copy(kvp[64:128, which, v, 0:S - 1], head[:, 1:S]))
                    tell(emptied)
                    for v in range(2):
                        src = free(kvp[:, which, v, 0:1], [[2, 16], [16, NCMP]])
                        pe_ = free(colC[:, 32 * which + 16 * l:32 * which + 16 * l + 1], [[1, 16], [0, NCMP]])
                        go(ve.tensor_tensor(blk[:, which, :, v, :], src, pe_, ALU.add))
                tell(blocks_ready)
                for br in range(2):
                    t, filled, uses, emptied = bank()
                    ve.wait_ge(filled, uses)
                    go(ve.tensor_copy(qkz[:, :, 8 + 2 * br:10 + 2 * br, :],
                                      t[:, :].rearrange("p (t h d) -> p t h d", t=QT, h=4)[:, :, 0:2, :]))
                    go(ve.tensor_copy(val1[:, :, 128 * br:128 * br + 128],
                                      t[:, :].rearrange("p (t n) -> p t n", t=QT)[:, :, 128:256]))
                    tell(emptied)
                t, filled, uses, emptied = bank()
                ve.wait_ge(filled, uses)
                go(ve.tensor_copy(glog, t[:, :].rearrange("p (t n) -> p t n", t=QT)[:, :, 0:24]))
                tell(emptied)
                tell(gate_logits)
                for j in range(4):
                    t, filled, uses, emptied = bank()
                    ve.wait_ge(filled, uses)
                    go(ve.tensor_copy(ug[:, 2 * j:2 * j + 2, :], t[:, :].rearrange("p (k t) -> p k t", k=2)))
                    tell(emptied)
                tell(u_ready)
                for which in range(2):
                    t, filled, uses, emptied = bank()
                    ve.wait_ge(filled, uses)
                    go(ve.tensor_copy(hid[:, 30 * which:30 * which + 30], t[:, 0:30]))
                    tell(emptied)
                tell(hidden_raw)
                z = big[:, 0:QT * 12 * HD].rearrange("p (h d) -> p h d", d=HD)
                sq = work[:, 0:QT * 12 * HD].rearrange("p (h d) -> p h d", d=HD)
                head_norm(z, 24, None, 64, sq)
                root()
                head_scale(z, 24, 64)
                for q in range(QT):
                    for h0, nh, g in ((0, 8, 0), (8, 2, 1), (10, 2, 2)):
                        v = qkz[:, q, h0:h0 + nh, :]
                        go(ve.tensor_tensor(v, v, free(gain1[:, 256 * l + 64 * g:256 * l + 64 * g + 1], [[0, nh], [1, HD]]), ALU.mult))
                settle()
                for q in range(QT):
                    rotate(qkz[:, q, :, 0:8], qkz[:, q, :, 8:16], free(cos1[:, 8 * q:8 * q + 1], [[0, 12], [1, 8]]),
                           free(sin1[:, 8 * q:8 * q + 1], [[0, 12], [1, 8]]), (12, 8))
                ve.sem_inc(qk_ready, 1)
                t, filled, uses, emptied = bank()
                ve.wait_ge(filled, uses)
                go(ve.tensor_copy(kcm[0:NCMP, :], t[0:NCMP, 0:256]))
                tell(emptied)
                for q in range(QT):
                    t, filled, uses, emptied = bank()
                    ve.wait_ge(filled, uses)
                    go(ve.tensor_copy(qTv[:, 0:4, q * P:q * P + P], t[:, :].rearrange("p (c t) -> p c t", c=4)))
                    tell(emptied)
                t, filled, uses, emptied = bank()
                ve.wait_ge(filled, uses)
                go(ve.tensor_copy(kT[:, 0:512], t[:, :]))
                tell(emptied)
                z = kcm[0:NCMP, 0:128].rearrange("p (h d) -> p h d", d=HD)
                head_norm(z, 2, None, 96, work[0:NCMP, 0:128].rearrange("p (h d) -> p h d", d=HD))
                root()
                head_scale(z, 2, 96)
                link(ve.tensor_tensor(z, z, free(gain1[0:NCMP, 256 * l + 192:256 * l + 193], [[0, 2], [1, HD]]), ALU.mult))
                rotate(z[:, :, 0:8], z[:, :, 8:16], free(cos1[0:NCMP, 16:17], [[0, 2], [1, 8]]),
                       free(sin1[0:NCMP, 16:17], [[0, 2], [1, 8]]), (2, 8))
                ve.sem_inc(kcm_ready, 1)
                t, filled, uses, emptied = bank()
                ve.wait_ge(filled, uses)
                go(ve.tensor_copy(kcT[:, 0:NCMP], t[:, 0:NCMP]))
                tell(emptied)
                leave_bank(MODS_EARLY)
                ve.wait_ge(conv_gate, due("conv_gate"))
                link(ve.tensor_tensor(padded[:, :, TAPS - 1:], ug[:, 0:4, :], ug[:, 4:8, :], ALU.mult))
                for k in range(TAPS):
                    for cc in range(CC):
                        wk = convv[:, cc, l * TAPS + k:l * TAPS + k + 1]
                        src = padded[:, cc, k:k + S]
                        if k == 0:
                            o = COL["conv_b"] + CC * l + cc
                            go(ve.tensor_scalar(y[:, cc, :], src, wk, colA[:, o:o + 1], ALU.mult, ALU.add))
                        else:
                            go(ve.scalar_tensor_tensor(out=y[:, cc, :], in0=src, scalar=wk, in1=y[:, cc, :],
                                                       op0=ALU.mult, op1=ALU.add))
                    settle()
                ve.sem_inc(conv_ready, 1)
                t, filled, uses, emptied = bank()
                ve.wait_ge(filled, uses)
                link(ve.scalar_tensor_tensor(out=y, in0=free(t[:, 0:1], [[0, CC], [1, S]]), scalar=-1.0 / CW, in1=y,
                                             op0=ALU.mult, op1=ALU.add))
                ve.sem_inc(emptied, 1)
                link(ve.tensor_tensor(y2, y, y, ALU.mult))
                ve.sem_inc(conv_ready, 1)
                t, filled, uses, emptied = bank()
                ve.wait_ge(filled, uses)
                link(ve.tensor_scalar(y2[:, 0, :], t[:, 0:S], 1.0 / CW, EPS, ALU.mult, ALU.add))
                ve.sem_inc(emptied, 1)
                link(ve.reciprocal(y2[:, 0, :], y2[:, 0, :]))
                root()
                link(ve.tensor_tensor(y, y, free(y2[:, 0, 0:1], [[0, CC], [1, S]]), ALU.mult))
                ve.sem_inc(conv_normed, 1)
                ve.wait_ge(gates_sigmoid, due("gates_sigmoid"))
                ve.sem_inc(qT_ready, 1)
                attention(first_batches(), 24 - MODS_EARLY)
                if l == 1:
                    ve.wait_ge(ada_done, 1)
                    src = pada[:, 0:192].rearrange("p (l c s) -> p l c s", l=2, c=48)
                    for i in range(2):
                        go(ve.tensor_tensor(modv[:, i, :, :], src[:, i, :, :],
                                            free(colB[:, 48 * i:48 * i + 1], [[1, 48], [0, 2]]), ALU.add))
                    settle()
                add_sum(x)
                ve.sem_inc(x_ready, 1)
                norm(xv, gains("ffn_norm_g", l), None, hTv)
                if l == 0:
                    ffn(0, FF1 // COLW)
                else:
                    lg = logit[:, 0:16].rearrange("p (t e) -> p t e", t=QT)
                    t, filled, uses, emptied = bank()
                    ve.wait_ge(filled, uses)
                    go(ve.tensor_copy(logit[:, 0:16], t[:, 0:16]))
                    tell(emptied)
                    for q in range(QT):
                        link(ve.max(logit[:, 16 + 8 * q:24 + 8 * q], logit[:, 8 * q:8 * q + 8]))
                        link(ve.max_index(top_i[:, 8 * q:8 * q + 8], logit[:, 16 + 8 * q:24 + 8 * q], logit[:, 8 * q:8 * q + 8]))
                    link(ve.tensor_copy(logit[:, 32:48], top_i[:, :]))
                    for q in range(QT):
                        link(ve.tensor_tensor(logit[:, 64 + q:65 + q], logit[:, 17 + 8 * q:18 + 8 * q],
                                              logit[:, 16 + 8 * q:17 + 8 * q], ALU.subtract))
                    ve.sem_inc(top_shifted, 1)
                    ve.wait_ge(top_exp, due("top_exp"))
                    link(ve.tensor_scalar(logit[:, 66:68], logit[:, 64:66], 1.0, None, ALU.add))
                    link(ve.reciprocal(logit[:, 66:68], logit[:, 66:68]))
                    link(ve.tensor_tensor(logit[:, 68:70], logit[:, 64:66], logit[:, 66:68], ALU.mult))
                    for q in range(QT):
                        link(ve.tensor_scalar(logit[:, 48:56], cst("iota")[:, 0:NE], logit[:, 32 + 8 * q:33 + 8 * q],
                                              logit[:, 66 + q:67 + q], ALU.is_equal, ALU.mult))
                        link(ve.tensor_scalar(logit[:, 56:64], cst("iota")[:, 0:NE], logit[:, 33 + 8 * q:34 + 8 * q],
                                              logit[:, 68 + q:69 + q], ALU.is_equal, ALU.mult))
                        link(ve.tensor_tensor(logit[:, 80 + 8 * q:88 + 8 * q], logit[:, 48:56], logit[:, 56:64], ALU.add))
                        link(ve.tensor_scalar(logit[:, 48:56], cst("iota")[:, 0:NE], logit[:, 32 + 8 * q:33 + 8 * q],
                                              None, ALU.is_equal))
                        link(ve.tensor_scalar(logit[:, 56:64], cst("iota")[:, 0:NE], logit[:, 33 + 8 * q:34 + 8 * q],
                                              None, ALU.is_equal))
                        link(ve.tensor_tensor(route[:, 8 * q:8 * q + 8], logit[:, 48:56], logit[:, 56:64], ALU.add))
                    ve.sem_inc(gates_ready, 1)
                    t, filled, uses, emptied = bank()
                    ve.wait_ge(filled, uses)
                    link(ve.scalar_tensor_tensor(out=route[:, 16:32], in0=t[:, 0:16], scalar=1.0, in1=route[:, 0:16],
                                                 op0=ALU.add, op1=ALU.mult))
                    link(ve.tensor_scalar(route[:, 16:32], route[:, 16:32], -1.0, None, ALU.add))
                    link(ve.tensor_reduce(route[:, 40:41], t[:, 16:24], AX.X, ALU.max))
                    ve.sem_inc(emptied, 1)
                    link(ve.tensor_copy(most[:, :], route[:, 40:41]))
                    ve.sem_inc(routed, 1)
                    fullest = ve.value_load(most[0:1, 0:1], min_val=0, max_val=S)
                    state = dict(pos), group0[0], list(ffn_tiles), chain[0], list(fills)
                    with ve.If(fullest <= P):
                        moe_sparse()
                    after = chain[0]
                    pos.update(state[0])
                    group0[0] = state[1]
                    ffn_tiles[:] = state[2]
                    chain[0] = state[3]
                    fills[:] = state[4]
                    with ve.If(fullest > P):
                        moe_dense(after)
                    ve.sem_inc(x_ready, 1)
                    continue
                add_sum(x)
                ve.sem_inc(x_ready, 1)

            def modulated(src, i, which, s, name, dst):
                sc = modv[:, i, 8 * (3 * which + 1):8 * (3 * which + 2), s]
                link(ve.scalar_tensor_tensor(out=gsc[:, :], in0=sc, scalar=1.0, in1=gains(name, i),
                                             op0=ALU.add, op1=ALU.mult))
                norm(src, gsc, lambda kc: modv[:, i, 8 * 3 * which + kc, s:s + 1], dst)

            def project_evac(i):
                for n in range(6 if i == 0 else 12):
                    w = (1536, 3072)[i]
                    def place(buf, w, m, stats):
                        t, filled, uses, emptied = bank()
                        ve.wait_ge(filled, uses)
                        v = buf[:, 0:QT * w].rearrange("p (t h d) -> p t h d", t=QT, d=HD)
                        src = t[:, :].rearrange("p (t h d) -> p t h d", t=QT, d=HD)
                        if i == 0 and m < 4:
                            o, step = 8 * (m // 2) + m % 2, 2
                        else:
                            o, step = 4 * m, 1
                        heads = v[:, :, o:o + 3 * step + 1:step, :]
                        go(ve.tensor_copy(heads, src))
                        tell(emptied)
                        if stats:
                            base, each, gain = stats
                            sq = work[:, 0:512].rearrange("p (t h d) -> p t h d", t=QT, d=HD)
                            go(ve.tensor_tensor(sq, heads, heads, ALU.mult))
                            settle()
                            go(ve.tensor_reduce(free(norms[:, base + o:base + o + 1], [[each, QT], [step, 4]]), sq,
                                                AX.X, ALU.add))
                            for q in range(QT):
                                hq = v[:, q, o:o + 3 * step + 1:step, :]
                                go(ve.tensor_tensor(hq, hq, free(gain2[:, 64 * gain:64 * gain + 1], [[0, 4], [1, HD]]),
                                                    ALU.mult))
                            settle()

                    if i == 0:
                        stats = (20, 0) if n < 4 else (20, 1) if n == 4 else None
                        place(big, w, n, stats and (0,) + stats)
                        place(bigc, 1536, n, stats and (40,) + stats)
                    else:
                        place(big, w, n, (0, 32, 2 + n // 4) if n < 8 else None)
                        if n >= 4:
                            place(bigc, 2048, n - 4, (64, 16, 3) if n < 8 else None)

            def heads_of(src, width, first, n, q):
                return src[:, q * width + first:q * width + first + n * HD].rearrange("p (h d) -> p h d", d=HD)

            def heads_norm_all(parts):
                r = norms[:, 0:sum(n for _, n in parts)]
                link(ve.tensor_scalar(r, r, 1.0 / HD, EPS, ALU.mult, ALU.add))
                link(ve.reciprocal(r, r))
                root()
                at = 0
                for z, n in parts:
                    go(ve.tensor_tensor(z, z, free(norms[:, at:at + 1], [[1, n], [0, HD]]), ALU.mult))
                    at += n
                settle()

            norms = small[:, 0:160]

            def heads_evac(nheads, dst, off=0):
                for q in range(QT):
                    for c4 in range(0, nheads // 2, 4):
                        m = min(4, nheads // 2 - c4)
                        t, filled, uses, emptied = bank()
                        ve.wait_ge(filled, uses)
                        go(ve.tensor_copy(dst[:, c4:c4 + m, off + q * P:off + q * P + P],
                                          t[:, 0:m * P].rearrange("p (c t) -> p c t", c=m)))
                        tell(emptied)

            kTv = kT[:, :].rearrange("p (c t) -> p c t", c=8)

            def mixer_end(i, s, res, resv, dst, last=False):
                add_gated(res)
                ve.sem_inc(x_ready, 1)
                modulated(resv, i, 1, s, "g_ffn_2", dst)
                ffn(0, FF2 // COLW)
                add_gated(res)

            for i in range(2):
                if i == 1:
                    ve.sem_inc(x_ready, 1)
                modulated(xv, i, 0, 0, "g_mix_2", hTv)
                ve.sem_inc(x_ready, 1)
                modulated(xcv, i, 0, 1, "g_mix_2", hTcv)
                project_evac(i)
                if i == 0:
                    heads_norm_all([(heads_of(s_, 1536, 0, 20, q), 20) for s_ in (big, bigc) for q in range(QT)])
                    for q in range(QT):
                        for f, n in ((0, 16), (1024, 4)):
                            v = big[:, q * 1536 + f:q * 1536 + f + n * HD].rearrange("p (h d) -> p h d", d=HD)
                            for axis in range(2):
                                o = 32 * axis
                                rotate(v[:, :, o:o + 16], v[:, :, o + 16:o + 32],
                                       free(cst("cos2")[:, 32 * q + 16 * axis:32 * q + 16 * axis + 1], [[0, n], [1, 16]]),
                                       free(cst("sin2")[:, 32 * q + 16 * axis:32 * q + 16 * axis + 1], [[0, n], [1, 16]]), (n, 16))
                    ve.sem_inc(qk_ready, 1)
                    heads_evac(16, qTv)
                    heads_evac(4, kTv)
                    heads_evac(4, kTv, S)
                    tell(qT_ready)
                    attention(swa_batches(False))
                    mixer_end(0, 0, x, xv, hTv)
                    heads_evac(16, qTv)
                    tell(qT_ready)
                    attention(swa_batches(True))
                    mixer_end(0, 1, xc, xcv, hTv)
                else:
                    heads_norm_all([(heads_of(big, 3072, 0, 32, q), 32) for q in range(QT)]
                                   + [(heads_of(bigc, 2048, 0, 16, q), 16) for q in range(QT)])
                    ve.sem_inc(qk_ready, 1)
                    heads_evac(16, qTv)
                    heads_evac(16, kTv)
                    heads_evac(16, kTv, S)
                    tell(qT_ready)
                    attention(na_batches())
                    mixer_end(1, 0, x, xv, hTv)
            ve.sem_inc(x_final, 1)
            assert bank_log == scalar_banks()


UNUSED = ("pool_", "mla_")


def kernel(**inputs):
    import concourse.bacc as bacc
    from concourse.bass_utils import run_bass_kernel_spmd

    nc = bacc.Bacc("TRN2", target_bir_lowering=False, num_devices=1)
    arrays, args = {}, {}
    laid = {n: np.ascontiguousarray(v) for n, v in inputs.items() if not n.startswith(UNUSED)}
    laid["shape_constants"] = shape_constants()
    for name, v in laid.items():
        arrays[f"in_{name}"] = v
        args[name] = nc.dram_tensor(f"in_{name}", v.shape, mybir.dt.from_np(v.dtype), kind="ExternalInput").ap()
    out = nc.dram_tensor("out_0", (1, S, D), F32, kind="ExternalOutput").ap()
    build(nc, args, out)
    r = run_bass_kernel_spmd(nc, [arrays], core_ids=[0])
    return r.results[0]["out_0"]
```
